# Optimizing a Trainium2 kernel written in Bass

```python
import jax, jax.numpy as jnp
from jax import lax
import numpy as np
import math

D_MODEL = 1024
BATCH = 1
SEQ = 1024
DEPTH = 1

CHUNK = 128
A_WIDTH = D_MODEL
A_GROUPS = 8
A_GROUP_DIM = A_WIDTH // A_GROUPS
N_HEADS = 16
HEAD_DIM = 64
B_WIDTH = N_HEADS * HEAD_DIM
DILATED_PATTERNS = ((128, 1), (512, 4), (2048, 16))
BLOCK = 128
N_BRANCHES = 2
EPS = 1e-6
NEG_INF = -1e30
IN_COLS = 3 * A_WIDTH + 4 * B_WIDTH + N_BRANCHES * D_MODEL


def rmsnorm(x, g):
    xf = x.astype(jnp.float32)
    y = xf * lax.rsqrt(jnp.mean(xf * xf, axis=-1, keepdims=True) + EPS)
    return (y * g.astype(jnp.float32)).astype(x.dtype)

def chunked_spatial_gating(u, v, w_s, b_s, g_v):
    Bn, S, _ = v.shape
    v = rmsnorm(v, g_v)
    vc = v.reshape(Bn, S // CHUNK, CHUNK, A_GROUPS, A_GROUP_DIM)
    causal = jnp.tril(jnp.ones((CHUNK, CHUNK), dtype=bool))
    w = jnp.where(causal[None], w_s, 0).astype(v.dtype)
    mixed = jnp.einsum('gts,bcsgd->bctgd', w, vc) + b_s.T[None, None, :, :, None]
    return u * mixed.reshape(Bn, S, A_WIDTH)

def dilated_pattern(q, k, v, slopes, window, dilation):
    Bn, H, S, Dh = q.shape
    L = S // dilation
    nback = window // dilation
    nb = -(-L // BLOCK)
    pad = nb * BLOCK - L

    def to_blocks(t):
        t = t.reshape(Bn, H, L, dilation, Dh).transpose(0, 1, 3, 2, 4)
        t = jnp.pad(t, ((0, 0), (0, 0), (0, 0), (0, pad), (0, 0)))
        return t.reshape(Bn, H, dilation, nb, BLOCK, Dh)

    qb, kb, vb = to_blocks(q), to_blocks(k), to_blocks(v)

    def with_prev(t):
        prev = jnp.pad(t, ((0, 0), (0, 0), (0, 0), (1, 0), (0, 0), (0, 0)))[:, :, :, :-1]
        return jnp.concatenate([prev, t], axis=4)

    kw, vw = with_prev(kb), with_prev(vb)
    qpos = jnp.arange(BLOCK)[:, None] + BLOCK
    kpos = jnp.arange(2 * BLOCK)[None, :]
    dist = qpos - kpos
    key_idx = (jnp.arange(nb)[:, None, None] - 1) * BLOCK + kpos[None]
    valid = (dist >= 0) & (dist <= nback) & (key_idx >= 0)

    s = jnp.einsum('bhrnqd,bhrnkd->bhrnqk', qb, kw) * (Dh ** -0.5)
    s = s - slopes[None, :, None, None, None, None] * (dist * dilation).astype(jnp.float32)
    s = jnp.where(valid[None, None, None], s, NEG_INF)
    m = jnp.max(s, axis=-1)
    p = jnp.exp(s - m[..., None])
    l = jnp.sum(p, axis=-1)
    o = jnp.einsum('bhrnqk,bhrnkd->bhrnqd', p, vw) / l[..., None]

    def from_blocks(t):
        t = t.reshape(Bn, H, dilation, nb * BLOCK, *t.shape[5:])[:, :, :, :L]
        t = jnp.moveaxis(t, 2, 3)
        return t.reshape(Bn, H, S, *t.shape[4:])

    return from_blocks(o), from_blocks(m), from_blocks(l)

def dilated_attention(q, k, v):
    Bn, S, _ = q.shape
    heads = lambda t: t.astype(jnp.float32).reshape(Bn, S, N_HEADS, HEAD_DIM).transpose(0, 2, 1, 3)
    qh, kh, vh = heads(q), heads(k), heads(v)
    slopes = 2.0 ** (-8.0 * jnp.arange(1, N_HEADS + 1, dtype=jnp.float32) / N_HEADS)
    outs = [dilated_pattern(qh, kh, vh, slopes, w, d) for (w, d) in DILATED_PATTERNS]
    m_all = jnp.max(jnp.stack([m for (_, m, _) in outs]), axis=0)
    alphas = [l * jnp.exp(m - m_all) for (_, m, l) in outs]
    num = sum(a[..., None] * o for a, (o, _, _) in zip(alphas, outs))
    o = num / sum(alphas)[..., None]
    return o.transpose(0, 2, 1, 3).reshape(Bn, S, B_WIDTH).astype(q.dtype)

def first_inputs(seed: int = 0) -> dict:
    key = jax.random.key(seed)
    ks = jax.random.split(key, 10)
    f32 = jnp.float32
    x = jax.random.normal(ks[0], (BATCH, SEQ, D_MODEL), f32)
    g_norm = 1.0 + 0.05 * jax.random.normal(ks[1], (DEPTH, D_MODEL), f32)
    w_in = jax.random.normal(ks[2], (DEPTH, D_MODEL, IN_COLS), f32) * D_MODEL ** -0.5
    w_s = jax.random.normal(ks[3], (DEPTH, A_GROUPS, CHUNK, CHUNK), f32) * CHUNK ** -0.5
    b_s = 1.0 + 0.1 * jax.random.normal(ks[4], (DEPTH, A_GROUPS, CHUNK), f32)
    g_v = 1.0 + 0.05 * jax.random.normal(ks[5], (DEPTH, A_WIDTH), f32)
    w_proj_a = jax.random.normal(ks[6], (DEPTH, A_WIDTH, D_MODEL), f32) * A_WIDTH ** -0.5
    w_proj_b = jax.random.normal(ks[7], (DEPTH, B_WIDTH, D_MODEL), f32) * B_WIDTH ** -0.5
    w_out = jax.random.normal(ks[8], (DEPTH, D_MODEL, D_MODEL), f32) * D_MODEL ** -0.5
    g_final = 1.0 + 0.05 * jax.random.normal(ks[9], (D_MODEL,), f32)
    return {"x": x, "g_norm": g_norm, "w_in": w_in, "w_s": w_s, "b_s": b_s, "g_v": g_v,
            "w_proj_a": w_proj_a, "w_proj_b": w_proj_b, "w_out": w_out, "g_final": g_final}

def first_block(x, g_norm, w_in, w_s, b_s, g_v, w_proj_a, w_proj_b, w_out, g_final):
    splits = [A_WIDTH, 2 * A_WIDTH, 3 * A_WIDTH,
              3 * A_WIDTH + B_WIDTH, 3 * A_WIDTH + 2 * B_WIDTH,
              3 * A_WIDTH + 3 * B_WIDTH, 3 * A_WIDTH + 4 * B_WIDTH]
    for layer in range(DEPTH):
        h = rmsnorm(x, g_norm[layer])
        proj = h @ w_in[layer]
        a_u, a_v, a_gate, q, k, v, b_gate, gate_logits = jnp.split(proj, splits, axis=-1)
        y_a = chunked_spatial_gating(jax.nn.gelu(a_u), jax.nn.gelu(a_v),
                                     w_s[layer], b_s[layer], g_v[layer]) * jax.nn.silu(a_gate)
        y_b = dilated_attention(q, k, v) * jax.nn.silu(b_gate)
        g_a, g_b = jnp.split(jax.nn.sigmoid(gate_logits), N_BRANCHES, axis=-1)
        merged = g_a * (y_a @ w_proj_a[layer]) + g_b * (y_b @ w_proj_b[layer])
        x = x + merged @ w_out[layer]
    return rmsnorm(x, g_final)


DEPTH_2 = 2

N_A = DEPTH_2 // 2
N_B = DEPTH_2 - N_A

EXPAND = 2
D_INNER = EXPAND * D_MODEL
SSM_HEAD_DIM = 64
SSM_HEADS = D_INNER // SSM_HEAD_DIM
N_GROUPS = 4
HEADS_PER_GROUP = SSM_HEADS // N_GROUPS
D_STATE = 128
CONV_K = 4
CONV_DIM = D_INNER + 2 * N_GROUPS * D_STATE
IN_PROJ_DIM = 2 * D_INNER + 2 * N_GROUPS * D_STATE + SSM_HEADS
DT_MIN = 0.001
DT_MAX = 0.1

SB_HEAD_DIM = 64
SB_HEADS = D_MODEL // SB_HEAD_DIM
SB_WIDTH = SB_HEADS * SB_HEAD_DIM
SB_BLOCK = 128

PLE_DIM = 256

NORM_EPS = 1e-6


def rms(x):
    xf = x.astype(jnp.float32)
    return (xf * lax.rsqrt(jnp.mean(xf * xf, axis=-1, keepdims=True) + NORM_EPS)).astype(x.dtype)

def rmsnorm_2(x, g):
    return rms(x) * g.astype(x.dtype)

def causal_depthwise_conv(u, w, b):
    k = w.shape[0]
    s = u.shape[1]
    up = jnp.pad(u, ((0, 0), (k - 1, 0), (0, 0)))
    out = b
    for j in range(k):
        out = out + w[j] * up[:, j:j + s]
    return out

def ssd_chunked_scan(xs, dt, A, Bm, Cm):
    bsz, s, _, _ = xs.shape
    nc = s // CHUNK
    G, HG, P, N, L = N_GROUPS, HEADS_PER_GROUP, SSM_HEAD_DIM, D_STATE, CHUNK
    xc = xs.astype(jnp.float32).reshape(bsz, nc, L, G, HG, P).transpose(1, 0, 2, 3, 4, 5)
    dtc = dt.reshape(bsz, nc, L, G, HG).transpose(1, 0, 2, 3, 4)
    Bc = Bm.astype(jnp.float32).reshape(bsz, nc, L, G, N).transpose(1, 0, 2, 3, 4)
    Cc = Cm.astype(jnp.float32).reshape(bsz, nc, L, G, N).transpose(1, 0, 2, 3, 4)
    Ag = A.reshape(G, HG)
    causal = jnp.tril(jnp.ones((L, L), dtype=bool))

    def step(state, inp):
        x_k, dt_k, B_k, C_k = inp
        acum = jnp.cumsum(dt_k * Ag, axis=1)
        seg = acum[:, :, None] - acum[:, None, :]
        decay = jnp.exp(jnp.where(causal[None, :, :, None, None], seg, -jnp.inf))
        xdt = x_k * dt_k[..., None]
        cb = jnp.einsum('blgn,bsgn->blsg', C_k, B_k)
        y_intra = jnp.einsum('blsgh,bsghp->blghp', cb[..., None] * decay, xdt)
        y_inter = jnp.einsum('blgn,bghpn->blghp', C_k, state) * jnp.exp(acum)[..., None]
        to_end = jnp.exp(acum[:, -1:] - acum)
        new_state = state * jnp.exp(acum[:, -1])[..., None, None] + jnp.einsum(
            'bsgn,bsghp->bghpn', B_k, xdt * to_end[..., None])
        return new_state, y_intra + y_inter

    state0 = jnp.zeros((bsz, G, HG, P, N), jnp.float32)
    _, y = lax.scan(step, state0, (xc, dtc, Bc, Cc))
    y = y.transpose(1, 0, 2, 3, 4, 5).reshape(bsz, s, SSM_HEADS, P)
    return y.astype(xs.dtype)

def mamba2_mixer(h, norm_g, w_in, conv_w, conv_b, dt_bias, A_log, d_skip, y_g, w_out):
    bsz, s, _ = h.shape
    u = rmsnorm_2(h, norm_g)
    zxbcdt = u @ w_in
    z = zxbcdt[..., :D_INNER]
    xbc = zxbcdt[..., D_INNER:D_INNER + CONV_DIM]
    dt = zxbcdt[..., D_INNER + CONV_DIM:]
    xbc = jax.nn.silu(causal_depthwise_conv(xbc, conv_w, conv_b))
    xs = xbc[..., :D_INNER].reshape(bsz, s, SSM_HEADS, SSM_HEAD_DIM)
    Bm = xbc[..., D_INNER:D_INNER + N_GROUPS * D_STATE].reshape(bsz, s, N_GROUPS, D_STATE)
    Cm = xbc[..., D_INNER + N_GROUPS * D_STATE:].reshape(bsz, s, N_GROUPS, D_STATE)
    dt = jax.nn.softplus(dt.astype(jnp.float32) + dt_bias.astype(jnp.float32))
    A = -jnp.exp(A_log.astype(jnp.float32))
    y = ssd_chunked_scan(xs, dt, A, Bm, Cm)
    y = y + d_skip.astype(y.dtype)[:, None] * xs
    y = y.reshape(bsz, s, D_INNER) * jax.nn.silu(z)
    y = rms(y.reshape(bsz, s, N_GROUPS, D_INNER // N_GROUPS)).reshape(bsz, s, D_INNER) * y_g
    return y @ w_out

def shared_kv(h, norm_g, w_kv, k_g):
    bsz, s, _ = h.shape
    kv = rmsnorm_2(h, norm_g) @ w_kv
    k = rmsnorm_2(kv[..., :SB_WIDTH].reshape(bsz, s, SB_HEADS, SB_HEAD_DIM), k_g)
    v = kv[..., SB_WIDTH:].reshape(bsz, s, SB_HEADS, SB_HEAD_DIM)
    return k.transpose(0, 2, 1, 3), v.transpose(0, 2, 1, 3)

def stick_breaking_mixer(h, k, v, norm_g, w_in, q_g, w_out):
    bsz, s, _ = h.shape
    qg = rmsnorm_2(h, norm_g) @ w_in
    gate = qg[..., SB_WIDTH:]
    q = rmsnorm_2(qg[..., :SB_WIDTH].reshape(bsz, s, SB_HEADS, SB_HEAD_DIM), q_g)
    q = (q * (1.0 / math.sqrt(SB_HEAD_DIM))).transpose(0, 2, 1, 3)
    outs = []
    for blk in range(s // SB_BLOCK):
        q0 = blk * SB_BLOCK
        kend = q0 + SB_BLOCK
        z = jnp.einsum('bhtd,bhsd->bhts', q[:, :, q0:kend], k[:, :, :kend]).astype(jnp.float32)
        t_idx = q0 + jnp.arange(SB_BLOCK)[:, None]
        s_idx = jnp.arange(kend)[None, :]
        strict = s_idx < t_idx
        log_keep = jnp.where(strict, jax.nn.log_sigmoid(-z), 0.0)
        suffix = lax.cumsum(log_keep, axis=3, reverse=True) - log_keep
        weights = jnp.where(strict, jnp.exp(jax.nn.log_sigmoid(z) + suffix), 0.0)
        outs.append(jnp.einsum('bhts,bhsd->bhtd', weights.astype(v.dtype), v[:, :, :kend]))
    o = jnp.concatenate(outs, axis=2).transpose(0, 2, 1, 3).reshape(bsz, s, SB_WIDTH)
    return (o * jax.nn.silu(gate)) @ w_out

def per_layer_embedding(h, p_i, norm_g, w_gate, w_proj):
    return h + (p_i @ w_proj) * jax.nn.sigmoid(rmsnorm_2(h, norm_g) @ w_gate)

def second_inputs(seed: int = 0) -> dict:
    key = jax.random.key(seed)
    ks = jax.random.split(key, 24)

    def nrm(k, shape, scale):
        return jax.random.normal(k, shape, jnp.float32) * scale

    def gain(k, shape):
        return 1.0 + 0.05 * jax.random.normal(k, shape, jnp.float32)

    u = jax.random.uniform(ks[6], (N_A, SSM_HEADS), jnp.float32)
    dt = jnp.exp(u * (math.log(DT_MAX) - math.log(DT_MIN)) + math.log(DT_MIN))
    dt_bias = dt + jnp.log(-jnp.expm1(-dt))
    A_log = jnp.log(jax.random.uniform(ks[7], (N_A, SSM_HEADS), jnp.float32, minval=1.0, maxval=16.0))
    return {
        "x": nrm(ks[0], (BATCH, SEQ, D_MODEL), 1.0),
        "p": nrm(ks[1], (DEPTH_2, BATCH, SEQ, PLE_DIM), 1.0),
        "m_norm": gain(ks[2], (N_A, D_MODEL)),
        "m_in": nrm(ks[3], (N_A, D_MODEL, IN_PROJ_DIM), D_MODEL ** -0.5),
        "m_conv_w": nrm(ks[4], (N_A, CONV_K, CONV_DIM), CONV_K ** -0.5),
        "m_conv_b": nrm(ks[5], (N_A, CONV_DIM), 0.01),
        "m_dt_bias": dt_bias,
        "m_A_log": A_log,
        "m_D": gain(ks[8], (N_A, SSM_HEADS)),
        "m_ynorm": gain(ks[9], (N_A, D_INNER)),
        "m_out": nrm(ks[10], (N_A, D_INNER, D_MODEL), D_INNER ** -0.5),
        "kv_norm": gain(ks[11], (D_MODEL,)),
        "w_kv": nrm(ks[12], (D_MODEL, 2 * SB_WIDTH), D_MODEL ** -0.5),
        "k_norm": gain(ks[13], (SB_HEAD_DIM,)),
        "s_norm": gain(ks[14], (N_B, D_MODEL)),
        "s_in": nrm(ks[15], (N_B, D_MODEL, 2 * SB_WIDTH), D_MODEL ** -0.5),
        "q_norm": gain(ks[16], (N_B, SB_HEAD_DIM)),
        "s_out": nrm(ks[17], (N_B, SB_WIDTH, D_MODEL), SB_WIDTH ** -0.5),
        "ple_norm": gain(ks[18], (DEPTH_2, D_MODEL)),
        "ple_gate": nrm(ks[19], (DEPTH_2, D_MODEL, D_MODEL), D_MODEL ** -0.5),
        "ple_proj": nrm(ks[20], (DEPTH_2, PLE_DIM, D_MODEL), PLE_DIM ** -0.5),
    }

def second_block(x, p, m_norm, m_in, m_conv_w, m_conv_b, m_dt_bias, m_A_log, m_D, m_ynorm, m_out,
              kv_norm, w_kv, k_norm, s_norm, s_in, q_norm, s_out, ple_norm, ple_gate, ple_proj):
    h = x
    k = v = None
    for i in range(DEPTH_2):
        if i < N_A:
            h = h + mamba2_mixer(h, m_norm[i], m_in[i], m_conv_w[i], m_conv_b[i], m_dt_bias[i],
                                 m_A_log[i], m_D[i], m_ynorm[i], m_out[i])
        else:
            if i == N_A:
                k, v = shared_kv(h, kv_norm, w_kv, k_norm)
            j = i - N_A
            h = h + stick_breaking_mixer(h, k, v, s_norm[j], s_in[j], q_norm[j], s_out[j])
        h = per_layer_embedding(h, p[i], ple_norm[i], ple_gate[i], ple_proj[i])
    return h


def setup_inputs(seed=0):
    out = dict(first_inputs(seed))
    for name, value in second_inputs(seed + 1).items():
        if name != "x":
            out[name + "_2"] = value
    return out


def reference(
    x, g_norm, w_in, w_s, b_s, g_v, w_proj_a, w_proj_b, w_out, g_final, p_2, m_norm_2, m_in_2,
    m_conv_w_2, m_conv_b_2, m_dt_bias_2, m_A_log_2, m_D_2, m_ynorm_2, m_out_2, kv_norm_2,
    w_kv_2, k_norm_2, s_norm_2, s_in_2, q_norm_2, s_out_2, ple_norm_2, ple_gate_2, ple_proj_2,
):
    x = first_block(
        x, g_norm, w_in, w_s, b_s, g_v, w_proj_a, w_proj_b, w_out, g_final,
    )
    return second_block(
        x, p_2, m_norm_2, m_in_2, m_conv_w_2, m_conv_b_2, m_dt_bias_2, m_A_log_2, m_D_2,
        m_ynorm_2, m_out_2, kv_norm_2, w_kv_2, k_norm_2, s_norm_2, s_in_2, q_norm_2, s_out_2,
        ple_norm_2, ple_gate_2, ple_proj_2,
    )


_drawn_inputs = setup_inputs


def setup_inputs(seed=0):
    import zlib

    import numpy as np

    out = dict(_drawn_inputs(seed))
    spreads = {}
    factors = {'g_v': 6.271,
     'm_conv_b_2': 5.911,
     'kv_norm_2': 4.08,
     'k_norm_2': 8.0,
     's_norm_2': 4.242,
     'q_norm_2': 8.0,
     'ple_norm_2': 5.928}
    for name, (base, spread) in spreads.items():
        noise = np.random.default_rng([zlib.crc32(name.encode()), seed]).standard_normal(out[name].shape)
        drawn = base * np.exp(spread * noise) if base else spread * noise
        out[name] = __import__('jax').numpy.asarray(drawn.astype(out[name].dtype))
    for name, factor in factors.items():
        out[name] = (out[name] * factor).astype(out[name].dtype)
    return out
```

```python
from contextlib import ExitStack

import numpy as np
import concourse.bass as bass
from concourse import mybir

F32 = mybir.dt.float32
F32R = mybir.dt.float32r
ALU = mybir.AluOpType
ACT = mybir.ActivationFunctionType

P = 128
S = 1024
DM = 1024
KT = DM // P
NC = S // P
H = 512
EPS = 1e-6
HEADS = 16
HD = 64
PAIRS = HEADS // 2
NEG = -1e30
GROUPS = 4
GT = 4

N_V, N_UG, N_PA, N_ATT, N_PB, N_OUT = 8, 16, 16, 32, 16, 8
GROUP_TILES = 2 + 4 + 4 + 4
N_SSM, N_PLE, N_STICK, N_SOUT = GROUPS * GROUP_TILES, 8, 32, 8
STAGES = dict(v=N_V, ug=N_UG, pa=N_PA, att=N_ATT, pb=N_PB, out=N_OUT, ssm=N_SSM, ple0=N_PLE,
              stick=N_STICK, sout=N_SOUT, ple1=N_PLE)
FIRST, N_TILES = {}, 0
for _name, _n in STAGES.items():
    FIRST[_name] = N_TILES
    N_TILES += _n

VEC_WIDTH = dict(g_norm=8, g_v=8, g_final=8, m_norm=8, conv_w=96, conv_b=24, d_skip=16, y_norm=16,
                 kv_norm=8, s_norm=8, ple0=8, ple1=8, q_g=1, k_g=1)
VEC, N_VEC = {}, 0
for _name, _n in VEC_WIDTH.items():
    VEC[_name] = N_VEC
    N_VEC += _n


def halves(ap):
    return [ap[:, 0:H], ap[:, H:S]]


class Kernel:

    def __init__(self, nc, ctx, io):
        self.nc, self.io = nc, io

        def sb(name, shape, dt=F32):
            return ctx.enter_context(nc.sbuf_tensor(name, shape, dt))

        self.ones = sb("ones", [P, P])
        self.ident = sb("ident", [P, P])
        self.vec = sb("vec", [P, N_VEC])
        self.eps = sb("eps", [P, 1])
        self.root = sb("root", [P, NC])
        self.rtok = sb("rtok", [P, NC])
        self.R = sb("R", [P, S])
        self.acc = sb("acc", [P, S])
        self.sq = sb("sq", [P, 2, S])
        self.wraw = sb("wraw", [P, 2, 8, P])
        self.whi = sb("whi", [P, 2, 8, P], F32R)
        self.wlo = sb("wlo", [P, 2, 8, P], F32R)
        self.w_land = [ctx.enter_context(nc.semaphore(f"w_land{s}")) for s in range(2)]
        self.w_hi = ctx.enter_context(nc.semaphore("w_hi"))
        self.w_lo = ctx.enter_context(nc.semaphore("w_lo"))

    def semaphores(self, ctx, prefix):
        nc, taken = self.nc, []

        def give_back():
            nc.clear_and_free_semaphores(taken)
            nc.all_engine_barrier()

        ctx.callback(give_back)

        def sem(name):
            taken.append(nc.alloc_semaphore(prefix + name))
            return taken[-1]

        return sem

    def gain(self, name, k):
        return self.vec[:, VEC[name] + k:VEC[name] + k + 1]

    def load_weight(self, sp, n, s):
        sp.dma_start(self.wraw[:, s, :, :], self.io["w"][n, :, :, :]).then_inc(self.w_land[s], 16)

    def load_ahead(self, sp, stage, skip_last=False):
        n0, count = FIRST[stage], STAGES[stage]
        pairs = count // 2 - (1 if skip_last else 0)
        with sp.Fori(0, pairs) as i:
            for s in range(2):
                sp.wait_ge(self.w_lo, 2 * i + (n0 + s + 1))
                self.load_weight(sp, 2 * i + (n0 + s + 2), s)

    def split_hi(self, act, lap, s):
        act.wait_ge(self.w_land[s], 16 * lap + 16)
        act.activation(self.whi[:, s, :, :], self.wraw[:, s, :, :], ACT.Copy).then_inc(self.w_hi, 1)

    def split_lo(self, dve, lap, s):
        dve.wait_ge(self.w_hi, 2 * lap + (s + 1))
        dve.tensor_tensor(self.wlo[:, s, :, :], self.wraw[:, s, :, :],
                          self.whi[:, s, :, :].bitcast(F32), ALU.subtract).then_inc(self.w_lo, 1)

    def products(self, pe, out, s, w0, k, xhi, xlo, half, start, stop):
        cols = slice(half * H, half * H + H)
        pe.matmul(out, self.whi[:, s, w0, :], xhi[:, k, cols], start=start, stop=False)
        pe.matmul(out, self.whi[:, s, w0, :], xlo[:, k, cols], start=False, stop=False)
        return pe.matmul(out, self.wlo[:, s, w0, :], xhi[:, k, cols], start=False, stop=stop)

    def dense(self, pe, out, s, xhi, xlo, x_ready=None):
        for k in range(KT):
            if x_ready is not None:
                pe.wait_ge(x_ready, k + 1)
            for half in range(2):
                last = self.products(pe, out[:, half * H:half * H + H], s, k, k, xhi, xlo, half,
                                     k == 0, k == KT - 1)
        return last

    def tile_hi(self, act, xhi, src, k, gain, done):
        if gain is None:
            act.activation(xhi[:, k, :], src[:, k, :], ACT.Copy).then_inc(done, 1)
        else:
            act.activation(xhi[:, k, :], src[:, k, :], ACT.Copy, scale=self.gain(gain, k)).then_inc(done, 1)

    def tile_lo(self, dve, xlo, xhi, src, k, gain, hi_done, done):
        dve.wait_ge(hi_done, k + 1)
        high = xhi[:, k, :].bitcast(F32)
        if gain is None:
            dve.tensor_tensor(xlo[:, k, :], src[:, k, :], high, ALU.subtract).then_inc(done, 1)
        else:
            dve.scalar_tensor_tensor(xlo[:, k, :], src[:, k, :], self.gain(gain, k), high,
                                     ALU.mult, ALU.subtract).then_inc(done, 1)

    def square(self, act, src, k, sq_done, acc_done):
        if k >= 2:
            act.wait_ge(acc_done, k - 1)
        act.activation(self.sq[:, k % 2, :], src, ACT.Square).then_inc(sq_done, 1)

    def sum_squares(self, pool, tiles, sq_done, acc_done):
        for k in range(tiles):
            pool.wait_ge(sq_done, k + 1)
            if k == 0:
                pool.tensor_copy(self.acc[:, :], self.sq[:, 0, :]).then_inc(acc_done, 1)
            else:
                pool.wait_ge(acc_done, k)
                pool.tensor_tensor(self.acc[:, :], self.acc[:, :], self.sq[:, k % 2, :],
                                   ALU.add).then_inc(acc_done, 1)

    def square_tile(self, act, dst, src, n, added, count, acc_done, first):
        act.wait_ge(added, count)
        if not first:
            act.wait_ge(acc_done, n - 1)
        return act.activation(dst, src, ACT.Square)

    def sum_tiles(self, pool, sq, sq_done, acc_done, go):
        pool.wait_ge(sq_done, 1)
        pool.sem_inc(go, 1)
        pool.tensor_copy(self.acc[:, :], sq[:, 0, :]).then_inc(acc_done, 1)
        pool.wait_ge(sq_done, 2)
        pool.wait_ge(acc_done, 1)
        pool.tensor_tensor(self.acc[:, :], self.acc[:, :], sq[:, 1, :], ALU.add).then_inc(acc_done, 1)
        with pool.Fori(1, KT // 2) as i:
            for s in range(2):
                pool.wait_ge(sq_done, 2 * i + s + 1)
                pool.wait_ge(acc_done, 2 * i + s)
                pool.tensor_tensor(self.acc[:, :], self.acc[:, :], sq[:, s, :], ALU.add).then_inc(acc_done, 1)

    def norm_sums(self, pe, sums, sums_done):
        for c in range(NC):
            last = pe.matmul(sums[:, c:c + 1], self.acc[:, c * P:c * P + P], self.ones[:, 0:1],
                             start=True, stop=True)
        last.then_inc(sums_done, 1)

    def norm_root(self, act, sums, features, sums_done, root_done):
        act.wait_ge(sums_done, 1)
        act.activation(self.root[:, :], sums[:, 0:NC], ACT.Sqrt, scale=1.0 / features,
                       bias=self.eps[:, 0:1]).then_inc(root_done, 1)

    def norm_recip(self, dve, root_done, rtok_done):
        dve.wait_ge(root_done, 1)
        dve.reciprocal(self.rtok[:, :], self.root[:, :]).then_inc(rtok_done, 1)
        dve.wait_ge(rtok_done, 1)

    def norm_diag(self, dve, diag_done):
        diag = self.sq[:, 0, :].rearrange("p (c t) -> p c t", c=NC)
        dve.tensor_tensor(diag, self.ident[:, :].unsqueeze(1).to_broadcast([P, NC, P]),
                          self.rtok[:, :].unsqueeze(2).to_broadcast([P, NC, P]), ALU.mult).then_inc(diag_done, 1)

    def norm_spread(self, pe, spread, diag_done, spread_done):
        pe.wait_ge(diag_done, 1)
        for half in range(2):
            last = pe.matmul(spread[:, half * H:half * H + H], self.ones[:, :],
                             self.sq[:, 0, half * H:half * H + H], start=True, stop=True)
        last.then_inc(spread_done, 1)

    def norm_copy(self, dve, spread, spread_done, r_done):
        dve.wait_ge(spread_done, 1)
        dve.tensor_copy(self.R[:, :], spread[:, :]).then_inc(r_done, 1)
        dve.wait_ge(r_done, 1)


def stage_v(K, x_sb, xhi, xlo, vN):
    nc, n0 = K.nc, FIRST["v"]
    with ExitStack() as ctx:
        sem = K.semaphores(ctx, "v_")
        D = ctx.enter_context(nc.psum_tensor("v_D", [P, 2, S], F32))
        turned = ctx.enter_context(nc.psum_tensor("v_turned", [P, S], F32))
        sums = ctx.enter_context(nc.psum_tensor("v_sums", [P, H], F32))
        scaled = ctx.enter_context(nc.sbuf_tensor("v_scaled", [P, 2, S], F32))
        x_hi, x_lo, sq_done, acc_done = sem("x_hi"), sem("x_lo"), sem("sq"), sem("acc")
        sums_done, root_done, rtok_done = sem("sums"), sem("root"), sem("rtok")
        diag_done, spread_done, r_done = sem("diag"), sem("spread"), sem("r")
        mm, evac, gelu, vsq, vacc = sem("mm"), sem("evac"), sem("gelu"), sem("vsq"), sem("vacc")
        turn, stored, sums2, root2, rtok2 = sem("turn"), sem("stored"), sem("sums2"), sem("root2"), sem("rtok2")
        x_land, const_land, eps_done = [sem(f"x_land{k}") for k in range(KT)], sem("const_land"), sem("eps")
        with nc.Block() as block:
            @block.sync
            def _(sp):
                x_tiles = K.io["xT"].rearrange("(k p) t -> k p t", p=P)
                K.load_weight(sp, 0, 0)
                for name, tile in (("vec", K.vec), ("ident", K.ident), ("ones", K.ones)):
                    sp.dma_start(tile[:, :], K.io[name][:, :]).then_inc(const_land, 16)
                for k in range(KT):
                    sp.dma_start(x_sb[:, k, :], x_tiles[k]).then_inc(x_land[k], 16)
                    if k == 3:
                        K.load_weight(sp, 1, 1)
                K.load_ahead(sp, "v")

            @block.tensor
            def _(pe):
                pe.wait_ge(const_land, 48)

                def turn_tile(n, s):
                    pe.wait_ge(gelu, n + 1)
                    if not (isinstance(n, int) and n == 0):
                        pe.wait_ge(stored, n)
                    for c in range(NC):
                        last = pe.transpose(turned[:, c * P:c * P + P], scaled[:, s, c * P:c * P + P],
                                            K.ident[:, :])
                    last.then_inc(turn, 1)

                def tiles(i, first=False):
                    for s in range(2):
                        n = 2 * i + s
                        pe.wait_ge(K.w_lo, n + (n0 + 1))
                        if not first:
                            pe.wait_ge(evac, n - 1)
                        K.dense(pe, D[:, s, :], s, xhi, xlo, x_lo if first and s == 0 else None).then_inc(mm, 1)
                        if first and s == 0:
                            pe.wait_ge(acc_done, KT)
                            K.norm_sums(pe, sums, sums_done)
                        elif first:
                            K.norm_spread(pe, turned, diag_done, spread_done)
                            pe.wait_ge(spread_done, 1)
                            pe.wait_ge(r_done, 1)
                            turn_tile(0, 0)
                        else:
                            turn_tile(n - 1, 1 - s)

                tiles(0, first=True)
                with pe.Fori(1, N_V // 2) as i:
                    tiles(i)
                turn_tile(N_V - 1, 1)
                pe.wait_ge(vacc, N_V)
                K.norm_sums(pe, sums, sums2)

            @block.scalar
            def _(act):
                def tiles(i, first=False, last=False):
                    for s in range(2):
                        n = 2 * i + s
                        act.wait_ge(evac, n + 1)
                        act.activation(scaled[:, s, :], scaled[:, s, :], ACT.Gelu_apprx_tanh).then_inc(gelu, 1)
                        act.wait_ge(gelu, n + 1)
                        if not first:
                            act.wait_ge(vacc, n - 1)
                        act.activation(K.sq[:, s, :], scaled[:, s, :], ACT.Square).then_inc(vsq, 1)
                        if not last:
                            act.wait_ge(mm, n + 1)
                            K.split_hi(act, i + (n0 // 2 + 1), s)
                        act.wait_ge(turn, n + 1)
                        act.activation(vN[:, n, :], turned[:, :], ACT.Copy).then_inc(stored, 1)

                K.split_hi(act, n0 // 2, 0)
                act.wait_ge(const_land, 48)
                for k in range(KT):
                    act.wait_ge(x_land[k], 16)
                    K.tile_hi(act, xhi, x_sb, k, "g_norm", x_hi)
                    K.square(act, x_sb[:, k, :], k, sq_done, acc_done)
                    if k == 4:
                        K.split_hi(act, n0 // 2, 1)
                act.wait_ge(eps_done, 1)
                K.norm_root(act, sums, DM, sums_done, root_done)
                act.wait_ge(spread_done, 1)
                tiles(0, first=True)
                with act.Fori(1, N_V // 2 - 1) as i:
                    tiles(i)
                tiles(N_V // 2 - 1, last=True)
                K.norm_root(act, sums, DM, sums2, root2)

            @block.vector
            def _(dve):
                def tiles(i, first=False, last=False):
                    for s in range(2):
                        n = 2 * i + s
                        dve.wait_ge(mm, n + 1)
                        if not first:
                            dve.wait_ge(turn, n - 1)
                            dve.wait_ge(vsq, n - 1)
                        dve.tensor_tensor(scaled[:, s, :], D[:, s, :], K.R[:, :], ALU.mult).then_inc(evac, 1)
                        if not last:
                            K.split_lo(dve, i + (n0 // 2 + 1), s)

                dve.memset(K.eps[:, :], EPS).then_inc(eps_done, 1)
                K.split_lo(dve, n0 // 2, 0)
                dve.wait_ge(const_land, 48)
                for k in range(KT):
                    dve.wait_ge(x_land[k], 16)
                    K.tile_lo(dve, xlo, xhi, x_sb, k, "g_norm", x_hi, x_lo)
                    if k == 4:
                        K.split_lo(dve, n0 // 2, 1)
                K.norm_recip(dve, root_done, rtok_done)
                K.norm_diag(dve, diag_done)
                K.norm_copy(dve, turned, spread_done, r_done)
                tiles(0, first=True)
                with dve.Fori(1, N_V // 2 - 1) as i:
                    tiles(i)
                tiles(N_V // 2 - 1, last=True)
                K.norm_recip(dve, root2, rtok2)

            @block.gpsimd
            def _(pool):
                K.sum_squares(pool, KT, sq_done, acc_done)
                pool.wait_ge(sums_done, 1)
                pool.wait_ge(vsq, 1)
                pool.tensor_copy(K.acc[:, :], K.sq[:, 0, :]).then_inc(vacc, 1)
                pool.wait_ge(vsq, 2)
                pool.wait_ge(vacc, 1)
                pool.tensor_tensor(K.acc[:, :], K.acc[:, :], K.sq[:, 1, :], ALU.add).then_inc(vacc, 1)
                with pool.Fori(1, N_V // 2) as i:
                    for s in range(2):
                        pool.wait_ge(vsq, 2 * i + s + 1)
                        pool.wait_ge(vacc, 2 * i + s)
                        pool.tensor_tensor(K.acc[:, :], K.acc[:, :], K.sq[:, s, :], ALU.add).then_inc(vacc, 1)


def stage_ug(K, xhi, xlo, vN, yhi, ylo):
    nc, io, n0 = K.nc, K.io, FIRST["ug"]
    with ExitStack() as ctx:
        sem = K.semaphores(ctx, "ug_")
        D = ctx.enter_context(nc.psum_tensor("ug_D", [P, 2, S], F32))
        mixed = ctx.enter_context(nc.psum_tensor("ug_mixed", [P, S], F32))
        vS = ctx.enter_context(nc.sbuf_tensor("ug_vS", [P, NC, P], F32))
        ws = ctx.enter_context(nc.sbuf_tensor("ug_ws", [P, P], F32))
        bs = ctx.enter_context(nc.sbuf_tensor("ug_bs", [P, P], F32))
        wm = ctx.enter_context(nc.sbuf_tensor("ug_wm", [P, P], F32))
        u, gate = K.sq[:, 0, :], K.sq[:, 1, :]
        y = K.acc[:, :]
        mm, u_scaled, g_scaled, u_gelu, g_silu = sem("mm"), sem("us"), sem("gs"), sem("gelu"), sem("silu")
        ws_land, bs_land, select_go = sem("ws_land"), sem("bs_land"), sem("select_go")
        wm_done, v_scaled, mix, biased, uy, y_done = sem("wm"), sem("vs"), sem("mix"), sem("biased"), sem("uy"), sem("y")
        y_hi, y_lo = sem("y_hi"), sem("y_lo")
        with nc.Block() as block:
            @block.sync
            def _(sp):
                K.load_ahead(sp, "ug")

            @block.gpsimd
            def _(pool):
                pool.sem_inc(wm_done, 1)
                with pool.Fori(0, KT) as g:
                    pool.wait_ge(wm_done, g + 1)
                    pool.dma_start(ws[:, :], io["w_sT"][g, :, :]).then_inc(ws_land, 16)
                    pool.wait_ge(biased, g + 1)
                    pool.dma_start(bs[:, :], io["b_s"][g, :].partition_broadcast(P)).then_inc(bs_land, 16)
                    pool.wait_ge(ws_land, 16 * g + 16)
                    pool.wait_ge(mix, g + 1)
                    pool.sem_inc(select_go, 1)
                    pool.affine_select(out=wm[:, :], in_=ws[:, :], compare_op=ALU.is_ge, fill=0.0, base=0,
                                       pattern=[[1, P]], channel_multiplier=-1).then_inc(wm_done, 1)

            @block.tensor
            def _(pe):
                pe.sem_inc(mix, 1)
                with pe.Fori(0, KT) as g:
                    pe.wait_ge(K.w_lo, 2 * g + (n0 + 1))
                    pe.wait_ge(u_scaled, g + 1)
                    K.dense(pe, D[:, 0, :], 0, xhi, xlo).then_inc(mm, 1)
                    pe.wait_ge(v_scaled, g + 1)
                    pe.wait_ge(wm_done, g + 2)
                    pe.wait_ge(uy, g + 1)
                    for c in range(NC):
                        last = pe.matmul(mixed[:, c * P:c * P + P], vS[:, c, :], wm[:, :], start=True, stop=True)
                    last.then_inc(mix, 1)
                    pe.wait_ge(K.w_lo, 2 * g + (n0 + 2))
                    pe.wait_ge(g_scaled, g + 1)
                    K.dense(pe, D[:, 1, :], 1, xhi, xlo).then_inc(mm, 1)

            @block.scalar
            def _(act):
                def group(g, last=False):
                    act.wait_ge(u_scaled, g + 2)
                    act.activation(u, u, ACT.Gelu_apprx_tanh).then_inc(u_gelu, 1)
                    if not last:
                        act.wait_ge(mm, 2 * g + 1)
                        K.split_hi(act, g + (n0 // 2 + 1), 0)
                    act.wait_ge(g_scaled, g + 2)
                    act.activation(gate, gate, ACT.Silu).then_inc(g_silu, 1)
                    if not last:
                        act.wait_ge(mm, 2 * g + 2)
                        K.split_hi(act, g + (n0 // 2 + 1), 1)
                    act.wait_ge(y_done, g + 1)
                    act.activation(yhi[:, g, :], y, ACT.Copy).then_inc(y_hi, 1)

                for s in range(2):
                    K.split_hi(act, n0 // 2, s)
                with act.Fori(0, KT - 1) as g:
                    group(g)
                group(KT - 1, last=True)

            @block.vector
            def _(dve):
                def scale_v(g):
                    dve.wait_ge(mix, g + 1)
                    dve.tensor_tensor(vS[:, :, :], vN[:, g, :].rearrange("p (c d) -> p c d", c=NC),
                                      K.rtok[:, :].unsqueeze(2).to_broadcast([P, NC, P]),
                                      ALU.mult).then_inc(v_scaled, 1)

                def group(g, last=False):
                    gv = K.vec[:, bass.ds(g + VEC["g_v"], 1)]
                    dve.wait_ge(mm, 2 * g + 1)
                    dve.tensor_tensor(u, D[:, 0, :], K.R[:, :], ALU.mult).then_inc(u_scaled, 1)
                    if not last:
                        K.split_lo(dve, g + (n0 // 2 + 1), 0)
                    dve.wait_ge(mix, g + 2)
                    dve.wait_ge(bs_land, 16 * g + 16)
                    b = bs[:, :].unsqueeze(1).to_broadcast([P, NC, P])
                    m = mixed[:, :].rearrange("p (c t) -> p c t", c=NC)
                    dve.scalar_tensor_tensor(m, m, gv, b, ALU.mult, ALU.add).then_inc(biased, 1)
                    dve.wait_ge(biased, g + 2)
                    dve.wait_ge(u_gelu, g + 1)
                    dve.tensor_tensor(u, mixed[:, :], u, ALU.mult).then_inc(uy, 1)
                    if not last:
                        scale_v(g + 1)
                    dve.wait_ge(mm, 2 * g + 2)
                    dve.tensor_tensor(gate, D[:, 1, :], K.R[:, :], ALU.mult).then_inc(g_scaled, 1)
                    if not last:
                        K.split_lo(dve, g + (n0 // 2 + 1), 1)
                    dve.wait_ge(g_silu, g + 1)
                    dve.tensor_tensor(y, u, gate, ALU.mult).then_inc(y_done, 1)
                    dve.wait_ge(y_hi, g + 1)
                    dve.tensor_tensor(ylo[:, g, :], y, yhi[:, g, :].bitcast(F32), ALU.subtract).then_inc(y_lo, 1)

                for q in (u_scaled, g_scaled, biased, uy):
                    dve.sem_inc(q, 1)
                for s in range(2):
                    K.split_lo(dve, n0 // 2, s)
                scale_v(0)
                with dve.Fori(0, KT - 1) as g:
                    group(g)
                group(KT - 1, last=True)


def stage_pa(K, xhi, xlo, yhi, ylo, spill):
    nc, n0 = K.nc, FIRST["pa"]
    with ExitStack() as ctx:
        sem = K.semaphores(ctx, "pa_")
        D = ctx.enter_context(nc.psum_tensor("pa_D", [P, 2, S], F32))
        gate, merged = K.sq[:, 0, :], K.sq[:, 1, :]
        mm, g_scaled, g_sig, m_done, spilled = sem("mm"), sem("gs"), sem("sig"), sem("merged"), sem("spilled")
        with nc.Block() as block:
            @block.sync
            def _(sp):
                K.load_ahead(sp, "pa")

            @block.gpsimd
            def _(pool):
                with pool.Fori(0, KT) as j:
                    pool.wait_ge(m_done, j + 2)
                    pool.dma_start(spill[j, :, :], merged).then_inc(spilled, 16)
                pool.wait_ge(spilled, 16 * KT)

            @block.tensor
            def _(pe):
                with pe.Fori(0, KT) as j:
                    pe.wait_ge(K.w_lo, 2 * j + (n0 + 1))
                    pe.wait_ge(g_scaled, j + 1)
                    K.dense(pe, D[:, 0, :], 0, xhi, xlo).then_inc(mm, 1)
                    pe.wait_ge(K.w_lo, 2 * j + (n0 + 2))
                    pe.wait_ge(m_done, j + 1)
                    K.dense(pe, D[:, 1, :], 1, yhi, ylo).then_inc(mm, 1)

            @block.scalar
            def _(act):
                def tile(j, last=False):
                    act.wait_ge(g_scaled, j + 2)
                    act.activation(gate, gate, ACT.Sigmoid).then_inc(g_sig, 1)
                    if not last:
                        for s in range(2):
                            act.wait_ge(mm, 2 * j + s + 1)
                            K.split_hi(act, j + (n0 // 2 + 1), s)

                for s in range(2):
                    K.split_hi(act, n0 // 2, s)
                with act.Fori(0, KT - 1) as j:
                    tile(j)
                tile(KT - 1, last=True)

            @block.vector
            def _(dve):
                def tile(j, last=False):
                    dve.wait_ge(mm, 2 * j + 1)
                    dve.wait_ge(m_done, j + 1)
                    dve.tensor_tensor(gate, D[:, 0, :], K.R[:, :], ALU.mult).then_inc(g_scaled, 1)
                    if not last:
                        K.split_lo(dve, j + (n0 // 2 + 1), 0)
                    dve.wait_ge(mm, 2 * j + 2)
                    dve.wait_ge(g_sig, j + 1)
                    if not (isinstance(j, int) and j == 0):
                        dve.wait_ge(spilled, 16 * j)
                    dve.tensor_tensor(merged, D[:, 1, :], gate, ALU.mult).then_inc(m_done, 1)
                    if not last:
                        K.split_lo(dve, j + (n0 // 2 + 1), 1)

                for q in (g_scaled, m_done):
                    dve.sem_inc(q, 1)
                for s in range(2):
                    K.split_lo(dve, n0 // 2, s)
                tile(0)
                with dve.Fori(1, KT - 1) as j:
                    tile(j)
                tile(KT - 1, last=True)


UNITS = [3] * 16 + [5, 5, 6]
N_UNITS = 4 * 2 * KT
SLOT_OF = [slot for slot, n in enumerate(UNITS) for _ in range(n)]
ROWS = [(h, i) for h in range(2) for i in range(NC)]
T_GROUPS = [(i + 4) // 4 for _, i in ROWS]
T_BEFORE = [sum(T_GROUPS[:r]) for r in range(17)]
T_PAIR = T_BEFORE[16]


def half_done_slot(c, half):
    return SLOT_OF[(2 * c + half) * KT + KT - 1]


def stage_attention(K, xhi, xlo, stack, out):
    nc, io = K.nc, K.io
    name = "att"
    n0 = FIRST[name]
    TV, TQ, TK, TG = range(4)
    with ExitStack() as ctx:
        sem = K.semaphores(ctx, name + "_")
        sb = lambda n, shape: ctx.enter_context(nc.sbuf_tensor(f"{name}_{n}", shape, F32))
        ps = lambda n, cols: ctx.enter_context(nc.psum_tensor(f"{name}_{n}", [P, cols], F32))
        D = ps("D", S)
        scores = ps("scores", S)
        turned = [ps(f"turned{b}", H) for b in range(2)]
        pO = ps("pO", H)
        pV = ps("pV", H)
        vN, gT, y_sb = (sb(n, [P, 2, S]) for n in ("vN", "gT", "y"))
        qT, kT = K.sq[:, 0, :], K.sq[:, 1, :]
        q_low = ctx.enter_context(nc.sbuf_tensor("att_q_low", [P, S], F32R))
        k_low = ctx.enter_context(nc.sbuf_tensor("att_k_low", [P, 2, S], F32R))
        vT = K.acc
        bias = sb("bias", [P, 2, S])
        rows = sb("rows", [P, 2, S])
        wT = sb("wT", [P, 2, S])
        yN = sb("yN", [P, NC, P])
        stat = sb("stat", [P, 16])
        rsum = sb("rsum", [P, 16])
        rinv = sb("rinv", [P, 16])

        dn, evac = sem("dn"), sem("evac")
        v_turn, v_copy = sem("v_turn"), sem("v_copy")
        qk, biased, ex = sem("qk"), sem("biased"), sem("ex")
        turn, tcopy, pv, ri, yn = sem("turn"), sem("tcopy"), sem("pv"), sem("ri"), sem("yn")
        reduce_go = sem("reduce_go")
        y_turn, y_out, silu = sem("y_turn"), sem("y_out"), sem("silu")
        q_hi, q_lo, k_hi, k_lo, stacked = sem("q_hi"), sem("q_lo"), sem("k_hi"), sem("k_lo"), sem("stacked")
        y_left, y_free, dma_go = sem("y_left"), sem("y_free"), sem("dma_go")
        b_land = [sem(f"b_land{h}") for h in range(2)]

        with nc.Block() as block:
            @block.sync
            def _(sp):
                for h in range(2):
                    sp.dma_start(bias[:, h, :], io["alibi"][h, :, :]).then_inc(b_land[h], 16)

                def pair(p):
                    for c in range(4):
                        n = 4 * p + (n0 + 4 + c)
                        sp.wait_ge(K.w_lo, n + 1)
                        K.load_weight(sp, n + 2, c % 2)
                        if c % 2 == 1:
                            h = c // 2
                            sp.wait_ge(biased, 16 * p + (8 * h + 8 + 1))
                            sp.dma_start(bias[:, h, :], io["alibi"][2 * p + (2 + h), :, :]).then_inc(b_land[h], 16)

                for c in range(4):
                    sp.wait_ge(K.w_lo, n0 + c + 1)
                    K.load_weight(sp, n0 + c + 2, c % 2)
                with sp.Fori(0, PAIRS - 1) as p:
                    pair(p)

            @block.gpsimd
            def _(pool):
                def stack_parts(P_, q):
                    pool.wait_ge(q_lo, P_ + 1)
                    pool.sem_inc(dma_go, 1)
                    for h in range(2):
                        pool.dma_start(stack[HD - HD * h:P - HD * h, q, h, :],
                                       q_low[HD * h:HD * h + HD, :]).then_inc(stacked, 16)
                    pool.wait_ge(k_hi, P_ + 1)
                    pool.sem_inc(dma_go, 1)
                    for h in range(2):
                        pool.dma_start(stack[HD - HD * h:P - HD * h, q, 2 + h, :],
                                       stack[HD * h:HD * h + HD, q, 2 + h, :]).then_inc(stacked, 16)

                def store(p, q):
                    pool.wait_ge(y_out, 2 * p + 4)
                    pool.sem_inc(dma_go, 1)
                    pool.dma_start(out[p, :, :], y_sb[:, q, :]).then_inc(y_left, 16)
                    pool.wait_ge(y_left, 16 * p + 16)
                    pool.sem_inc(y_free, 1)

                stack_parts(0, 0)
                with pool.Fori(0, 3) as i:
                    for q in range(2):
                        stack_parts(2 * i + (q + 1), 1 - q)
                        store(2 * i + q, q)
                stack_parts(7, 1)
                store(6, 0)
                store(7, 1)

            @block.tensor
            def _(pe):
                def units(p, a, b):
                    for u in range(a, b):
                        c, half, k = u // (2 * KT), (u // KT) % 2, u % KT
                        if half == 0 and k == 0:
                            pe.wait_ge(K.w_lo, 4 * p + (n0 + c + 1))
                        if k == 0:
                            pe.wait_ge(evac, 8 * p + (2 * c + half + 1))
                        last = K.products(pe, D[:, half * H:half * H + H], c % 2, k, k, xhi, xlo, half,
                                          k == 0, k == KT - 1)
                        if k == KT - 1:
                            last.then_inc(dn, 1)

                def turn_v(p, g):
                    pe.wait_ge(evac, 8 * p + (2 * TV + g + 3))
                    pe.wait_ge(v_copy, 2 * p + (g + 1))
                    for c in range(4):
                        col = (4 * g + c) * P
                        last = pe.transpose(pV[:, c * P:c * P + P], vT[:, col:col + P], K.ident[:, :])
                    last.then_inc(v_turn, 1)

                def score(p, q, r):
                    h, i = ROWS[r]
                    rows_h = slice(HD * h, HD * h + HD)
                    if r == 0:
                        pe.wait_ge(k_lo, p + 1)
                        pe.wait_ge(stacked, 64 * p + 64)
                    pe.wait_ge(biased, 16 * p + (r + 1))
                    for c0 in range(0, (i + 1) * P, H):
                        c1 = min(c0 + H, (i + 1) * P)
                        pe.matmul(scores[:, c0:c1], stack[:, q, h, i * P:i * P + P], stack[:, q, 2 + h, c0:c1],
                                  start=True, stop=False)
                        last = pe.matmul(scores[:, c0:c1], stack[rows_h, q, h, i * P:i * P + P],
                                         k_low[rows_h, q, c0:c1], start=False, stop=True)
                    last.then_inc(qk, 1)

                def turn_weights(p, r):
                    h, i = ROWS[r]
                    pe.wait_ge(ex, 16 * p + (r + 1))
                    for g in range(T_GROUPS[r]):
                        n = T_BEFORE[r] + g
                        pe.wait_ge(tcopy, T_PAIR * p + (n + 1))
                        for b in range(4 * g, min(4 * g + 4, i + 1)):
                            last = pe.transpose(turned[n % 2][:, (b % 4) * P:(b % 4) * P + P],
                                                rows[:, r % 2, b * P:b * P + P], K.ident[:, :])
                        last.then_inc(turn, 1)

                def values(p, q, r):
                    h, i = ROWS[r]
                    if r == 0:
                        pe.wait_ge(v_copy, 2 * p + 3)
                    pe.wait_ge(tcopy, T_PAIR * p + (T_BEFORE[r + 1] + 2))
                    pe.wait_ge(yn, 16 * p + (r + 1))
                    for b in range(i + 1):
                        last = pe.matmul(pO[:, 0:HD], wT[:, r % 2, b * P:b * P + P],
                                         vN[:, q, b * P + HD * h:b * P + HD * h + HD],
                                         start=b == 0, stop=b == i)
                    last.then_inc(pv, 1)

                def turn_y(p, g):
                    if g == 0:
                        pe.wait_ge(yn, 16 * p + 17)
                    pe.wait_ge(tcopy, T_PAIR * p + (T_PAIR + 2))
                    for c in range(4):
                        last = pe.transpose(turned[g][:, c * P:c * P + P], yN[:, 4 * g + c, :], K.ident[:, :])
                    last.then_inc(y_turn, 1)

                def pair(p, q, more):
                    u = 0
                    for slot in range(19):
                        if slot < 16:
                            score(p, q, slot)
                        if more:
                            units(p + 1, u, u + UNITS[slot])
                            u += UNITS[slot]
                        if 1 <= slot <= 16:
                            if slot == 1:
                                pe.wait_ge(y_out, 2 * p + 2)
                            turn_weights(p, slot - 1)
                        if 2 <= slot <= 17:
                            values(p, q, slot - 2)
                        if more and slot in (8, 9):
                            turn_v(p + 1, slot - 8)
                    for g in range(2):
                        turn_y(p, g)

                pe.sem_inc(pv, 2)
                pe.sem_inc(turn, 4)
                for c in range(4):
                    units(0, 16 * c, 16 * c + 16)
                    if c == 1:
                        for g in range(2):
                            turn_v(0, g)
                with pe.Fori(0, 3) as i:
                    for q in range(2):
                        pair(2 * i + q, q, True)
                pair(6, 0, True)
                pair(7, 1, False)

            @block.scalar
            def _(act):
                def split(p, c):
                    if not (isinstance(p, int) and p == 0 and c < 2):
                        act.wait_ge(dn, 8 * p + (2 * c - 2))
                    K.split_hi(act, 2 * p + (n0 // 2 + c // 2), c % 2)

                def copy_v(p, q, g):
                    act.wait_ge(v_turn, 2 * p + (g + 1))
                    if not (isinstance(p, int) and p == 0):
                        act.wait_ge(pv, 16 * p - 14)
                    act.activation(vN[:, q, g * H:g * H + H], pV[:, :], ACT.Copy).then_inc(v_copy, 1)

                def gate(p, q):
                    act.wait_ge(evac, 8 * p + 10)
                    act.activation(gT[:, q, :], gT[:, q, :], ACT.Silu).then_inc(silu, 1)

                def high(p, q, c):
                    act.wait_ge(evac, 8 * p + (2 * c + 4))
                    src, at, done = (qT, 0, q_hi) if c == TQ else (kT, 2, k_hi)
                    for h in range(2):
                        rows_h = slice(HD * h, HD * h + HD)
                        last = act.activation(stack[rows_h, q, at + h, :], src[rows_h, :], ACT.Copy)
                    last.then_inc(done, 1)

                def weights(p, r):
                    h, i = ROWS[r]
                    n = (i + 1) * P
                    act.wait_ge(biased, 16 * p + (r + 2))
                    act.activation(rows[:, r % 2, 0:n], rows[:, r % 2, 0:n], ACT.Exp, scale=-1.0,
                                   bias=stat[:, r:r + 1], accum_out=rsum[:, r:r + 1]).then_inc(ex, 1)

                def copy_weights(p, r):
                    h, i = ROWS[r]
                    act.wait_ge(pv, 16 * p + (r + 1))
                    for g in range(T_GROUPS[r]):
                        n = T_BEFORE[r] + g
                        act.wait_ge(turn, T_PAIR * p + (n + 5))
                        cols = (min(4 * g + 4, i + 1) - 4 * g) * P
                        act.activation(wT[:, r % 2, g * H:g * H + cols], turned[n % 2][:, 0:cols],
                                       ACT.Copy).then_inc(tcopy, 1)

                def pair(p, q, more, more2):
                    for slot in range(19):
                        if slot < 16:
                            weights(p, slot)
                        if 1 <= slot <= 16:
                            copy_weights(p, slot - 1)
                        if more:
                            if slot == 0:
                                split(p + 1, 1)
                            if slot == half_done_slot(0, 1) + 1:
                                split(p + 1, 2)
                            if slot == half_done_slot(1, 1) + 1:
                                split(p + 1, 3)
                            if slot in (9, 10):
                                copy_v(p + 1, 1 - q, slot - 9)
                            for c in (TQ, TK):
                                if slot == half_done_slot(c, 1) + 1:
                                    high(p + 1, 1 - q, c)
                        if more2 and slot == half_done_slot(2, 1) + 1:
                            split(p + 2, 0)
                    if more:
                        gate(p + 1, 1 - q)

                act.sem_inc(v_copy, 1)
                act.sem_inc(tcopy, 2)
                split(0, 0)
                split(0, 1)
                split(0, 2)
                for g in range(2):
                    copy_v(0, 0, g)
                high(0, 0, TQ)
                split(0, 3)
                high(0, 0, TK)
                split(1, 0)
                gate(0, 0)
                with act.Fori(0, 3) as i:
                    for q in range(2):
                        pair(2 * i + q, q, True, True)
                pair(6, 0, True, False)
                pair(7, 1, False, False)

            @block.vector
            def _(dve):
                def split(p, c):
                    K.split_lo(dve, 2 * p + (n0 // 2 + c // 2), c % 2)

                def scale(p, q, c, half):
                    cols = slice(half * H, half * H + H)
                    dve.wait_ge(dn, 8 * p + (2 * c + half + 1))
                    if c == TV and not (isinstance(p, int) and p == 0):
                        dve.wait_ge(v_turn, 2 * p)
                    dst = {TV: vT[:, cols], TQ: qT[:, cols], TK: kT[:, cols], TG: gT[:, q, cols]}[c]
                    if c == TQ:
                        dve.scalar_tensor_tensor(dst, D[:, cols], HD ** -0.5, K.R[:, cols],
                                                 ALU.mult, ALU.mult).then_inc(evac, 1)
                    else:
                        dve.tensor_tensor(dst, D[:, cols], K.R[:, cols], ALU.mult).then_inc(evac, 1)

                def low(p, q, c):
                    src, at, hi_done, done = (qT, 0, q_hi, q_lo) if c == TQ else (kT, 2, k_hi, k_lo)
                    dve.wait_ge(hi_done, p + 1)
                    for h in range(2):
                        rows_h = slice(HD * h, HD * h + HD)
                        dst = q_low[rows_h, :] if c == TQ else k_low[rows_h, q, :]
                        last = dve.tensor_tensor(dst, src[rows_h, :], stack[rows_h, q, at + h, :].bitcast(F32),
                                                 ALU.subtract)
                    last.then_inc(done, 1)

                def add_bias(p, r):
                    h, i = ROWS[r]
                    n = (i + 1) * P
                    dve.wait_ge(qk, 16 * p + (r + 1))
                    if i == 0:
                        dve.wait_ge(b_land[h], 16 * p + 16)
                    dve.wait_ge(turn, T_PAIR * p + (T_BEFORE[r - 1] + 4 if r >= 1 else 2))
                    dve.sem_inc(reduce_go, 1)
                    dve.tensor_tensor_reduce(rows[:, r % 2, 0:n], scores[:, 0:n], bias[:, h, S - n:S],
                                             -1.0, 3e38, ALU.add, ALU.min, stat[:, r:r + 1]).then_inc(biased, 1)

                def normalise(p, r):
                    h, i = ROWS[r]
                    dve.wait_ge(ex, 16 * p + (r + 1))
                    dve.reciprocal(rinv[:, r:r + 1], rsum[:, r:r + 1]).then_inc(ri, 1)
                    dve.wait_ge(ri, 16 * p + (r + 1))
                    dve.wait_ge(pv, 16 * p + (r + 3))
                    if r == 0:
                        dve.wait_ge(y_turn, 2 * p + 1)
                    dve.tensor_scalar(yN[:, i, HD * h:HD * h + HD], pO[:, 0:HD],
                                      rinv[:, r:r + 1], None, ALU.mult).then_inc(yn, 1)

                def output(p, q, g):
                    cols = slice(g * H, g * H + H)
                    dve.wait_ge(y_turn, 2 * p + (g + 2))
                    dve.wait_ge(silu, p + 1)
                    dve.wait_ge(y_free, p + 1)
                    dve.tensor_tensor(y_sb[:, q, cols], turned[g][:, :], gT[:, q, cols], ALU.mult).then_inc(y_out, 1)

                def pair(p, q, more, more2):
                    for slot in range(19):
                        if slot < 16:
                            add_bias(p, slot)
                        if more:
                            for c in range(4):
                                for half in range(2):
                                    if half_done_slot(c, half) + 1 == slot:
                                        scale(p + 1, 1 - q, c, half)
                                if c in (TQ, TK) and slot == half_done_slot(c, 1) + 2:
                                    low(p + 1, 1 - q, c)
                            if slot == 0:
                                split(p + 1, 1)
                            if slot == half_done_slot(0, 1) + 1:
                                split(p + 1, 2)
                            if slot == half_done_slot(1, 1) + 1:
                                split(p + 1, 3)
                        if more2 and slot == half_done_slot(2, 1) + 1:
                            split(p + 2, 0)
                        if 2 <= slot <= 17:
                            normalise(p, slot - 2)
                    if more:
                        scale(p + 1, 1 - q, 3, 1)
                    for g in range(2):
                        output(p, q, g)

                dve.sem_inc(evac, 2)
                dve.sem_inc(biased, 1)
                dve.sem_inc(yn, 1)
                dve.sem_inc(y_out, 2)
                dve.sem_inc(y_free, 2)
                dve.sem_inc(y_turn, 1)
                split(0, 0)
                split(0, 1)
                for c in range(4):
                    for half in range(2):
                        scale(0, 0, c, half)
                    if c < 2:
                        split(0, c + 2)
                    if c in (TQ, TK):
                        low(0, 0, c)
                    if c == 2:
                        split(1, 0)
                with dve.Fori(0, 3) as i:
                    for q in range(2):
                        pair(2 * i + q, q, True, True)
                pair(6, 0, True, False)
                pair(7, 1, False, False)


def stage_pb(K, xhi, xlo, y_dram, y, yhi, ylo, spill, merged):
    nc, n0 = K.nc, FIRST["pb"]
    with ExitStack() as ctx:
        sem = K.semaphores(ctx, "pb_")
        D = ctx.enter_context(nc.psum_tensor("pb_D", [P, 2, S], F32))
        gate, part_a = K.sq[:, 0, :], K.sq[:, 1, :]
        y_hi, y_lo, y_land = sem("y_hi"), sem("y_lo"), [sem(f"y_land{k}") for k in range(KT)]
        mm, g_scaled, g_sig, prod, m_done, a_land = sem("mm"), sem("gs"), sem("sig"), sem("prod"), sem("merged"), sem("a_land")
        with nc.Block() as block:
            @block.sync
            def _(sp):
                for k in range(KT):
                    sp.dma_start(y[:, k, :], y_dram[k, :, :]).then_inc(y_land[k], 16)
                K.load_ahead(sp, "pb")

            @block.gpsimd
            def _(pool):
                with pool.Fori(0, KT) as j:
                    pool.wait_ge(m_done, j + 1)
                    pool.dma_start(part_a, spill[j, :, :]).then_inc(a_land, 16)

            @block.tensor
            def _(pe):
                def tile(j, first=False):
                    pe.wait_ge(K.w_lo, 2 * j + (n0 + 1))
                    if not first:
                        pe.wait_ge(g_scaled, j)
                    K.dense(pe, D[:, 0, :], 0, xhi, xlo).then_inc(mm, 1)
                    pe.wait_ge(K.w_lo, 2 * j + (n0 + 2))
                    if not first:
                        pe.wait_ge(prod, j)
                    K.dense(pe, D[:, 1, :], 1, yhi, ylo, y_lo if first else None).then_inc(mm, 1)

                tile(0, first=True)
                with pe.Fori(1, KT) as j:
                    tile(j)

            @block.scalar
            def _(act):
                def tile(j, last=False):
                    act.wait_ge(g_scaled, j + 1)
                    act.activation(gate, gate, ACT.Sigmoid).then_inc(g_sig, 1)
                    if not last:
                        for s in range(2):
                            act.wait_ge(mm, 2 * j + s + 1)
                            K.split_hi(act, j + (n0 // 2 + 1), s)

                for s in range(2):
                    K.split_hi(act, n0 // 2, s)
                for k in range(KT):
                    act.wait_ge(y_land[k], 16)
                    K.tile_hi(act, yhi, y, k, None, y_hi)
                with act.Fori(0, KT - 1) as j:
                    tile(j)
                tile(KT - 1, last=True)

            @block.vector
            def _(dve):
                def tile(j, last=False):
                    dve.wait_ge(mm, 2 * j + 1)
                    dve.wait_ge(m_done, j + 1)
                    dve.tensor_tensor(gate, D[:, 0, :], K.R[:, :], ALU.mult).then_inc(g_scaled, 1)
                    if not last:
                        K.split_lo(dve, j + (n0 // 2 + 1), 0)
                    dve.wait_ge(mm, 2 * j + 2)
                    dve.wait_ge(g_sig, j + 1)
                    dve.tensor_tensor(gate, D[:, 1, :], gate, ALU.mult).then_inc(prod, 1)
                    dve.wait_ge(prod, j + 1)
                    dve.wait_ge(a_land, 16 * j + 16)
                    dve.tensor_tensor(merged[:, j, :], gate, part_a, ALU.add).then_inc(m_done, 1)
                    if not last:
                        K.split_lo(dve, j + (n0 // 2 + 1), 1)

                dve.sem_inc(m_done, 1)
                for s in range(2):
                    K.split_lo(dve, n0 // 2, s)
                for k in range(KT):
                    K.tile_lo(dve, ylo, yhi, y, k, None, y_hi, y_lo)
                with dve.Fori(0, KT - 1) as j:
                    tile(j)
                tile(KT - 1, last=True)


def stage_residual(K, name, src, xhi, xlo, f_sb, x_dram):
    nc, n0 = K.nc, FIRST[name]
    with ExitStack() as ctx:
        sem = K.semaphores(ctx, name + "_")
        D = ctx.enter_context(nc.psum_tensor(name + "_D", [P, 2, S], F32))
        x_hi, x_lo, mm, added, landed = sem("x_hi"), sem("x_lo"), sem("mm"), sem("added"), sem("landed")
        sq_done, acc_done, copy_go = sem("sq"), sem("acc"), sem("copy_go")
        with nc.Block() as block:
            @block.sync
            def _(sp):
                sp.dma_start(f_sb[:, :, :], x_dram).then_inc(landed, 16)
                K.load_ahead(sp, name)

            @block.gpsimd
            def _(pool):
                K.sum_tiles(pool, K.sq, sq_done, acc_done, copy_go)

            @block.tensor
            def _(pe):
                def tiles(i, first=False):
                    for s in range(2):
                        n = 2 * i + s
                        pe.wait_ge(K.w_lo, n + (n0 + 1))
                        if not first:
                            pe.wait_ge(added, n - 1)
                        K.dense(pe, D[:, s, :], s, xhi, xlo, x_lo if first and s == 0 else None).then_inc(mm, 1)

                tiles(0, first=True)
                with pe.Fori(1, KT // 2) as i:
                    tiles(i)

            @block.scalar
            def _(act):
                for s in range(2):
                    K.split_hi(act, n0 // 2, s)
                for k in range(KT):
                    K.tile_hi(act, xhi, src, k, None, x_hi)

                def tiles(i, first=False, last=False):
                    for s in range(2):
                        n = 2 * i + s
                        if not last:
                            act.wait_ge(mm, n + 1)
                            K.split_hi(act, i + (n0 // 2 + 1), s)
                        K.square_tile(act, K.sq[:, s, :], f_sb[:, n, :], n, added, n + 1, acc_done,
                                      first).then_inc(sq_done, 1)

                tiles(0, first=True)
                with act.Fori(1, KT // 2 - 1) as i:
                    tiles(i)
                tiles(KT // 2 - 1, last=True)

            @block.vector
            def _(dve):
                def tiles(i, last=False):
                    for s in range(2):
                        n = 2 * i + s
                        dve.wait_ge(mm, n + 1)
                        dve.tensor_tensor(f_sb[:, n, :], D[:, s, :], f_sb[:, n, :], ALU.add).then_inc(added, 1)
                        if not last:
                            K.split_lo(dve, i + (n0 // 2 + 1), s)

                for s in range(2):
                    K.split_lo(dve, n0 // 2, s)
                for k in range(KT):
                    K.tile_lo(dve, xlo, xhi, src, k, None, x_hi, x_lo)
                dve.wait_ge(landed, 16)
                with dve.Fori(0, KT // 2 - 1) as i:
                    tiles(i)
                tiles(KT // 2 - 1, last=True)


SH = 32
GH = SH // GROUPS
SD = 64
GC = GH * SD
TAPS = 4
Z_FIRST, Z_UNITS, Z_LAST = 16, [(1, 3)] * 8 + [(1, 4), (0, 0)], 11
assert Z_FIRST + sum(a + b for a, b in Z_UNITS) + Z_LAST == GT * 2 * KT
OUTS = 6 * 2 + GT * 2 + KT * 2


def stage_dt(K, x_sb, f_sb, xhi, xlo, dt, dte, acum, e_acum, e_end, acum_dram):
    nc, io = K.nc, K.io
    with ExitStack() as ctx:
        sem = K.semaphores(ctx, "dt_")
        sb = lambda n, shape, dt=F32: ctx.enter_context(nc.sbuf_tensor("dt_" + n, shape, dt))
        D = ctx.enter_context(nc.psum_tensor("dt_D", [P, S], F32))
        spread = ctx.enter_context(nc.psum_tensor("dt_spread", [P, S], F32))
        sums = ctx.enter_context(nc.psum_tensor("dt_sums", [P, H], F32))
        pN = ctx.enter_context(nc.psum_tensor("dt_pN", [P, H], F32))
        pA = ctx.enter_context(nc.psum_tensor("dt_pA", [P, H], F32))
        raw, hi, lo = sb("raw", [P, KT, P]), sb("hi", [P, KT, P], F32R), sb("lo", [P, KT, P], F32R)
        tri = sb("tri", [P, P])
        head = sb("head", [P, 2, SH])
        expA = sb("expA", [P, SH])
        rows = sb("rows", [SH, S])
        W = NC * SH
        v, e, l, d, r, dA, end = (sb(n, [P, W]) for n in ("v", "e", "l", "d", "r", "dA", "end"))
        f_done, x_hi, x_lo, sq_done, acc_done = sem("f"), sem("x_hi"), sem("x_lo"), sem("sq"), sem("acc")
        sums_done, root_done, rtok_done = sem("sums"), sem("root"), sem("rtok")
        diag_done, spread_done, r_done = sem("diag"), sem("spread"), sem("r")
        sums2, root2, rtok2, diag2, spread2, r2 = (sem(n + "2") for n in ("sums", "root", "rtok", "diag", "spread", "r"))
        landed, h_done, l_done, mm = sem("landed"), sem("hi"), sem("lo"), sem("mm")
        a_step, v_step, t_step, stored = sem("a_step"), sem("v_step"), sem("t_step"), sem("stored")
        copied, copy_go = sem("copied"), sem("copy_go")
        by_head = lambda t: t.rearrange("p (c h) -> p c h", c=NC)
        all_blocks = lambda t: t.unsqueeze(1).to_broadcast([P, NC, SH])
        with nc.Block() as block:
            @block.sync
            def _(sp):
                sp.dma_start(raw[:, :, :], io["w_dt"][:, :, :]).then_inc(landed, 16)
                sp.dma_start(head[:, :, :], io["dt_head"][:, :].partition_broadcast(P)).then_inc(landed, 16)
                sp.dma_start(tri[:, :], io["causal"][:, :]).then_inc(landed, 16)
                sp.wait_ge(copied, 2)
                sp.dma_start(acum_dram, rows[:, :]).then_inc(stored, 16)
                sp.wait_ge(stored, 16)

            @block.tensor
            def _(pe):
                K.norm_sums(pe, sums, sums_done)
                K.norm_spread(pe, spread, diag_done, spread_done)
                pe.wait_ge(l_done, 1)
                for k in range(KT):
                    pe.wait_ge(x_lo, k + 1)
                    for half in range(2):
                        cols = slice(half * H, half * H + H)
                        pe.matmul(D[:, cols], hi[:, k, :], xhi[:, k, cols], start=k == 0, stop=False)
                        pe.matmul(D[:, cols], hi[:, k, :], xlo[:, k, cols], start=False, stop=False)
                        last = pe.matmul(D[:, cols], lo[:, k, :], xhi[:, k, cols], start=False, stop=k == KT - 1)
                last.then_inc(mm, 1)
                pe.wait_ge(acc_done, KT)
                K.norm_sums(pe, sums, sums2)
                pe.wait_ge(copied, 1)
                for c in range(NC):
                    last = pe.transpose(pN[:, c * SH:c * SH + SH], rows[:, c * P:c * P + P], K.ident[0:SH, 0:SH])
                last.then_inc(t_step, 1)
                pe.wait_ge(r_done, 1)
                K.norm_spread(pe, spread, diag2, spread2)
                pe.wait_ge(v_step, 9)
                for c in range(NC):
                    last = pe.matmul(D[0:SH, c * P:c * P + P], dA[:, c * SH:c * SH + SH], tri[:, :],
                                     start=True, stop=True)
                last.then_inc(t_step, 1)
                pe.matmul(pA[:, 0:W], tri[:, :], dA[:, :], start=True, stop=True)
                pe.matmul(pA[:, W:2 * W], K.ones[:, :], dA[:, :], start=True, stop=True).then_inc(t_step, 1)

            @block.scalar
            def _(act):
                act.wait_ge(landed, 48)
                K.norm_root(act, sums, DM, sums_done, root_done)
                act.activation(hi[:, :, :], raw[:, :, :], ACT.Copy).then_inc(h_done, 1)
                act.activation(expA[:, :], head[:, 1, :], ACT.Exp).then_inc(a_step, 1)
                for k in range(KT):
                    act.wait_ge(f_done, k + 1)
                    K.tile_hi(act, xhi, f_sb, k, "m_norm", x_hi)
                    K.square(act, f_sb[:, k, :], k, sq_done, acc_done)
                K.norm_root(act, sums, DM, sums2, root2)
                act.wait_ge(mm, 1)
                act.activation(rows[:, :], D[0:SH, :], ACT.Copy).then_inc(copied, 1)
                act.wait_ge(v_step, 2)
                act.activation(e[:, :], v[:, :], ACT.Abs).then_inc(a_step, 1)
                act.wait_ge(a_step, 2)
                act.activation(e[:, :], e[:, :], ACT.Exp, scale=-1.0).then_inc(a_step, 1)
                act.wait_ge(a_step, 3)
                act.activation(l[:, :], e[:, :], ACT.Ln, bias=K.ones[:, 0:1]).then_inc(a_step, 1)
                act.wait_ge(t_step, 2)
                act.activation(rows[:, :], D[0:SH, :], ACT.Copy).then_inc(copied, 1)
                act.wait_ge(v_step, 11)
                act.activation(e_acum[:, :], acum[:, :], ACT.Exp).then_inc(a_step, 1)
                act.activation(dte[:, :], dte[:, :], ACT.Exp).then_inc(a_step, 1)
                act.wait_ge(v_step, 12)
                act.activation(e_end[:, :], end[:, :], ACT.Exp).then_inc(a_step, 1)

            @block.vector
            def _(dve):
                dve.wait_ge(h_done, 1)
                dve.tensor_tensor(lo[:, :, :], raw[:, :, :], hi[:, :, :].bitcast(F32), ALU.subtract).then_inc(l_done, 1)
                K.norm_recip(dve, root_done, rtok_done)
                K.norm_diag(dve, diag_done)
                K.norm_copy(dve, spread, spread_done, r_done)
                for k in range(KT + 1):
                    if k < KT:
                        dve.scalar_tensor_tensor(f_sb[:, k, :], x_sb[:, k, :], K.gain("g_final", k), K.R[:, :],
                                                 ALU.mult, ALU.mult).then_inc(f_done, 1)
                    if k >= 1:
                        dve.wait_ge(f_done, k)
                        K.tile_lo(dve, xlo, xhi, f_sb, k - 1, "m_norm", x_hi, x_lo)
                dve.wait_ge(diag_done, 1)
                dve.wait_ge(f_done, KT)
                K.norm_recip(dve, root2, rtok2)
                K.norm_diag(dve, diag2)
                steps = [0]

                def step(ins):
                    steps[0] += 1
                    ins.then_inc(v_step, 1)
                    dve.wait_ge(v_step, steps[0])

                dve.wait_ge(t_step, 1)
                step(dve.tensor_tensor(by_head(v[:, :]), by_head(pN[:, 0:W]),
                                       K.rtok[:, :].unsqueeze(2).to_broadcast([P, NC, SH]), ALU.mult))
                dve.wait_ge(landed, 48)
                step(dve.tensor_tensor(by_head(v[:, :]), by_head(v[:, :]), all_blocks(head[:, 0, :]), ALU.add))
                K.norm_copy(dve, spread, spread2, r2)
                dve.wait_ge(a_step, 4)
                step(dve.tensor_scalar(d[:, :], e[:, :], 1.0, None, ALU.add))
                step(dve.tensor_scalar(d[:, :], d[:, :], -1.0, 1e-30, ALU.add, ALU.add))
                step(dve.reciprocal(r[:, :], d[:, :]))
                step(dve.scalar_tensor_tensor(l[:, :], l[:, :], 1e-30, r[:, :], ALU.add, ALU.mult))
                step(dve.tensor_tensor(l[:, :], l[:, :], e[:, :], ALU.mult))
                step(dve.scalar_tensor_tensor(dt[:, :], v[:, :], 0.0, l[:, :], ALU.max, ALU.add))
                step(dve.scalar_tensor_tensor(by_head(dA[:, :]), by_head(dt[:, :]), -1.0, all_blocks(expA[:, :]),
                                              ALU.mult, ALU.mult))
                dve.wait_ge(t_step, 3)
                step(dve.tensor_copy(acum[:, :], pA[:, 0:W]))
                step(dve.tensor_tensor(dte[:, :], pA[:, W:2 * W], acum[:, :], ALU.subtract))
                dve.tensor_copy(end[:, :], pA[:, W:2 * W]).then_inc(v_step, 1)
                dve.wait_ge(a_step, 6)
                dve.tensor_tensor(dte[:, :], dte[:, :], dt[:, :], ALU.mult)

            @block.gpsimd
            def _(pool):
                K.sum_squares(pool, KT, sq_done, acc_done)


def stage_ssm(K, xhi, xlo, f_sb, dt, dte, acum, e_acum, e_end, acum_dram):
    nc, io, n0 = K.nc, K.io, FIRST["ssm"]
    LAST = GROUPS - 1
    with ExitStack() as ctx:
        sem = K.semaphores(ctx, "ssm_")
        sb = lambda n, shape, dt=F32: ctx.enter_context(nc.sbuf_tensor("ssm_" + n, shape, dt))
        D = ctx.enter_context(nc.psum_tensor("ssm_D", [P, S], F32))
        pX = ctx.enter_context(nc.psum_tensor("ssm_pX", [P, H], F32))
        pCB = ctx.enter_context(nc.psum_tensor("ssm_pCB", [P, H], F32))
        pY = ctx.enter_context(nc.psum_tensor("ssm_pY", [P, S], F32))
        pS = ctx.enter_context(nc.psum_tensor("ssm_pS", [P, H], F32))
        pT = ctx.enter_context(nc.psum_tensor("ssm_pT", [P, H], F32))
        banks = [D[:, 0:H], D[:, H:S], pX[:, :], pT[:, :]]
        BC = sb("BC", [P, 2, S])
        xs = sb("xs", [P, GT, S])
        with ExitStack() as shared:
            xd_odd = shared.enter_context(nc.sbuf_tensor("ssm_xd_odd", [P, S], F32))
        yhi = sb("yhi", [P, GT, S], F32R)
        with ExitStack() as shared:
            z = shared.enter_context(nc.sbuf_tensor("ssm_z", [P, GT, S], F32))
        ylo = sb("ylo", [P, GT, S], F32R)
        cb = sb("cb", [P, 2, 2, P])
        state, decayed = sb("state", [P, GC]), sb("decayed", [P, GC])
        y_sb = sb("y_sb", [P, GC])
        u = K.sq
        E = [K.sq[:, s, :].rearrange("p (h l) -> p h l", h=GH) for s in range(2)]
        x_dt, x_dte = [t[:, 0:GC] for t in (K.acc[:, :], xd_odd)], [t[:, GC:2 * GC] for t in (K.acc[:, :], xd_odd)]
        tmp = K.sq[:, 1, :]

        dn, evac = sem("dn"), sem("evac")
        cv_a, cv_d, cv_s = sem("cv_a"), sem("cv_d"), sem("cv_s")
        row_land = [sem("row0"), sem("row1")]
        seg, sel, ex, weighted, select_go = sem("seg"), sem("sel"), sem("ex"), sem("weighted"), sem("select_go")
        s1, ps_done, s2, s3, cb_copy, xd = sem("s1"), sem("ps"), sem("s2"), sem("s3"), sem("cb_copy"), sem("xd")
        y_inter, y_done, st_decay, st_done, y_turned = sem("y_inter"), sem("y_done"), sem("st_decay"), sem("st_done"), sem("y_turned")
        silu, yz, y_hi, y_lo = sem("silu"), sem("yz"), sem("y_hi"), sem("y_lo")
        sq_done, acc_done = sem("sq"), sem("acc")
        sums_done, root_done, rtok_done = sem("sums"), sem("root"), sem("rtok")
        diag_done, spread_done, r_done, scaled = sem("diag"), sem("spread"), sem("r"), sem("scaled")
        Rg = K.acc

        def heads(t, c, g, width):
            return t[:, bass.ds(8 * g + c * SH, GH)].unsqueeze(2).to_broadcast([P, GH, width])

        with nc.Block() as block:
            @block.sync
            def _(sp):
                def group(g):
                    def load(m):
                        n = GROUP_TILES * g + (n0 + m)
                        sp.wait_ge(K.w_lo, n + 1)
                        K.load_weight(sp, n + 2, m % 2)

                    def row(c):
                        if c == 0:
                            sp.wait_ge(cv_d, 18 * g + 18)
                        if c >= 2:
                            sp.wait_ge(s2, 8 * g + (c - 1))
                        sp.dma_start(E[c % 2], acum_dram[bass.ds(8 * g, GH), c * P:c * P + P]
                                     .partition_broadcast(P)).then_inc(row_land[c % 2], 16)

                    for m in range(6):
                        load(m)
                    for c in range(NC):
                        row(c)
                        if c % 2 == 1:
                            load(6 + c // 2)
                    for m in range(10, 14):
                        load(m)

                with sp.Fori(0, GROUPS) as g:
                    group(g)

            @block.tensor
            def _(pe):
                def units(g, c, a, b):
                    for q in range(a, b):
                        half, k = q // KT, q % KT
                        if q == 0:
                            pe.wait_ge(K.w_lo, GROUP_TILES * g + (n0 + c + 1))
                        if k == 0:
                            pe.wait_ge(evac, OUTS * g + (2 * c + half + 1))
                        last = K.products(pe, D[:, half * H:half * H + H], c % 2, k, k, xhi, xlo, half,
                                          k == 0, k == KT - 1)
                        if k == KT - 1:
                            last.then_inc(dn, 1)

                def turn_in(g, c):
                    cols = slice(c * P, c * P + P)
                    if c == 0:
                        pe.wait_ge(cv_s, 6 * g + 6)
                    pe.wait_ge(xd, 8 * g + (c + 1))
                    pe.wait_ge(cb_copy, 8 * g + (c + 1))
                    for k in range(GT):
                        pe.transpose(pX[:, k * P:k * P + P], xs[:, k, cols], K.ident[:, :])
                    pe.transpose(pCB[:, P:2 * P], BC[:, 0, cols], K.ident[:, :])
                    pe.matmul(pCB[:, 0:P], BC[:, 0, cols], BC[:, 1, cols], start=True, stop=True).then_inc(s1, 1)

                def products(g, c):
                    pe.wait_ge(st_done, 9 * g + (c + 1))
                    pe.wait_ge(y_done, 8 * g + (c + 1))
                    pe.matmul(pY[:, 0:H], BC[:, 1, c * P:c * P + P], state[:, :], start=True, stop=True)
                    pe.wait_ge(xd, 8 * g + (c + 2))
                    pe.wait_ge(cb_copy, 8 * g + (c + 2))
                    pe.matmul(pS[:, :], cb[:, c % 2, 1, :], x_dte[c % 2], start=True, stop=True).then_inc(ps_done, 1)
                    pe.wait_ge(weighted, 8 * g + (c + 1))
                    for h in range(GH):
                        last = pe.matmul(pY[:, H + h * SD:H + h * SD + SD], E[c % 2][:, h, :],
                                         x_dt[c % 2][:, h * SD:h * SD + SD], start=True, stop=True)
                    last.then_inc(s2, 1)

                def turn_out(g, c):
                    pe.wait_ge(y_done, 8 * g + (c + 2))
                    pe.wait_ge(y_turned, 8 * g + (c + 1))
                    for k in range(GT):
                        last = pe.transpose(pT[:, k * P:k * P + P], y_sb[:, k * P:k * P + P], K.ident[:, :])
                    last.then_inc(s3, 1)

                def group(g):
                    for c in range(6):
                        units(g, c, 0, 16)
                    def z_units(a, b):
                        for q in range(a, b):
                            units(g, 6 + q // 16, q % 16, q % 16 + 1)

                    z_units(0, Z_FIRST)
                    turn_in(g, 0)
                    q = Z_FIRST
                    for slot in range(10):
                        for part, n in enumerate(Z_UNITS[slot]):
                            z_units(q, q + n)
                            q += n
                            if part == 0 and 1 <= slot <= 8:
                                products(g, slot - 1)
                        if slot >= 2:
                            turn_out(g, slot - 2)
                        if slot < 7:
                            turn_in(g, slot + 1)
                    z_units(q, q + Z_LAST)

                    def out_products(o, k):
                        j, half = o // 2, o % 2
                        return K.products(pe, banks[o % 4], j // 2 % 2, 4 * (j % 2) + k, k, yhi, ylo, half,
                                          k == 0, k == GT - 1)

                    pe.wait_ge(K.w_lo, GROUP_TILES * g + (n0 + 11))
                    pe.wait_ge(xd, 8 * g + 9)
                    pe.wait_ge(y_turned, 8 * g + 9)
                    for o in (2, 3, 0, 1):
                        if o < 2:
                            pe.wait_ge(evac, OUTS * g + (20 + o + 1))
                        for k in range(GT - 1):
                            if o == 2:
                                pe.wait_ge(y_lo, 4 * g + (k + 1))
                            out_products(o, k)
                    pe.wait_ge(y_lo, 4 * g + 4)
                    for o in range(4):
                        out_products(o, GT - 1).then_inc(dn, 1)
                    pe.wait_ge(acc_done, 4 * g + 4)
                    K.norm_sums(pe, pCB, sums_done)
                    pe.wait_ge(diag_done, g + 1)
                    for half in range(2):
                        last = pe.matmul(pY[:, half * H:half * H + H], K.ones[:, :],
                                         K.sq[:, 0, half * H:half * H + H], start=True, stop=True)
                    last.then_inc(spread_done, 1)
                    for o in range(4, 2 * KT):
                        if o % 4 == 0:
                            pe.wait_ge(K.w_lo, GROUP_TILES * g + (n0 + 11 + o // 4))
                        pe.wait_ge(evac, OUTS * g + (20 + o - 1))
                        for k in range(GT):
                            last = out_products(o, k)
                        last.then_inc(dn, 1)

                with pe.Fori(0, GROUPS) as g:
                    group(g)

            @block.scalar
            def _(act):
                def split(g, m, outs):
                    act.wait_ge(dn, OUTS * g + outs)
                    K.split_hi(act, 7 * g + (n0 // 2 + m // 2), m % 2)

                def conv_tile(c, g):
                    return (BC[:, c, :], 16 + 4 * c + g) if c < 2 else (xs[:, c - 2, :], 4 * g + (c - 2))

                def group(g, last=False):
                    for c in range(6):
                        dst, t = conv_tile(c, g)
                        act.wait_ge(evac, OUTS * g + (2 * c + 4))
                        act.activation(dst, u[:, c % 2, :], ACT.Identity,
                                       scale=K.vec[:, bass.ds(4 * t + (VEC["conv_w"] + 3), 1)],
                                       bias=K.vec[:, bass.ds(t + VEC["conv_b"], 1)]).then_inc(cv_a, 1)
                        split(g, c + 2, 2 * c + 2)
                        act.wait_ge(cv_d, 18 * g + (3 * c + 3))
                        act.activation(dst, dst, ACT.Silu).then_inc(cv_s, 1)

                    def silu_z(zt):
                        act.wait_ge(evac, OUTS * g + (12 + 2 * zt + 4))
                        act.activation(z[:, zt, :], z[:, zt, :], ACT.Silu).then_inc(silu, 1)
                        split(g, 8 + zt, 14 + 2 * zt)

                    silu_z(0)
                    q = Z_FIRST
                    for slot in range(10):
                        if slot < 8:
                            c = slot
                            act.wait_ge(s1, 8 * g + (c + 1))
                            if c >= 2:
                                act.wait_ge(s2, 8 * g + (c - 1))
                            act.activation(cb[:, c % 2, :, :], pCB[:, 0:2 * P].rearrange("p (a b) -> p a b", a=2),
                                           ACT.Copy).then_inc(cb_copy, 1)
                            act.wait_ge(sel, 8 * g + (c + 1))
                            act.activation(E[c % 2], E[c % 2], ACT.Exp).then_inc(ex, 1)
                        q_old, q = q, q + sum(Z_UNITS[slot])
                        if q // 16 > q_old // 16:
                            silu_z(q // 16 - 1)
                    for k in range(GT):
                        if k == GT - 1:
                            silu_z(k)
                        act.wait_ge(yz, 4 * g + (k + 1))
                        act.activation(yhi[:, k, :], xs[:, k, :], ACT.Copy,
                                       scale=K.vec[:, bass.ds(4 * g + (VEC["y_norm"] + k), 1)]).then_inc(y_hi, 1)
                        if k >= 2:
                            act.wait_ge(acc_done, 4 * g + (k - 1))
                        act.activation(K.sq[:, k % 2, :], xs[:, k, :], ACT.Square).then_inc(sq_done, 1)
                    act.wait_ge(sums_done, g + 1)
                    act.activation(K.root[:, :], pCB[:, 0:NC], ACT.Sqrt, scale=1.0 / GC,
                                   bias=K.eps[:, 0:1]).then_inc(root_done, 1)
                    for m in range(4):
                        if m < 2 or not last:
                            split(g, 12 + m, 24 + 4 * m)

                split0 = lambda s: K.split_hi(act, n0 // 2, s)
                split0(0)
                split0(1)
                act.sem_inc(cb_copy, 1)
                with act.Fori(0, LAST) as g:
                    group(g)
                group(LAST, last=True)

            @block.vector
            def _(dve):
                def split(g, m):
                    K.split_lo(dve, 7 * g + (n0 // 2 + m // 2), m % 2)

                def scale(g, o, dst, half):
                    cols = slice(half * H, half * H + H)
                    dve.wait_ge(dn, OUTS * g + (o + 1))
                    dve.tensor_tensor(dst[:, cols], D[:, cols], K.R[:, cols], ALU.mult).then_inc(evac, 1)

                def block_work(g, c):
                    pXh = pX[:, :].rearrange("p (h d) -> p h d", h=GH)
                    dve.wait_ge(s1, 8 * g + (c + 1))
                    dve.tensor_tensor(x_dt[c % 2].rearrange("p (h d) -> p h d", h=GH), pXh, heads(dt, c, g, SD),
                                      ALU.mult)
                    dve.tensor_tensor(x_dte[c % 2].rearrange("p (h d) -> p h d", h=GH), pXh, heads(dte, c, g, SD),
                                      ALU.mult).then_inc(xd, 1)

                def weigh(g, c):
                    dve.wait_ge(ex, 8 * g + (c + 1))
                    dve.wait_ge(cb_copy, 8 * g + (c + 2))
                    dve.tensor_tensor(E[c % 2], E[c % 2], cb[:, c % 2, 0, :].unsqueeze(1).to_broadcast([P, GH, P]),
                                      ALU.mult).then_inc(weighted, 1)

                def finish(g, c):
                    y3 = y_sb[:, :].rearrange("p (h d) -> p h d", h=GH)
                    dve.wait_ge(ps_done, 8 * g + (c + 1))
                    dve.wait_ge(st_decay, 8 * g + (c + 1))
                    dve.tensor_tensor(state[:, :], decayed[:, :], pS[:, :], ALU.add).then_inc(st_done, 1)
                    dve.wait_ge(s2, 8 * g + (c + 1))
                    if c >= 1:
                        dve.wait_ge(s3, 8 * g + c)
                    dve.tensor_tensor(y3, pY[:, 0:H].rearrange("p (h d) -> p h d", h=GH),
                                      heads(e_acum, c, g, SD), ALU.mult).then_inc(y_inter, 1)
                    dve.wait_ge(y_inter, 8 * g + (c + 1))
                    dve.tensor_tensor(y_sb[:, :], y_sb[:, :], pY[:, H:S], ALU.add).then_inc(y_done, 1)

                def skip(g, c):
                    cols = slice(c * P, c * P + P)
                    dve.wait_ge(s3, 8 * g + (c + 1))
                    for k in range(GT):
                        last = dve.scalar_tensor_tensor(xs[:, k, cols], xs[:, k, cols],
                                                        K.vec[:, bass.ds(4 * g + (VEC["d_skip"] + k), 1)],
                                                        pT[:, k * P:k * P + P], ALU.mult, ALU.add)
                    last.then_inc(y_turned, 1)

                def group(g, last=False):
                    for c in range(6):
                        dst, t = (BC[:, c, :], 16 + 4 * c + g) if c < 2 else (xs[:, c - 2, :], 4 * g + (c - 2))
                        for half in range(2):
                            scale(g, 2 * c + half, u[:, c % 2, :], half)
                        dve.wait_ge(cv_a, 6 * g + (c + 1))
                        for tap in range(3):
                            lag = 3 - tap
                            w = K.vec[:, bass.ds(4 * t + (VEC["conv_w"] + tap), 1)]
                            dve.scalar_tensor_tensor(dst[:, lag:S], u[:, c % 2, 0:S - lag], w, dst[:, lag:S],
                                                     ALU.mult, ALU.add).then_inc(cv_d, 1)
                            dve.wait_ge(cv_d, 18 * g + (3 * c + tap + 1))
                        split(g, c + 2)
                    def scale_z(o):
                        scale(g, 12 + o, z[:, o // 2, :], o % 2)
                        if o % 2 == 1:
                            split(g, 8 + o // 2)

                    dve.memset(state[:, :], 0.0).then_inc(st_done, 1)
                    scale_z(0)
                    scale_z(1)
                    block_work(g, 0)
                    weigh(g, 0)
                    q = Z_FIRST
                    for slot in range(10):
                        if 1 <= slot <= 8:
                            if slot < 8:
                                block_work(g, slot)
                            finish(g, slot - 1)
                            if slot < 8:
                                weigh(g, slot)
                        q_old, q = q, q + sum(Z_UNITS[slot])
                        if q // 8 > q_old // 8:
                            scale_z(q // 8 - 1)
                        if slot >= 2:
                            skip(g, slot - 2)
                    dve.wait_ge(y_turned, 8 * g + 9)

                    def gate_y(k):
                        dve.wait_ge(silu, 4 * g + (k + 1))
                        dve.tensor_tensor(xs[:, k, :], xs[:, k, :], z[:, k, :], ALU.mult).then_inc(yz, 1)

                    def low_y(k):
                        dve.wait_ge(y_hi, 4 * g + (k + 1))
                        dve.scalar_tensor_tensor(ylo[:, k, :], xs[:, k, :],
                                                 K.vec[:, bass.ds(4 * g + (VEC["y_norm"] + k), 1)],
                                                 yhi[:, k, :].bitcast(F32), ALU.mult, ALU.subtract).then_inc(y_lo, 1)

                    gate_y(0)
                    scale_z(6)
                    for k in range(1, GT - 1):
                        gate_y(k)
                        low_y(k - 1)
                    scale_z(7)
                    low_y(GT - 2)
                    gate_y(GT - 1)
                    low_y(GT - 1)
                    dve.wait_ge(root_done, g + 1)
                    dve.reciprocal(K.rtok[:, :], K.root[:, :]).then_inc(rtok_done, 1)
                    dve.wait_ge(rtok_done, g + 1)
                    K.norm_diag(dve, diag_done)
                    dve.wait_ge(spread_done, g + 1)
                    dve.tensor_copy(Rg[:, :], pY[:, :]).then_inc(r_done, 1)
                    dve.wait_ge(r_done, g + 1)
                    for j in range(KT):
                        for half in range(2):
                            cols = slice(half * H, half * H + H)
                            dve.wait_ge(dn, OUTS * g + (20 + 2 * j + half + 1))
                            dve.tensor_tensor(tmp[:, cols], banks[(2 * j + half) % 4], Rg[:, cols],
                                              ALU.mult).then_inc(evac, 1)
                            dve.wait_ge(evac, OUTS * g + (20 + 2 * j + half + 3))
                            dve.tensor_tensor(f_sb[:, j, cols], f_sb[:, j, cols], tmp[:, cols], ALU.add).then_inc(scaled, 1)
                        if j % 2 == 1 and (j < 4 or not last):
                            split(g, 12 + j // 2)
                        dve.wait_ge(scaled, 16 * g + (2 * j + 2))

                dve.sem_inc(evac, 2)
                for q in (xd, y_done, y_turned):
                    dve.sem_inc(q, 1)
                for s in range(2):
                    K.split_lo(dve, n0 // 2, s)
                with dve.Fori(0, LAST) as g:
                    group(g)
                group(LAST, last=True)

            @block.gpsimd
            def _(pool):
                def group(g):
                    for c in range(NC):
                        pool.wait_ge(st_done, 9 * g + (c + 1))
                        pool.tensor_tensor(decayed[:, :].rearrange("p (h d) -> p h d", h=GH),
                                           state[:, :].rearrange("p (h d) -> p h d", h=GH),
                                           heads(e_end, c, g, SD), ALU.mult).then_inc(st_decay, 1)
                        for b in ([0, 1] if c == 0 else [c + 1] if c + 1 < NC else []):
                            pool.wait_ge(row_land[b % 2], 64 * g + (16 * (b // 2) + 16))
                            pool.tensor_tensor(E[b % 2], E[b % 2], heads(acum, b, g, P), ALU.subtract).then_inc(seg, 1)
                            pool.wait_ge(seg, 8 * g + (b + 1))
                            pool.sem_inc(select_go, 1)
                            pool.affine_select(out=E[b % 2], in_=E[b % 2], compare_op=ALU.is_ge, fill=NEG, base=0,
                                               pattern=[[0, GH], [1, P]], channel_multiplier=-1).then_inc(sel, 1)
                    for k in range(GT):
                        pool.wait_ge(sq_done, 4 * g + (k + 1))
                        if k == 0:
                            pool.sem_inc(select_go, 1)
                            pool.tensor_copy(K.acc[:, :], K.sq[:, 0, :]).then_inc(acc_done, 1)
                        else:
                            pool.wait_ge(acc_done, 4 * g + k)
                            pool.tensor_tensor(K.acc[:, :], K.acc[:, :], K.sq[:, k % 2, :], ALU.add).then_inc(acc_done, 1)

                with pool.Fori(0, GROUPS) as g:
                    group(g)


AUX_SLOT = dict(k_square=6, k_sum=7, k_turn0=8, k_turn1=9, k_back0=10, k_back1=11, v_turn0=12,
                v_turn1=13, q_square=16, q_sum=17)


def stage_stick(K, xhi, xlo, out, f_dram):
    nc, io = K.nc, K.io
    name = "stick"
    n0 = FIRST[name]
    TK, TV, TQ, TG = range(4)
    with ExitStack() as ctx:
        sem = K.semaphores(ctx, name + "_")
        sb = lambda n, shape: ctx.enter_context(nc.sbuf_tensor(f"{name}_{n}", shape, F32))
        ps = lambda n, cols: ctx.enter_context(nc.psum_tensor(f"{name}_{n}", [P, cols], F32))
        D = ps("D", S)
        scores = ps("scores", S)
        turned = [ps(f"turned{b}", H) for b in range(2)]
        pO = ps("pO", H)
        pV = ps("pV", H)
        qT, kT, vN, gT = (sb(n, [P, 2, S]) for n in ("qT", "kT", "vN", "gT"))
        vT = K.acc
        keep = sb("keep", [P, 2, S + 1])
        rows = sb("rows", [P, 2, S])
        wT = sb("wT", [P, 2, S])
        yN = sb("yN", [P, NC, P])
        k_root, k_inv = sb("k_root", [P, 16]), sb("k_inv", [P, 16])
        q_root, q_inv = sb("q_root", [P, 16]), sb("q_inv", [P, 16])
        q_pos, q_neg = sb("q_pos", [P, 2, 16]), sb("q_neg", [P, 2, 16])
        gains = sb("gains", [P, 1])
        select = sb("select", [P, 2])
        raw_mask = sb("raw_mask", [P, P])
        identr = ctx.enter_context(nc.sbuf_tensor("stick_identr", [P, P], F32R))
        maskr = ctx.enter_context(nc.sbuf_tensor("stick_maskr", [P, P], F32R))
        kRaw, square, kN = K.sq[:, 0, :], K.sq[:, 1, :], K.sq[:, 1, :]

        dn, evac = sem("dn"), sem("evac")
        v_turn, v_copy = sem("v_turn"), sem("v_copy")
        qk, sig, scan, ex = sem("qk"), sem("sig"), sem("scan"), sem("ex")
        squared, summed, rooted, k_ready, q_ready = sem("squared"), sem("summed"), sem("rooted"), sem("k_ready"), sem("q_ready")
        k_turn, kn_done, k_back, k_done = sem("k_turn"), sem("kn_done"), sem("k_back"), sem("k_done")
        landed, masks, w_gain, recip = sem("landed"), sem("masks"), sem("w_gain"), sem("recip")
        turn, tcopy, pv, yn = sem("turn"), sem("tcopy"), sem("pv"), sem("yn")
        y_turn, y_out, silu = sem("y_turn"), sem("y_out"), sem("silu")

        x_hi, x_lo, sums_done, root_done = sem("x_hi"), sem("x_lo"), sem("sums"), sem("root")
        rtok_done, diag_done, spread_done, r_done = sem("rtok"), sem("diag"), sem("spread"), sem("r")
        f_stored = sem("f_stored")

        with nc.Block() as block:
            @block.sync
            def _(sp):
                sp.dma_start(f_dram, out[:, :, :]).then_inc(f_stored, 16)
                sp.dma_start(select[:, :], io["select"][:, :]).then_inc(landed, 16)
                sp.dma_start(raw_mask[:, :], io["strict"][:, :]).then_inc(landed, 16)

                def pair(p):
                    for c in range(4):
                        n = 4 * p + (n0 + 4 + c)
                        sp.wait_ge(K.w_lo, n + 1)
                        K.load_weight(sp, n + 2, c % 2)

                for c in range(4):
                    sp.wait_ge(K.w_lo, n0 + c + 1)
                    K.load_weight(sp, n0 + c + 2, c % 2)
                with sp.Fori(0, PAIRS - 1) as p:
                    pair(p)

            @block.tensor
            def _(pe):
                def units(p, a, b):
                    for u in range(a, b):
                        c, half, k = u // (2 * KT), (u // KT) % 2, u % KT
                        if half == 0 and k == 0:
                            pe.wait_ge(K.w_lo, 4 * p + (n0 + c + 1))
                        if k == 0:
                            pe.wait_ge(evac, 8 * p + (2 * c + half + 1))
                        if isinstance(p, int) and p == 0 and u < KT:
                            pe.wait_ge(x_lo, k + 1)
                        last = K.products(pe, D[:, half * H:half * H + H], c % 2, k, k, xhi, xlo, half,
                                          k == 0, k == KT - 1)
                        if k == KT - 1:
                            last.then_inc(dn, 1)

                def turn_v(p, g):
                    if g == 0:
                        pe.wait_ge(evac, 8 * p + (2 * TV + 4))
                        pe.wait_ge(k_done, 2 * p + 2)
                    else:
                        pe.wait_ge(v_copy, 2 * p + 1)
                    for c in range(4):
                        col = (4 * g + c) * P
                        last = pe.transpose(pV[:, c * P:c * P + P], vT[:, col:col + P], K.ident[:, :])
                    last.then_inc(v_turn, 1)

                def head_sums(p, which):
                    pe.wait_ge(squared, 2 * p + (which + 1))
                    if which == 1:
                        pe.wait_ge(v_copy, 2 * p + 2)
                    elif not (isinstance(p, int) and p == 0):
                        pe.wait_ge(rooted, 2 * p)
                    for c in range(NC):
                        last = pe.matmul(pV[:, 2 * c:2 * c + 2], square[:, c * P:c * P + P], select[:, :],
                                         start=True, stop=True)
                    last.then_inc(summed, 1)

                def turn_k(p, g):
                    if g == 0:
                        pe.wait_ge(rooted, 2 * p + 1)
                    else:
                        pe.wait_ge(kn_done, 2 * p + 1)
                    for c in range(4):
                        col = (4 * g + c) * P
                        last = pe.transpose(pV[:, c * P:c * P + P], kRaw[:, col:col + P], K.ident[:, :])
                    last.then_inc(k_turn, 1)

                def back_k(p, g):
                    pe.wait_ge(kn_done, 2 * p + 2)
                    if g == 1:
                        pe.wait_ge(k_done, 2 * p + 1)
                    for c in range(4):
                        col = (4 * g + c) * P
                        last = pe.transpose(pV[:, c * P:c * P + P], kN[:, col:col + P], K.ident[:, :])
                    last.then_inc(k_back, 1)

                def score(p, q, r):
                    h, i = ROWS[r]
                    rows_h = slice(HD * h, HD * h + HD)
                    if r == 0:
                        pe.wait_ge(evac, 8 * p + 10)
                        pe.wait_ge(k_done, 2 * p + 2)
                    pe.wait_ge(sig, 16 * p + (r + 1))
                    for c0 in range(0, (i + 1) * P, H):
                        c1 = min(c0 + H, (i + 1) * P)
                        pe.matmul(scores[:, c0:c1], qT[rows_h, q, i * P:i * P + P],
                                  kT[rows_h, q, c0:c1], start=True, stop=c1 <= i * P)
                    pe.matmul(scores[:, i * P:i * P + P], identr[:, :], maskr[:, :],
                              start=False, stop=True).then_inc(qk, 1)

                def turn_weights(p, r):
                    h, i = ROWS[r]
                    pe.wait_ge(ex, 16 * p + (r + 3))
                    for g in range(T_GROUPS[r]):
                        n = T_BEFORE[r] + g
                        pe.wait_ge(tcopy, T_PAIR * p + (n + 1))
                        for b in range(4 * g, min(4 * g + 4, i + 1)):
                            last = pe.transpose(turned[n % 2][:, (b % 4) * P:(b % 4) * P + P],
                                                rows[:, r % 2, b * P:b * P + P], K.ident[:, :])
                        last.then_inc(turn, 1)

                def values(p, q, r):
                    h, i = ROWS[r]
                    if r == 0:
                        pe.wait_ge(v_copy, 2 * p + 2)
                    pe.wait_ge(tcopy, T_PAIR * p + (T_BEFORE[r + 1] + 2))
                    pe.wait_ge(yn, 16 * p + (r + 1))
                    for b in range(i + 1):
                        last = pe.matmul(pO[:, 0:HD], wT[:, r % 2, b * P:b * P + P],
                                         vN[:, q, b * P + HD * h:b * P + HD * h + HD],
                                         start=b == 0, stop=b == i)
                    last.then_inc(pv, 1)

                def turn_y(p, g):
                    if g == 0:
                        pe.wait_ge(yn, 16 * p + 17)
                    pe.wait_ge(tcopy, T_PAIR * p + (T_PAIR + 2))
                    for c in range(4):
                        last = pe.transpose(turned[g][:, c * P:c * P + P], yN[:, 4 * g + c, :], K.ident[:, :])
                    last.then_inc(y_turn, 1)

                def aux(p, slot):
                    for step, when in AUX_SLOT.items():
                        if when == slot and step in AUX:
                            AUX[step](p)

                AUX = dict(k_sum=lambda p: head_sums(p, 0), q_sum=lambda p: head_sums(p, 1),
                           k_turn0=lambda p: turn_k(p, 0), k_turn1=lambda p: turn_k(p, 1),
                           k_back0=lambda p: back_k(p, 0), k_back1=lambda p: back_k(p, 1),
                           v_turn0=lambda p: turn_v(p, 0), v_turn1=lambda p: turn_v(p, 1))

                def pair(p, q, more):
                    u = 0
                    for slot in range(19):
                        if slot < 16:
                            score(p, q, slot)
                        if more:
                            units(p + 1, u, u + UNITS[slot])
                            u += UNITS[slot]
                        if 1 <= slot <= 16:
                            if slot == 1:
                                pe.wait_ge(y_out, 2 * p + 2)
                            turn_weights(p, slot - 1)
                        if 2 <= slot <= 17:
                            values(p, q, slot - 2)
                        if more:
                            aux(p + 1, slot)
                    for g in range(2):
                        turn_y(p, g)

                pe.sem_inc(pv, 2)
                pe.sem_inc(turn, 4)
                pe.wait_ge(masks, 2)
                K.norm_sums(pe, pV, sums_done)
                units(0, 0, KT)
                K.norm_spread(pe, scores, diag_done, spread_done)
                units(0, KT, 4 * 2 * KT)
                for slot in range(19):
                    aux(0, slot)
                with pe.Fori(0, 3) as i:
                    for q in range(2):
                        pair(2 * i + q, q, True)
                pair(6, 0, True)
                pair(7, 1, False)

            @block.scalar
            def _(act):
                def split(p, c):
                    if not (isinstance(p, int) and p == 0 and c < 2):
                        act.wait_ge(dn, 8 * p + (2 * c - 2))
                    act.wait_ge(w_gain, 4 * p + (c + 1))
                    K.split_hi(act, 2 * p + (n0 // 2 + c // 2), c % 2)

                def copy_v(p, q, g):
                    act.wait_ge(v_turn, 2 * p + (g + 1))
                    if not (isinstance(p, int) and p == 0):
                        act.wait_ge(pv, 16 * p - 14)
                    act.activation(vN[:, q, g * H:g * H + H], pV[:, :], ACT.Copy).then_inc(v_copy, 1)

                def square_of(p, q, which):
                    act.wait_ge(evac, 8 * p + (2 * (TQ if which else TK) + 4))
                    if which:
                        act.wait_ge(k_back, 2 * p + 2)
                    elif not (isinstance(p, int) and p == 0):
                        act.wait_ge(summed, 2 * p)
                    act.activation(square, qT[:, q, :] if which else kRaw, ACT.Square).then_inc(squared, 1)

                def root_of(p, which):
                    act.wait_ge(summed, 2 * p + (which + 1))
                    act.activation((q_root if which else k_root)[:, :], pV[:, 0:16], ACT.Sqrt, scale=1.0 / HD,
                                   bias=K.eps[:, 0:1]).then_inc(rooted, 1)

                def store_k(p, q, g):
                    act.wait_ge(k_back, 2 * p + (g + 1))
                    act.activation(kT[:, q, g * H:g * H + H], pV[:, :], ACT.Copy,
                                   scale=gains[:, 0:1]).then_inc(k_done, 1)

                def aux(p, q, slot):
                    for step, when in AUX_SLOT.items():
                        if when == slot and step in AUX:
                            AUX[step](p, q)

                AUX = dict(k_square=lambda p, q: square_of(p, q, 0), q_square=lambda p, q: square_of(p, q, 1),
                           k_sum=lambda p, q: root_of(p, 0), q_sum=lambda p, q: root_of(p, 1),
                           k_back0=lambda p, q: store_k(p, q, 0), k_back1=lambda p, q: store_k(p, q, 1),
                           v_turn0=lambda p, q: copy_v(p, q, 0), v_turn1=lambda p, q: copy_v(p, q, 1))

                def gate(p, q):
                    act.wait_ge(evac, 8 * p + 10)
                    act.activation(gT[:, q, :], gT[:, q, :], ACT.Silu).then_inc(silu, 1)

                def weights(p, q, r):
                    h, i = ROWS[r]
                    n = (i + 1) * P
                    act.wait_ge(qk, 16 * p + (r + 1))
                    if r == 0:
                        act.wait_ge(q_ready, p + 1)
                    act.wait_ge(ex, 16 * p + (r + 1))
                    act.wait_ge(turn, T_PAIR * p + (T_BEFORE[r - 1] + 4 if r >= 1 else 2))
                    col = 2 * i + h
                    act.activation(keep[:, r % 2, S - n:S], scores[:, 0:n], ACT.Sigmoid,
                                   scale=q_neg[:, q, col:col + 1])
                    act.activation(rows[:, r % 2, 0:n], scores[:, 0:n], ACT.Sigmoid,
                                   scale=q_pos[:, q, col:col + 1]).then_inc(sig, 1)

                def copy_weights(p, r):
                    h, i = ROWS[r]
                    act.wait_ge(pv, 16 * p + (r + 1))
                    for g in range(T_GROUPS[r]):
                        n = T_BEFORE[r] + g
                        act.wait_ge(turn, T_PAIR * p + (n + 5))
                        cols = (min(4 * g + 4, i + 1) - 4 * g) * P
                        act.activation(wT[:, r % 2, g * H:g * H + cols], turned[n % 2][:, 0:cols],
                                       ACT.Copy).then_inc(tcopy, 1)

                def pair(p, q, more, more2):
                    for slot in range(19):
                        if slot < 16:
                            weights(p, q, slot)
                        if 1 <= slot <= 16:
                            copy_weights(p, slot - 1)
                        if more:
                            if slot == 0:
                                split(p + 1, 1)
                            if slot == half_done_slot(0, 1) + 1:
                                split(p + 1, 2)
                            if slot == half_done_slot(1, 1) + 1:
                                split(p + 1, 3)
                            aux(p + 1, 1 - q, slot)
                        if more2 and slot == half_done_slot(2, 1) + 1:
                            split(p + 2, 0)
                    if more:
                        gate(p + 1, 1 - q)

                act.sem_inc(tcopy, 2)
                act.sem_inc(sig, 1)
                act.wait_ge(masks, 4)
                split(0, 0)
                for k in range(KT):
                    K.tile_hi(act, xhi, out, k, None, x_hi)
                    if k == 3:
                        K.norm_root(act, pV, DM, sums_done, root_done)
                for c in range(1, 4):
                    split(0, c)
                split(1, 0)
                for slot in range(19):
                    aux(0, 0, slot)
                gate(0, 0)
                with act.Fori(0, 3) as i:
                    for q in range(2):
                        pair(2 * i + q, q, True, True)
                pair(6, 0, True, False)
                pair(7, 1, False, False)

            @block.vector
            def _(dve):
                def split(p, c):
                    K.split_lo(dve, 2 * p + (n0 // 2 + c // 2), c % 2)

                def scale(p, q, c, half):
                    cols = slice(half * H, half * H + H)
                    dve.wait_ge(dn, 8 * p + (2 * c + half + 1))
                    if c == TV and not (isinstance(p, int) and p == 0):
                        dve.wait_ge(v_turn, 2 * p)
                    dst = {TV: vT[:, cols], TQ: qT[:, q, cols], TK: kRaw[:, cols], TG: gT[:, q, cols]}[c]
                    dve.tensor_tensor(dst, D[:, cols], K.R[:, cols], ALU.mult).then_inc(evac, 1)

                def products(p, r):
                    h, i = ROWS[r]
                    n = (i + 1) * P
                    dve.wait_ge(sig, 16 * p + (r + 2))
                    k = keep[:, r % 2, S - n:S][:, ::-1]
                    dve.tensor_tensor_scan(k, k, k, 1.0, ALU.mult, ALU.bypass).then_inc(scan, 1)

                def store_y(p, r):
                    h, i = ROWS[r]
                    dve.wait_ge(pv, 16 * p + (r + 3))
                    if r == 0:
                        dve.wait_ge(y_turn, 2 * p + 1)
                    dve.tensor_copy(yN[:, i, HD * h:HD * h + HD], pO[:, 0:HD]).then_inc(yn, 1)

                def inverse_k(p):
                    dve.wait_ge(rooted, 2 * p + 1)
                    dve.reciprocal(k_inv[:, :], k_root[:, :]).then_inc(recip, 1)
                    dve.wait_ge(recip, 2 * p + 1)

                def norm_k(p, g):
                    dve.wait_ge(k_turn, 2 * p + (g + 1))
                    r = k_inv[:, 8 * g:8 * g + 8].unsqueeze(2).to_broadcast([P, 8, HD])
                    dve.tensor_tensor(kN[:, g * H:g * H + H].rearrange("p (a d) -> p a d", d=HD),
                                      pV[:, :].rearrange("p (a d) -> p a d", d=HD), r, ALU.mult).then_inc(kn_done, 1)

                def inverse_q(p, q):
                    dve.wait_ge(rooted, 2 * p + 2)
                    dve.reciprocal(q_inv[:, :], q_root[:, :]).then_inc(recip, 1)
                    dve.wait_ge(recip, 2 * p + 2)
                    dve.tensor_scalar(q_pos[:, q, :], q_inv[:, :], HD ** -0.5, None, ALU.mult)
                    dve.tensor_scalar(q_neg[:, q, :], q_inv[:, :], -HD ** -0.5, None, ALU.mult).then_inc(q_ready, 1)

                def aux(p, q, slot):
                    if slot == AUX_SLOT["k_sum"]:
                        inverse_k(p)
                    for g in range(2):
                        if slot == AUX_SLOT[f"k_turn{g}"]:
                            norm_k(p, g)
                    if slot == AUX_SLOT["q_sum"]:
                        inverse_q(p, q)

                def output(p, q, g):
                    cols = slice(g * H, g * H + H)
                    dve.wait_ge(y_turn, 2 * p + (g + 2))
                    dve.wait_ge(silu, p + 1)
                    dve.tensor_tensor(out[:, p, cols], turned[g][:, :], gT[:, q, cols], ALU.mult).then_inc(y_out, 1)

                def pair(p, q, more, more2):
                    for slot in range(19):
                        if slot < 16:
                            products(p, slot)
                        if more:
                            for c in range(4):
                                for half in range(2):
                                    if half_done_slot(c, half) + 1 == slot:
                                        scale(p + 1, 1 - q, c, half)
                            if slot == 0:
                                split(p + 1, 1)
                            if slot == half_done_slot(0, 1) + 1:
                                split(p + 1, 2)
                            if slot == half_done_slot(1, 1) + 1:
                                split(p + 1, 3)
                        if more2 and slot == half_done_slot(2, 1) + 1:
                            split(p + 2, 0)
                        if 2 <= slot <= 17:
                            store_y(p, slot - 2)
                        if more:
                            aux(p + 1, 1 - q, slot)
                    if more:
                        scale(p + 1, 1 - q, 3, 1)
                    for g in range(2):
                        output(p, q, g)

                dve.sem_inc(evac, 2)
                dve.wait_ge(landed, 32)
                dve.tensor_copy(identr[:, :], K.ident[:, :]).then_inc(masks, 1)
                dve.tensor_copy(maskr[:, :], raw_mask[:, :]).then_inc(masks, 1)
                dve.memset(keep[:, :, S:S + 1], 1.0).then_inc(masks, 1)
                dve.tensor_tensor(gains[:, :], K.gain("q_g", 0), K.gain("k_g", 0), ALU.mult).then_inc(masks, 1)
                dve.sem_inc(yn, 1)
                dve.sem_inc(y_out, 2)
                dve.sem_inc(y_turn, 1)
                split(0, 0)
                for k in range(KT):
                    K.tile_lo(dve, xlo, xhi, out, k, None, x_hi, x_lo)
                    if k == 3:
                        K.norm_recip(dve, root_done, rtok_done)
                        K.norm_diag(dve, diag_done)
                split(0, 1)
                K.norm_copy(dve, scores, spread_done, r_done)
                dve.wait_ge(f_stored, 16)
                for c in range(4):
                    for half in range(2):
                        scale(0, 0, c, half)
                    if c < 2:
                        split(0, c + 2)
                    if c == 2:
                        split(1, 0)
                for slot in range(19):
                    aux(0, 0, slot)
                with dve.Fori(0, 3) as i:
                    for q in range(2):
                        pair(2 * i + q, q, True, True)
                pair(6, 0, True, False)
                pair(7, 1, False, False)

            @block.gpsimd
            def _(pool):
                def gain(p, c):
                    n = (p + (n0 // 4)) * 2 + c // 2
                    pool.wait_ge(K.w_land[c % 2], 16 * n + 16)
                    g = K.vec[:, VEC["kv_norm"]:VEC["kv_norm"] + KT] if c in (TK, TV) else \
                        K.vec[:, VEC["s_norm"]:VEC["s_norm"] + KT]
                    tile = K.wraw[:, c % 2, :, :]
                    pool.tensor_tensor(tile, tile, g.unsqueeze(2).to_broadcast([P, KT, P]), ALU.mult).then_inc(w_gain, 1)

                def weigh(p, r):
                    h, i = ROWS[r]
                    n = (i + 1) * P
                    pool.wait_ge(scan, 16 * p + (r + 1))
                    pool.tensor_tensor(rows[:, r % 2, 0:n], rows[:, r % 2, 0:n],
                                       keep[:, r % 2, S - n + 1:S + 1], ALU.mult).then_inc(ex, 1)

                def pair(p, more, more2):
                    for slot in range(16):
                        weigh(p, slot)
                        if more and slot == 0:
                            gain(p + 1, 1)
                        if more and slot == half_done_slot(0, 1) + 1:
                            gain(p + 1, 2)
                        if more and slot == half_done_slot(1, 1) + 1:
                            gain(p + 1, 3)
                    if more2:
                        gain(p + 2, 0)

                pool.sem_inc(ex, 2)
                pool.wait_ge(masks, 4)
                for c in range(4):
                    gain(0, c)
                gain(1, 0)
                with pool.Fori(0, 6) as p:
                    pair(p, True, True)
                pair(6, True, False)
                pair(7, False, False)


def alibi_table():
    d = np.arange(P)[:, None] - np.arange(S)[None, :] + (S - P)
    count = np.zeros(d.shape)
    for window, dilation in ((128, 1), (512, 4), (2048, 16)):
        count += (d >= 0) & (d % dilation == 0) & (d <= window)
    log_count = np.where(count > 0, np.log(np.maximum(count, 1)), 0.0)
    slopes = 2.0 ** (-8.0 * np.arange(1, HEADS + 1) / HEADS)
    table = -slopes[:, None, None] * d + log_count
    return np.where(count > 0, table, NEG).astype(np.float32)


def weight_tiles(w):
    k, n = w.shape
    return w.reshape(k // P, P, n // P, P).transpose(2, 1, 0, 3)


def columns(v):
    return np.reshape(v, (-1, P)).T


def stage_ple(K, layer, xhi, xlo, f_sb, unused, squared, out=None):
    nc, io, name = K.nc, K.io, f"ple{layer}"
    n0 = FIRST[name]
    KP = 2
    with ExitStack() as ctx:
        sem = K.semaphores(ctx, name + "_")
        sb = lambda n, shape, dt=F32: ctx.enter_context(nc.sbuf_tensor(f"{name}_{n}", shape, dt))
        D = ctx.enter_context(nc.psum_tensor(name + "_D", [P, 2, S], F32))
        pP = ctx.enter_context(nc.psum_tensor(name + "_pP", [P, 2, S], F32))
        p_raw, p_hi, p_lo = unused[:, 0:KP, :], sb("p_hi", [P, KP, S], F32R), sb("p_lo", [P, KP, S], F32R)
        w_raw = unused[:, KP:2 * KP, :].rearrange("p a (b m) -> p (a b) m", m=P)
        w_raw = w_raw.rearrange("p (j k) m -> p j k m", k=KP)
        w_hi, w_lo = sb("w_hi", [P, KT, KP, P], F32R), sb("w_lo", [P, KT, KP, P], F32R)
        gate = K.sq
        squares = sb("squares", [P, 2, S]) if out is None else None
        sums, spread = pP[:, 1, :], pP[:, 1, :]
        landed, parts, p_lows = sem("landed"), sem("parts"), sem("p_lows")
        mm, pm, scaled, sig, gated, added = sem("mm"), sem("pm"), sem("scaled"), sem("sig"), sem("gated"), sem("added")
        x_hi, x_lo, sq_done, acc_done = sem("x_hi"), sem("x_lo"), sem("sq"), sem("acc")
        sums_done, root_done, rtok_done = sem("sums"), sem("root"), sem("rtok")
        diag_done, spread_done, r_done = sem("diag"), sem("spread"), sem("r")
        new_sq, new_acc, stored, copy_go = sem("new_sq"), sem("new_acc"), sem("stored"), sem("copy_go")
        with nc.Block() as block:
            @block.sync
            def _(sp):
                sp.dma_start(p_raw[:, :, :], io["pT"][layer].rearrange("(k p) t -> p k t", p=P)).then_inc(landed, 16)
                sp.dma_start(w_raw[:, :, :, :], io["w_ple"][layer].rearrange("j p k m -> p j k m")).then_inc(landed, 16)
                K.load_ahead(sp, name, skip_last=layer == 1)

            @block.tensor
            def _(pe):
                if squared:
                    K.norm_sums(pe, sums, sums_done)
                for j in range(KT):
                    s = j % 2
                    pe.wait_ge(K.w_lo, n0 + j + 1)
                    if j >= 2:
                        pe.wait_ge(added, j + 1)
                    K.dense(pe, D[:, s, :], s, xhi, xlo, x_lo if j == 0 else None).then_inc(mm, 1)
                    if j == 0:
                        pe.wait_ge(p_lows, 2)
                    if j == 1:
                        if not squared:
                            pe.wait_ge(acc_done, KT)
                            K.norm_sums(pe, sums, sums_done)
                            K.norm_spread(pe, spread, diag_done, spread_done)
                        pe.wait_ge(r_done, 1)
                    for k in range(KP):
                        for half in range(2):
                            cols = slice(half * H, half * H + H)
                            pe.matmul(pP[:, s, cols], w_hi[:, j, k, :], p_hi[:, k, cols], start=k == 0, stop=False)
                            pe.matmul(pP[:, s, cols], w_hi[:, j, k, :], p_lo[:, k, cols], start=False, stop=False)
                            last = pe.matmul(pP[:, s, cols], w_lo[:, j, k, :], p_hi[:, k, cols],
                                             start=False, stop=k == KP - 1)
                    last.then_inc(pm, 1)
                    if j == 0 and squared:
                        K.norm_spread(pe, spread, diag_done, spread_done)

            @block.scalar
            def _(act):
                for s in range(2):
                    K.split_hi(act, n0 // 2, s)
                for k in range(KT):
                    K.tile_hi(act, xhi, f_sb, k, name, x_hi)
                if squared:
                    K.norm_root(act, sums, DM, sums_done, root_done)
                act.wait_ge(landed, 32)
                act.activation(p_hi[:, :, :], p_raw[:, :, :], ACT.Copy).then_inc(parts, 1)
                act.activation(w_hi[:, :, :, :], w_raw[:, :, :, :], ACT.Copy).then_inc(parts, 1)
                if not squared:
                    for k in range(KT):
                        K.square(act, f_sb[:, k, :], k, sq_done, acc_done)
                    K.norm_root(act, sums, DM, sums_done, root_done)

                def tiles(i, first=False, last=False):
                    for s in range(2):
                        n = 2 * i + s
                        act.wait_ge(scaled, n + 1)
                        act.activation(gate[:, s, :], gate[:, s, :], ACT.Sigmoid).then_inc(sig, 1)
                        if not last:
                            act.wait_ge(mm, n + 1)
                            K.split_hi(act, i + (n0 // 2 + 1), s)
                        if out is None:
                            K.square_tile(act, squares[:, s, :], f_sb[:, n, :], n, added, n + 3, new_acc,
                                          first).then_inc(new_sq, 1)

                tiles(0, first=True)
                with act.Fori(1, KT // 2 - 1) as i:
                    tiles(i)
                tiles(KT // 2 - 1, last=True)

            @block.gpsimd
            def _(pool):
                if out is None:
                    K.sum_tiles(pool, squares, new_sq, new_acc, copy_go)
                else:
                    tiles = out.rearrange("(k p) t -> k p t", p=P)
                    with pool.Fori(0, KT) as n:
                        pool.wait_ge(added, n + 3)
                        pool.dma_start(tiles[n, :, :], f_sb[:, n, :]).then_inc(stored, 16)
                    pool.wait_ge(stored, 16 * KT)

            @block.vector
            def _(dve):
                for s in range(2):
                    K.split_lo(dve, n0 // 2, s)
                for k in range(KT):
                    K.tile_lo(dve, xlo, xhi, f_sb, k, name, x_hi, x_lo)
                dve.wait_ge(parts, 2)
                dve.tensor_tensor(p_lo[:, :, :], p_raw[:, :, :], p_hi[:, :, :].bitcast(F32), ALU.subtract).then_inc(p_lows, 1)
                dve.tensor_tensor(w_lo[:, :, :, :], w_raw[:, :, :, :], w_hi[:, :, :, :].bitcast(F32),
                                  ALU.subtract).then_inc(p_lows, 1)
                if not squared:
                    K.sum_squares(dve, KT, sq_done, acc_done)
                K.norm_recip(dve, root_done, rtok_done)
                K.norm_diag(dve, diag_done)
                K.norm_copy(dve, spread, spread_done, r_done)
                dve.sem_inc(added, 2)

                def tiles(i, last=False):
                    for s in range(2):
                        n = 2 * i + s
                        dve.wait_ge(mm, n + 1)
                        dve.wait_ge(added, n + 1)
                        dve.tensor_tensor(gate[:, s, :], D[:, s, :], K.R[:, :], ALU.mult).then_inc(scaled, 1)
                        if not last:
                            K.split_lo(dve, i + (n0 // 2 + 1), s)
                        dve.wait_ge(pm, n + 1)
                        dve.wait_ge(sig, n + 1)
                        dve.tensor_tensor(gate[:, s, :], pP[:, s, :], gate[:, s, :], ALU.mult).then_inc(gated, 1)
                        dve.wait_ge(gated, n + 1)
                        dve.tensor_tensor(f_sb[:, n, :], f_sb[:, n, :], gate[:, s, :], ALU.add).then_inc(added, 1)

                with dve.Fori(0, KT // 2 - 1) as i:
                    tiles(i)
                tiles(KT // 2 - 1, last=True)


def bass_program(nc, io, out):
    with ExitStack() as ctx:
        K = Kernel(nc, ctx, io)

        def tensors(stack, *names, dt=F32):
            return [stack.enter_context(nc.sbuf_tensor(n, [P, KT, S], dt)) for n in names]

        branch_a = nc.dram_tensor("branch_a", (KT, P, S), F32, kind="Internal").ap()
        y_dram = nc.dram_tensor("y_b", (KT, P, S), F32, kind="Internal").ap()
        f_dram = nc.dram_tensor("f_copy", (P, KT, S), F32, kind="Internal").ap()
        acum_dram = nc.dram_tensor("acum_rows", (SH, S), F32, kind="Internal").ap()
        x_dram = io["xT"].rearrange("(k p) t -> p k t", p=P)

        with ExitStack() as b1:
            with ExitStack() as shared:
                stack = shared.enter_context(nc.sbuf_tensor("stack", [P, 2, 4, S], F32R))
            f_sb, = tensors(b1, "f1")
            with ExitStack() as b2:
                xhi, xlo = tensors(b2, "x1hi", "x1lo", dt=F32R)
                vN = f_sb
                with ExitStack() as b3:
                    x_sb, = tensors(b3, "x_sb")
                    stage_v(K, x_sb, xhi, xlo, vN)
                with ExitStack() as b3:
                    yhi, ylo = tensors(b3, "ya_hi", "ya_lo", dt=F32R)
                    stage_ug(K, xhi, xlo, vN, yhi, ylo)
                    stage_pa(K, xhi, xlo, yhi, ylo, branch_a)
                y = f_sb
                stage_attention(K, xhi, xlo, stack, y_dram)
                with ExitStack() as b3:
                    yhi, ylo = tensors(b3, "yb_hi", "yb_lo", dt=F32R)
                    stage_pb(K, xhi, xlo, y_dram, y, yhi, ylo, branch_a, y)
                with ExitStack() as b3:
                    heads = [b3.enter_context(nc.sbuf_tensor("heads_" + n, [P, NC * SH], F32))
                             for n in ("dt", "dte", "acum", "e_acum", "e_end")]
                    with ExitStack() as b4:
                        merged = f_sb
                        x1, = tensors(b4, "x1")
                        stage_residual(K, "out", merged, xhi, xlo, x1, x_dram)
                        stage_dt(K, x1, f_sb, xhi, xlo, *heads, acum_dram)
                    stage_ssm(K, xhi, xlo, f_sb, *heads, acum_dram)
                with nc.sbuf_tensor("ple_in", [P, 4, S], F32) as unused:
                    stage_ple(K, 0, xhi, xlo, f_sb, unused, squared=False)
                stage_stick(K, xhi, xlo, f_sb, f_dram)
                with ExitStack() as b3:
                    h, = tensors(b3, "h")
                    stage_residual(K, "sout", f_sb, xhi, xlo, h, f_dram)
                    stage_ple(K, 1, xhi, xlo, h, f_sb, squared=True, out=out)


def kernel(**inputs):
    import concourse.bacc as bacc
    from concourse.bass_utils import run_bass_kernel_spmd

    a = {k: np.asarray(v) for k, v in inputs.items()}
    def merge(*xs):
        return np.stack(xs, 1).reshape(-1, P, KT, P)

    u, v, gate, q, k, val, b_gate, g_a, g_b = weight_tiles(a["w_in"][0]).reshape(9, 8, P, KT, P)
    weights = [v, merge(u, gate), merge(g_a, weight_tiles(a["w_proj_a"][0])), merge(val, q, k, b_gate),
               merge(g_b, weight_tiles(a["w_proj_b"][0])), weight_tiles(a["w_out"][0])]
    m_in = a["m_in_2"][0]
    channels, state = GROUPS * GC, GROUPS * P
    z, xs, b, c = (weight_tiles(m_in[:, i:j]) for i, j in (
        (0, channels), (channels, 2 * channels), (2 * channels, 2 * channels + state),
        (2 * channels + state, 2 * channels + 2 * state)))
    for g in range(GROUPS):
        of = slice(GT * g, GT * g + GT)
        m_out = weight_tiles(a["m_out_2"][0][GC * g:GC * g + GC]).reshape(4, 2, P, GT, P)
        weights += [b[g:g + 1], c[g:g + 1], xs[of], z[of], m_out.transpose(0, 2, 1, 3, 4).reshape(4, P, KT, P)]
    k2, v2 = weight_tiles(a["w_kv_2"]).reshape(2, 8, P, KT, P)
    q2, gate2 = weight_tiles(a["s_in_2"][0]).reshape(2, 8, P, KT, P)
    weights += [weight_tiles(a["ple_gate_2"][0]), merge(k2, v2, q2, gate2), weight_tiles(a["s_out_2"][0]),
                weight_tiles(a["ple_gate_2"][1])]

    w_dt = np.zeros((DM, P), np.float32)
    w_dt[:, :SH] = m_in[:, -SH:]
    vec = np.zeros((P, N_VEC), np.float32)

    def put(name, v):
        vec[:, VEC[name]:VEC[name] + VEC_WIDTH[name]] = columns(v)

    put("g_norm", a["g_norm"][0])
    put("g_v", a["g_v"][0])
    put("g_final", a["g_final"])
    put("m_norm", a["m_norm_2"][0])
    vec[:, VEC["conv_w"]:VEC["conv_w"] + 96] = a["m_conv_w_2"][0].reshape(TAPS, 24, P).transpose(2, 1, 0).reshape(P, 96)
    put("conv_b", a["m_conv_b_2"][0])
    put("d_skip", np.repeat(a["m_D_2"][0], SD))
    put("y_norm", a["m_ynorm_2"][0])
    put("kv_norm", a["kv_norm_2"])
    put("s_norm", a["s_norm_2"][0])
    put("ple0", a["ple_norm_2"][0])
    put("ple1", a["ple_norm_2"][1])
    put("q_g", np.tile(a["q_norm_2"][0], 2))
    put("k_g", np.tile(a["k_norm_2"], 2))
    arrays = {
        "w": np.concatenate(weights), "vec": vec, "xT": np.ascontiguousarray(a["x"][0].T),
        "ones": np.ones((P, P), np.float32), "ident": np.eye(P, dtype=np.float32),
        "causal": np.triu(np.ones((P, P), np.float32)),
        "strict": np.where(np.tril(np.ones((P, P)), -1) > 0, 0.0, NEG).astype(np.float32),
        "select": np.repeat(np.eye(2, dtype=np.float32), HD, axis=0),
        "w_sT": np.ascontiguousarray(a["w_s"][0].transpose(0, 2, 1)), "b_s": a["b_s"][0],
        "alibi": alibi_table(),
        "w_dt": np.ascontiguousarray(weight_tiles(w_dt)[0]),
        "dt_head": np.stack([a["m_dt_bias_2"][0], a["m_A_log_2"][0]]),
        "pT": np.ascontiguousarray(a["p_2"][:, 0].transpose(0, 2, 1)),
        "w_ple": np.stack([weight_tiles(a["ple_proj_2"][i]) for i in range(2)]),
    }
    nc = bacc.Bacc("TRN2", target_bir_lowering=False, num_devices=1)
    io = {n: nc.dram_tensor(n + "_dram", v.shape, mybir.dt.from_np(v.dtype), kind="ExternalInput").ap()
          for n, v in arrays.items()}
    out = nc.dram_tensor("out_dram", (DM, S), F32, kind="ExternalOutput").ap()
    bass_program(nc, io, out)
    r = run_bass_kernel_spmd(nc, [{n + "_dram": v for n, v in arrays.items()}], core_ids=[0])
    return np.ascontiguousarray(r.results[0]["out_dram"].T)[None]
```

```python
from contextlib import ExitStack

import numpy as np
import concourse.bass as bass
from concourse import mybir

F32 = mybir.dt.float32
F32R = mybir.dt.float32r
ALU = mybir.AluOpType
ACT = mybir.ActivationFunctionType

P = 128
S = 1024
DM = 1024
KT = DM // P
NC = S // P
H = 512
EPS = 1e-6
HEADS = 16
HD = 64
PAIRS = HEADS // 2
NEG = -1e30
GROUPS = 4
GT = 4

N_V, N_UG, N_PA, N_ATT, N_PB, N_OUT = 8, 16, 16, 32, 16, 8
GROUP_TILES = 2 + 4 + 4 + 4
N_SSM, N_PLE, N_STICK, N_SOUT = GROUPS * GROUP_TILES, 8, 32, 8
STAGES = dict(v=N_V, ug=N_UG, pa=N_PA, att=N_ATT, pb=N_PB, out=N_OUT, ssm=N_SSM, ple0=N_PLE,
              stick=N_STICK, sout=N_SOUT, ple1=N_PLE)
FIRST, N_TILES = {}, 0
for _name, _n in STAGES.items():
    FIRST[_name] = N_TILES
    N_TILES += _n

VEC_WIDTH = dict(g_norm=8, g_v=8, g_final=8, m_norm=8, conv_w=96, conv_b=24, d_skip=16, y_norm=16,
                 kv_norm=8, s_norm=8, ple0=8, ple1=8, q_g=1, k_g=1)
VEC, N_VEC = {}, 0
for _name, _n in VEC_WIDTH.items():
    VEC[_name] = N_VEC
    N_VEC += _n


def halves(ap):
    return [ap[:, 0:H], ap[:, H:S]]


class Kernel:

    def __init__(self, nc, ctx, io):
        self.nc, self.io = nc, io
        self.taken = []

        def sb(name, shape, dt=F32):
            return ctx.enter_context(nc.sbuf_tensor(name, shape, dt))

        self.ones = sb("ones", [P, P])
        self.ident = sb("ident", [P, P])
        self.vec = sb("vec", [P, N_VEC])
        self.eps = sb("eps", [P, 1])
        self.root = sb("root", [P, NC])
        self.rtok = sb("rtok", [P, NC])
        self.R = sb("R", [P, S])
        self.acc = sb("acc", [P, S])
        self.sq = sb("sq", [P, 2, S])
        self.wraw = sb("wraw", [P, 2, 8, P])
        self.whi = sb("whi", [P, 2, 8, P], F32R)
        self.wlo = sb("wlo", [P, 2, 8, P], F32R)
        self.w_land = [ctx.enter_context(nc.semaphore(f"w_land{s}")) for s in range(2)]
        self.w_hi = ctx.enter_context(nc.semaphore("w_hi"))
        self.w_lo = ctx.enter_context(nc.semaphore("w_lo"))

    def semaphores(self, prefix):

        def sem(name):
            self.taken.append(self.nc.alloc_semaphore(prefix + name))
            return self.taken[-1]

        return sem

    def clear_semaphores(self):
        self.nc.clear_and_free_semaphores(self.taken)
        self.nc.all_engine_barrier()
        self.taken = []

    def gain(self, name, k):
        return self.vec[:, VEC[name] + k:VEC[name] + k + 1]

    def load_weight(self, sp, n, s):
        sp.dma_start(self.wraw[:, s, :, :], self.io["w"][n, :, :, :]).then_inc(self.w_land[s], 16)

    def load_ahead(self, sp, stage, skip_last=False):
        n0, count = FIRST[stage], STAGES[stage]
        pairs = count // 2 - (1 if skip_last else 0)
        with sp.Fori(0, pairs) as i:
            for s in range(2):
                sp.wait_ge(self.w_lo, 2 * i + (n0 + s + 1))
                self.load_weight(sp, 2 * i + (n0 + s + 2), s)

    def split_hi(self, act, lap, s):
        act.wait_ge(self.w_land[s], 16 * lap + 16)
        act.activation(self.whi[:, s, :, :], self.wraw[:, s, :, :], ACT.Copy).then_inc(self.w_hi, 1)

    def split_lo(self, dve, lap, s):
        dve.wait_ge(self.w_hi, 2 * lap + (s + 1))
        dve.tensor_tensor(self.wlo[:, s, :, :], self.wraw[:, s, :, :],
                          self.whi[:, s, :, :].bitcast(F32), ALU.subtract).then_inc(self.w_lo, 1)

    def products(self, pe, out, s, w0, k, xhi, xlo, half, start, stop):
        cols = slice(half * H, half * H + H)
        pe.matmul(out, self.whi[:, s, w0, :], xhi[:, k, cols], start=start, stop=False)
        pe.matmul(out, self.whi[:, s, w0, :], xlo[:, k, cols], start=False, stop=False)
        return pe.matmul(out, self.wlo[:, s, w0, :], xhi[:, k, cols], start=False, stop=stop)

    def dense(self, pe, out, s, xhi, xlo, x_ready=None):
        for k in range(KT):
            if x_ready is not None:
                pe.wait_ge(x_ready, k + 1)
            for half in range(2):
                last = self.products(pe, out[:, half * H:half * H + H], s, k, k, xhi, xlo, half,
                                     k == 0, k == KT - 1)
        return last

    def tile_hi(self, act, xhi, src, k, gain, done):
        if gain is None:
            act.activation(xhi[:, k, :], src[:, k, :], ACT.Copy).then_inc(done, 1)
        else:
            act.activation(xhi[:, k, :], src[:, k, :], ACT.Copy, scale=self.gain(gain, k)).then_inc(done, 1)

    def tile_lo(self, dve, xlo, xhi, src, k, gain, hi_done, done):
        dve.wait_ge(hi_done, k + 1)
        high = xhi[:, k, :].bitcast(F32)
        if gain is None:
            dve.tensor_tensor(xlo[:, k, :], src[:, k, :], high, ALU.subtract).then_inc(done, 1)
        else:
            dve.scalar_tensor_tensor(xlo[:, k, :], src[:, k, :], self.gain(gain, k), high,
                                     ALU.mult, ALU.subtract).then_inc(done, 1)

    def square(self, act, src, k, sq_done, acc_done):
        if k >= 2:
            act.wait_ge(acc_done, k - 1)
        act.activation(self.sq[:, k % 2, :], src, ACT.Square).then_inc(sq_done, 1)

    def sum_squares(self, pool, tiles, sq_done, acc_done):
        for k in range(1, tiles):
            pool.wait_ge(sq_done, k + 1)
            if k == 1:
                pool.tensor_tensor(self.acc[:, :], self.sq[:, 0, :], self.sq[:, 1, :], ALU.add).then_inc(acc_done, 2)
            else:
                pool.wait_ge(acc_done, k)
                pool.tensor_tensor(self.acc[:, :], self.acc[:, :], self.sq[:, k % 2, :],
                                   ALU.add).then_inc(acc_done, 1)

    def square_tile(self, act, dst, src, n, added, count, acc_done, first):
        act.wait_ge(added, count)
        if not first:
            act.wait_ge(acc_done, n - 1)
        return act.activation(dst, src, ACT.Square)

    def sum_tiles(self, pool, sq, sq_done, acc_done):
        pool.wait_ge(sq_done, 2)
        pool.tensor_tensor(self.acc[:, :], sq[:, 0, :], sq[:, 1, :], ALU.add).then_inc(acc_done, 2)
        with pool.Fori(1, KT // 2) as i:
            for s in range(2):
                pool.wait_ge(sq_done, 2 * i + s + 1)
                pool.wait_ge(acc_done, 2 * i + s)
                pool.tensor_tensor(self.acc[:, :], self.acc[:, :], sq[:, s, :], ALU.add).then_inc(acc_done, 1)

    def norm_sums(self, pe, sums, sums_done):
        for c in range(NC):
            last = pe.matmul(sums[:, c:c + 1], self.acc[:, c * P:c * P + P], self.ones[:, 0:1],
                             start=True, stop=True)
        last.then_inc(sums_done, 1)

    def norm_root(self, act, sums, features, sums_done, root_done):
        act.wait_ge(sums_done, 1)
        act.activation(self.root[:, :], sums[:, 0:NC], ACT.Sqrt, scale=1.0 / features,
                       bias=self.eps[:, 0:1]).then_inc(root_done, 1)

    def norm_recip(self, dve, root_done, rtok_done):
        dve.wait_ge(root_done, 1)
        dve.reciprocal(self.rtok[:, :], self.root[:, :]).then_inc(rtok_done, 1)
        dve.wait_ge(rtok_done, 1)

    def norm_diag(self, dve, diag_done):
        diag = self.sq[:, 0, :].rearrange("p (c t) -> p c t", c=NC)
        dve.tensor_tensor(diag, self.ident[:, :].unsqueeze(1).to_broadcast([P, NC, P]),
                          self.rtok[:, :].unsqueeze(2).to_broadcast([P, NC, P]), ALU.mult).then_inc(diag_done, 1)

    def norm_spread(self, pe, spread, diag_done, spread_done):
        pe.wait_ge(diag_done, 1)
        for half in range(2):
            last = pe.matmul(spread[:, half * H:half * H + H], self.ones[:, :],
                             self.sq[:, 0, half * H:half * H + H], start=True, stop=True)
        last.then_inc(spread_done, 1)

    def norm_copy(self, dve, spread, spread_done, r_done):
        dve.wait_ge(spread_done, 1)
        dve.tensor_copy(self.R[:, :], spread[:, :]).then_inc(r_done, 1)
        dve.wait_ge(r_done, 1)


def stage_v(K, x_sb, xhi, xlo, vN):
    nc, n0 = K.nc, FIRST["v"]
    with ExitStack() as ctx:
        sem = K.semaphores("v_")
        D = ctx.enter_context(nc.psum_tensor("v_D", [P, 2, S], F32))
        turned = ctx.enter_context(nc.psum_tensor("v_turned", [P, S], F32))
        sums = ctx.enter_context(nc.psum_tensor("v_sums", [P, H], F32))
        scaled = ctx.enter_context(nc.sbuf_tensor("v_scaled", [P, 2, S], F32))
        x_hi, x_lo, sq_done, acc_done = sem("x_hi"), sem("x_lo"), sem("sq"), sem("acc")
        sums_done, root_done, rtok_done = sem("sums"), sem("root"), sem("rtok")
        diag_done, spread_done, r_done = sem("diag"), sem("spread"), sem("r")
        mm, evac, gelu, vsq, vacc = sem("mm"), sem("evac"), sem("gelu"), sem("vsq"), sem("vacc")
        turn, stored, sums2, root2, rtok2 = sem("turn"), sem("stored"), sem("sums2"), sem("root2"), sem("rtok2")
        x_land, const_land, eps_done = [sem(f"x_land{k}") for k in range(KT)], sem("const_land"), sem("eps")
        with nc.Block() as block:
            @block.sync
            def _(sp):
                x_tiles = K.io["xT"].rearrange("(k p) t -> k p t", p=P)
                K.load_weight(sp, 0, 0)
                for name, tile in (("vec", K.vec), ("ident", K.ident), ("ones", K.ones)):
                    sp.dma_start(tile[:, :], K.io[name][:, :]).then_inc(const_land, 16)
                for k in range(KT):
                    sp.dma_start(x_sb[:, k, :], x_tiles[k]).then_inc(x_land[k], 16)
                    if k == 3:
                        K.load_weight(sp, 1, 1)
                K.load_ahead(sp, "v")

            @block.tensor
            def _(pe):
                pe.wait_ge(const_land, 48)

                def turn_tile(n, s):
                    pe.wait_ge(gelu, n + 1)
                    if not (isinstance(n, int) and n == 0):
                        pe.wait_ge(stored, n)
                    for c in range(NC):
                        last = pe.transpose(turned[:, c * P:c * P + P], scaled[:, s, c * P:c * P + P],
                                            K.ident[:, :])
                    last.then_inc(turn, 1)

                def tiles(i, first=False):
                    for s in range(2):
                        n = 2 * i + s
                        pe.wait_ge(K.w_lo, n + (n0 + 1))
                        if not first:
                            pe.wait_ge(evac, n - 1)
                        K.dense(pe, D[:, s, :], s, xhi, xlo, x_lo if first and s == 0 else None).then_inc(mm, 1)
                        if first and s == 0:
                            pe.wait_ge(acc_done, KT)
                            K.norm_sums(pe, sums, sums_done)
                        elif first:
                            K.norm_spread(pe, turned, diag_done, spread_done)
                            pe.wait_ge(spread_done, 1)
                            pe.wait_ge(r_done, 1)
                            turn_tile(0, 0)
                        else:
                            turn_tile(n - 1, 1 - s)

                tiles(0, first=True)
                with pe.Fori(1, N_V // 2) as i:
                    tiles(i)
                turn_tile(N_V - 1, 1)
                pe.wait_ge(vacc, N_V)
                K.norm_sums(pe, sums, sums2)

            @block.scalar
            def _(act):
                def tiles(i, first=False):
                    for s in range(2):
                        n = 2 * i + s
                        act.wait_ge(evac, n + 1)
                        act.activation(scaled[:, s, :], scaled[:, s, :], ACT.Gelu_apprx_tanh).then_inc(gelu, 1)
                        act.wait_ge(gelu, n + 1)
                        if not first:
                            act.wait_ge(vacc, n - 1)
                        act.activation(K.sq[:, s, :], scaled[:, s, :], ACT.Square).then_inc(vsq, 1)
                        act.wait_ge(mm, n + 1)
                        K.split_hi(act, i + (n0 // 2 + 1), s)
                        act.wait_ge(turn, n + 1)
                        act.activation(vN[:, n, :], turned[:, :], ACT.Copy).then_inc(stored, 1)

                K.split_hi(act, n0 // 2, 0)
                act.wait_ge(const_land, 48)
                for k in range(KT):
                    act.wait_ge(x_land[k], 16)
                    K.tile_hi(act, xhi, x_sb, k, "g_norm", x_hi)
                    K.square(act, x_sb[:, k, :], k, sq_done, acc_done)
                    if k == 4:
                        K.split_hi(act, n0 // 2, 1)
                act.wait_ge(eps_done, 1)
                K.norm_root(act, sums, DM, sums_done, root_done)
                act.wait_ge(spread_done, 1)
                tiles(0, first=True)
                with act.Fori(1, N_V // 2) as i:
                    tiles(i)
                K.norm_root(act, sums, DM, sums2, root2)

            @block.vector
            def _(dve):
                def tiles(i, first=False):
                    for s in range(2):
                        n = 2 * i + s
                        dve.wait_ge(mm, n + 1)
                        if not first:
                            dve.wait_ge(turn, n - 1)
                            dve.wait_ge(vsq, n - 1)
                        dve.tensor_tensor(scaled[:, s, :], D[:, s, :], K.R[:, :], ALU.mult).then_inc(evac, 1)
                        K.split_lo(dve, i + (n0 // 2 + 1), s)

                dve.memset(K.eps[:, :], EPS).then_inc(eps_done, 1)
                K.split_lo(dve, n0 // 2, 0)
                dve.wait_ge(const_land, 48)
                for k in range(KT):
                    dve.wait_ge(x_land[k], 16)
                    K.tile_lo(dve, xlo, xhi, x_sb, k, "g_norm", x_hi, x_lo)
                    if k == 4:
                        K.split_lo(dve, n0 // 2, 1)
                K.norm_recip(dve, root_done, rtok_done)
                K.norm_diag(dve, diag_done)
                K.norm_copy(dve, turned, spread_done, r_done)
                tiles(0, first=True)
                with dve.Fori(1, N_V // 2) as i:
                    tiles(i)
                K.norm_recip(dve, root2, rtok2)

            @block.gpsimd
            def _(pool):
                K.sum_squares(pool, KT, sq_done, acc_done)
                pool.wait_ge(sums_done, 1)
                pool.wait_ge(vsq, 2)
                pool.tensor_tensor(K.acc[:, :], K.sq[:, 0, :], K.sq[:, 1, :], ALU.add).then_inc(vacc, 2)
                with pool.Fori(1, N_V // 2) as i:
                    for s in range(2):
                        pool.wait_ge(vsq, 2 * i + s + 1)
                        pool.wait_ge(vacc, 2 * i + s)
                        pool.tensor_tensor(K.acc[:, :], K.acc[:, :], K.sq[:, s, :], ALU.add).then_inc(vacc, 1)


def stage_ug(K, D, xhi, xlo, vN, yhi, ylo):
    nc, io, n0 = K.nc, K.io, FIRST["ug"]
    with ExitStack() as ctx:
        sem = K.semaphores("ug_")
        mixed = ctx.enter_context(nc.psum_tensor("ug_mixed", [P, S], F32))
        vS = ctx.enter_context(nc.sbuf_tensor("ug_vS", [P, NC, P], F32))
        ws = ctx.enter_context(nc.sbuf_tensor("ug_ws", [P, P], F32))
        bs = ctx.enter_context(nc.sbuf_tensor("ug_bs", [P, P], F32))
        wm = ctx.enter_context(nc.sbuf_tensor("ug_wm", [P, P], F32))
        u, gate = K.sq[:, 0, :], K.sq[:, 1, :]
        y = K.acc[:, :]
        mm, u_scaled, g_scaled, u_gelu, g_silu = sem("mm"), sem("us"), sem("gs"), sem("gelu"), sem("silu")
        ws_land, bs_land, select_go = sem("ws_land"), sem("bs_land"), sem("select_go")
        wm_done, v_scaled, mix, biased, uy, y_done = sem("wm"), sem("vs"), sem("mix"), sem("biased"), sem("uy"), sem("y")
        y_hi, y_lo = sem("y_hi"), sem("y_lo")
        with nc.Block() as block:
            @block.sync
            def _(sp):
                K.load_ahead(sp, "ug")

            @block.gpsimd
            def _(pool):
                pool.sem_inc(wm_done, 1)
                with pool.Fori(0, KT) as g:
                    pool.wait_ge(wm_done, g + 1)
                    pool.dma_start(ws[:, :], io["w_sT"][g, :, :]).then_inc(ws_land, 16)
                    pool.wait_ge(biased, g + 1)
                    pool.dma_start(bs[:, :], io["b_s"][g, :].partition_broadcast(P)).then_inc(bs_land, 16)
                    pool.wait_ge(ws_land, 16 * g + 16)
                    pool.wait_ge(mix, g + 1)
                    pool.sem_inc(select_go, 1)
                    pool.affine_select(out=wm[:, :], in_=ws[:, :], compare_op=ALU.is_ge, fill=0.0, base=0,
                                       pattern=[[1, P]], channel_multiplier=-1).then_inc(wm_done, 1)

            @block.tensor
            def _(pe):
                pe.sem_inc(mix, 1)
                with pe.Fori(0, KT) as g:
                    pe.wait_ge(K.w_lo, 2 * g + (n0 + 1))
                    pe.wait_ge(u_scaled, g + 1)
                    K.dense(pe, D[:, 0, :], 0, xhi, xlo).then_inc(mm, 1)
                    pe.wait_ge(v_scaled, g + 1)
                    pe.wait_ge(wm_done, g + 2)
                    pe.wait_ge(uy, g + 1)
                    for c in range(NC):
                        last = pe.matmul(mixed[:, c * P:c * P + P], vS[:, c, :], wm[:, :], start=True, stop=True)
                    last.then_inc(mix, 1)
                    pe.wait_ge(K.w_lo, 2 * g + (n0 + 2))
                    pe.wait_ge(g_scaled, g + 1)
                    K.dense(pe, D[:, 1, :], 1, xhi, xlo).then_inc(mm, 1)
                pe.wait_ge(K.w_lo, n0 + N_UG + 1)
                pe.wait_ge(u_scaled, KT + 1)
                K.dense(pe, D[:, 0, :], 0, xhi, xlo)

            @block.scalar
            def _(act):
                def group(g):
                    act.wait_ge(u_scaled, g + 2)
                    act.activation(u, u, ACT.Gelu_apprx_tanh).then_inc(u_gelu, 1)
                    act.wait_ge(mm, 2 * g + 1)
                    K.split_hi(act, g + (n0 // 2 + 1), 0)
                    act.wait_ge(g_scaled, g + 2)
                    act.activation(gate, gate, ACT.Silu).then_inc(g_silu, 1)
                    act.wait_ge(mm, 2 * g + 2)
                    K.split_hi(act, g + (n0 // 2 + 1), 1)
                    act.wait_ge(y_done, g + 1)
                    act.activation(yhi[:, g, :], y, ACT.Copy).then_inc(y_hi, 1)

                with act.Fori(0, KT) as g:
                    group(g)

            @block.vector
            def _(dve):
                def scale_v(g):
                    dve.wait_ge(mix, g + 1)
                    dve.tensor_tensor(vS[:, :, :], vN[:, g, :].rearrange("p (c d) -> p c d", c=NC),
                                      K.rtok[:, :].unsqueeze(2).to_broadcast([P, NC, P]),
                                      ALU.mult).then_inc(v_scaled, 1)

                def group(g, last=False):
                    gv = K.vec[:, bass.ds(g + VEC["g_v"], 1)]
                    dve.wait_ge(mm, 2 * g + 1)
                    dve.tensor_tensor(u, D[:, 0, :], K.R[:, :], ALU.mult).then_inc(u_scaled, 1)
                    K.split_lo(dve, g + (n0 // 2 + 1), 0)
                    dve.wait_ge(mix, g + 2)
                    dve.wait_ge(bs_land, 16 * g + 16)
                    b = bs[:, :].unsqueeze(1).to_broadcast([P, NC, P])
                    m = mixed[:, :].rearrange("p (c t) -> p c t", c=NC)
                    dve.scalar_tensor_tensor(m, m, gv, b, ALU.mult, ALU.add).then_inc(biased, 1)
                    dve.wait_ge(biased, g + 2)
                    dve.wait_ge(u_gelu, g + 1)
                    dve.tensor_tensor(u, mixed[:, :], u, ALU.mult).then_inc(uy, 1)
                    if not last:
                        scale_v(g + 1)
                    dve.wait_ge(mm, 2 * g + 2)
                    dve.tensor_tensor(gate, D[:, 1, :], K.R[:, :], ALU.mult).then_inc(g_scaled, 1)
                    K.split_lo(dve, g + (n0 // 2 + 1), 1)
                    dve.wait_ge(g_silu, g + 1)
                    dve.tensor_tensor(y, u, gate, ALU.mult).then_inc(y_done, 1)
                    dve.wait_ge(y_hi, g + 1)
                    dve.tensor_tensor(ylo[:, g, :], y, yhi[:, g, :].bitcast(F32), ALU.subtract).then_inc(y_lo, 1)

                for q in (u_scaled, g_scaled, biased, uy):
                    dve.sem_inc(q, 1)
                scale_v(0)
                with dve.Fori(0, KT - 1) as g:
                    group(g)
                group(KT - 1, last=True)


def stage_pa(K, D, xhi, xlo, yhi, ylo, spill):
    nc, n0 = K.nc, FIRST["pa"]
    with ExitStack() as ctx:
        sem = K.semaphores("pa_")
        gate, merged = K.sq[:, 0, :], K.sq[:, 1, :]
        mm, g_scaled, g_sig, m_done, spilled = sem("mm"), sem("gs"), sem("sig"), sem("merged"), sem("spilled")
        with nc.Block() as block:
            @block.sync
            def _(sp):
                K.load_ahead(sp, "pa")

            @block.gpsimd
            def _(pool):
                with pool.Fori(0, KT) as j:
                    pool.wait_ge(m_done, j + 2)
                    pool.dma_start(spill[j, :, :], merged).then_inc(spilled, 16)
                pool.wait_ge(spilled, 16 * KT)

            @block.tensor
            def _(pe):
                def gate_tile(j):
                    pe.wait_ge(K.w_lo, 2 * j + (n0 + 1))
                    pe.wait_ge(g_scaled, j + 1)
                    K.dense(pe, D[:, 0, :], 0, xhi, xlo).then_inc(mm, 1)

                def proj_tile(j):
                    pe.wait_ge(K.w_lo, 2 * j + (n0 + 2))
                    pe.wait_ge(m_done, j + 1)
                    K.dense(pe, D[:, 1, :], 1, yhi, ylo).then_inc(mm, 1)

                pe.sem_inc(mm, 1)
                proj_tile(0)
                with pe.Fori(1, KT) as j:
                    gate_tile(j)
                    proj_tile(j)

            @block.scalar
            def _(act):
                def tile(j):
                    act.wait_ge(g_scaled, j + 2)
                    act.activation(gate, gate, ACT.Sigmoid).then_inc(g_sig, 1)
                    for s in range(2):
                        act.wait_ge(mm, 2 * j + s + 1)
                        K.split_hi(act, j + (n0 // 2 + 1), s)

                with act.Fori(0, KT) as j:
                    tile(j)

            @block.vector
            def _(dve):
                def tile(j):
                    dve.wait_ge(mm, 2 * j + 1)
                    dve.wait_ge(m_done, j + 1)
                    dve.tensor_tensor(gate, D[:, 0, :], K.R[:, :], ALU.mult).then_inc(g_scaled, 1)
                    K.split_lo(dve, j + (n0 // 2 + 1), 0)
                    dve.wait_ge(mm, 2 * j + 2)
                    dve.wait_ge(g_sig, j + 1)
                    if not (isinstance(j, int) and j == 0):
                        dve.wait_ge(spilled, 16 * j)
                    dve.tensor_tensor(merged, D[:, 1, :], gate, ALU.mult).then_inc(m_done, 1)
                    K.split_lo(dve, j + (n0 // 2 + 1), 1)

                for q in (g_scaled, m_done):
                    dve.sem_inc(q, 1)
                tile(0)
                with dve.Fori(1, KT) as j:
                    tile(j)


UNITS = [3] * 16 + [5, 5, 6]
N_UNITS = 4 * 2 * KT
SLOT_OF = [slot for slot, n in enumerate(UNITS) for _ in range(n)]
ROWS = [(h, i) for h in range(2) for i in range(NC)]
T_GROUPS = [(i + 4) // 4 for _, i in ROWS]
T_BEFORE = [sum(T_GROUPS[:r]) for r in range(17)]
T_PAIR = T_BEFORE[16]


def half_done_slot(c, half):
    return SLOT_OF[(2 * c + half) * KT + KT - 1]


def stage_attention(K, D, xhi, xlo, stack, out, y_first):
    nc, io = K.nc, K.io
    name = "att"
    n0 = FIRST[name]
    TV, TQ, TK, TG = range(4)
    with ExitStack() as ctx:
        sem = K.semaphores(name + "_")
        sb = lambda n, shape: ctx.enter_context(nc.sbuf_tensor(f"{name}_{n}", shape, F32))
        ps = lambda n, cols: ctx.enter_context(nc.psum_tensor(f"{name}_{n}", [P, cols], F32))
        scores = ps("scores", S)
        turned = [ps(f"turned{b}", H) for b in range(2)]
        pO = ps("pO", H)
        pV = ps("pV", H)
        vN, gT, y_sb = (sb(n, [P, 2, S]) for n in ("vN", "gT", "y"))
        qT, kT = K.sq[:, 0, :], K.sq[:, 1, :]
        q_low = ctx.enter_context(nc.sbuf_tensor("att_q_low", [P, S], F32R))
        k_low = ctx.enter_context(nc.sbuf_tensor("att_k_low", [P, 2, S], F32R))
        vT = K.acc
        bias = sb("bias", [P, 2, S])
        rows = sb("rows", [P, 2, S])
        wT = sb("wT", [P, 2, S])
        yN = sb("yN", [P, NC, P])
        stat = sb("stat", [P, 16])
        rsum = sb("rsum", [P, 16])
        rinv = sb("rinv", [P, 16])

        dn, evac = sem("dn"), sem("evac")
        v_turn, v_copy = sem("v_turn"), sem("v_copy")
        qk, biased, ex = sem("qk"), sem("biased"), sem("ex")
        turn, tcopy, pv, ri, yn = sem("turn"), sem("tcopy"), sem("pv"), sem("ri"), sem("yn")
        reduce_go = sem("reduce_go")
        y_turn, y_out, silu = sem("y_turn"), sem("y_out"), sem("silu")
        q_hi, q_lo, k_hi, k_lo, stacked = sem("q_hi"), sem("q_lo"), sem("k_hi"), sem("k_lo"), sem("stacked")
        y_left, y_free, dma_go = sem("y_left"), sem("y_free"), sem("dma_go")
        reloaded = sem("reloaded")
        b_land = [sem(f"b_land{h}") for h in range(2)]

        with nc.Block() as block:
            @block.sync
            def _(sp):
                for h in range(2):
                    sp.dma_start(bias[:, h, :], io["alibi"][h, :, :]).then_inc(b_land[h], 16)

                def pair(p):
                    for c in range(4):
                        n = 4 * p + (n0 + 4 + c)
                        sp.wait_ge(K.w_lo, n + 1)
                        K.load_weight(sp, n + 2, c % 2)
                        if c % 2 == 1:
                            h = c // 2
                            sp.wait_ge(biased, 16 * p + (8 * h + 8 + 1))
                            sp.dma_start(bias[:, h, :], io["alibi"][2 * p + (2 + h), :, :]).then_inc(b_land[h], 16)

                for c in range(4):
                    sp.wait_ge(K.w_lo, n0 + c + 1)
                    K.load_weight(sp, n0 + c + 2, c % 2)
                with sp.Fori(0, PAIRS - 1) as p:
                    pair(p)
                sp.wait_ge(y_turn, 2 * (PAIRS - 1) + 1)
                sp.wait_ge(y_free, 2 + KT // 2)
                sp.dma_start(y_first[:, 0:KT // 2, :], out[0:KT // 2].rearrange("k p t -> p k t")).then_inc(reloaded, 16)
                sp.wait_ge(reloaded, 16)

            @block.gpsimd
            def _(pool):
                def stack_parts(P_, q):
                    pool.wait_ge(q_lo, P_ + 1)
                    pool.sem_inc(dma_go, 1)
                    for h in range(2):
                        pool.dma_start(stack[HD - HD * h:P - HD * h, q, h, :],
                                       q_low[HD * h:HD * h + HD, :]).then_inc(stacked, 16)
                    pool.wait_ge(k_hi, P_ + 1)
                    pool.sem_inc(dma_go, 1)
                    for h in range(2):
                        pool.dma_start(stack[HD - HD * h:P - HD * h, q, 2 + h, :],
                                       stack[HD * h:HD * h + HD, q, 2 + h, :]).then_inc(stacked, 16)

                def store(p, q):
                    pool.wait_ge(y_out, 2 * p + 4)
                    pool.sem_inc(dma_go, 1)
                    pool.dma_start(out[p, :, :], y_sb[:, q, :]).then_inc(y_left, 16)
                    pool.wait_ge(y_left, 16 * p + 16)
                    pool.sem_inc(y_free, 1)

                stack_parts(0, 0)
                with pool.Fori(0, 3) as i:
                    for q in range(2):
                        stack_parts(2 * i + (q + 1), 1 - q)
                        store(2 * i + q, q)
                stack_parts(7, 1)
                store(6, 0)
                store(7, 1)

            @block.tensor
            def _(pe):
                def units(p, a, b):
                    for u in range(a, b):
                        c, half, k = u // (2 * KT), (u // KT) % 2, u % KT
                        if half == 0 and k == 0:
                            pe.wait_ge(K.w_lo, 4 * p + (n0 + c + 1))
                        if k == 0:
                            pe.wait_ge(evac, 8 * p + (2 * c + half + 1))
                        last = K.products(pe, D[:, half * H:half * H + H], c % 2, k, k, xhi, xlo, half,
                                          k == 0, k == KT - 1)
                        if k == KT - 1:
                            last.then_inc(dn, 1)

                def turn_v(p, g):
                    pe.wait_ge(evac, 8 * p + (2 * TV + g + 3))
                    pe.wait_ge(v_copy, 2 * p + (g + 1))
                    for c in range(4):
                        col = (4 * g + c) * P
                        last = pe.transpose(pV[:, c * P:c * P + P], vT[:, col:col + P], K.ident[:, :])
                    last.then_inc(v_turn, 1)

                def score(p, q, r):
                    h, i = ROWS[r]
                    rows_h = slice(HD * h, HD * h + HD)
                    if r == 0:
                        pe.wait_ge(k_lo, p + 1)
                        pe.wait_ge(stacked, 64 * p + 64)
                    pe.wait_ge(biased, 16 * p + (r + 1))
                    for c0 in range(0, (i + 1) * P, H):
                        c1 = min(c0 + H, (i + 1) * P)
                        pe.matmul(scores[:, c0:c1], stack[:, q, h, i * P:i * P + P], stack[:, q, 2 + h, c0:c1],
                                  start=True, stop=False)
                        last = pe.matmul(scores[:, c0:c1], stack[rows_h, q, h, i * P:i * P + P],
                                         k_low[rows_h, q, c0:c1], start=False, stop=True)
                    last.then_inc(qk, 1)

                def turn_weights(p, r):
                    h, i = ROWS[r]
                    pe.wait_ge(ex, 16 * p + (r + 1))
                    for g in range(T_GROUPS[r]):
                        n = T_BEFORE[r] + g
                        pe.wait_ge(tcopy, T_PAIR * p + (n + 1))
                        for b in range(4 * g, min(4 * g + 4, i + 1)):
                            last = pe.transpose(turned[n % 2][:, (b % 4) * P:(b % 4) * P + P],
                                                rows[:, r % 2, b * P:b * P + P], K.ident[:, :])
                        last.then_inc(turn, 1)

                def values(p, q, r):
                    h, i = ROWS[r]
                    if r == 0:
                        pe.wait_ge(v_copy, 2 * p + 3)
                    pe.wait_ge(tcopy, T_PAIR * p + (T_BEFORE[r + 1] + 2))
                    pe.wait_ge(yn, 16 * p + (r + 1))
                    for b in range(i + 1):
                        last = pe.matmul(pO[:, 0:HD], wT[:, r % 2, b * P:b * P + P],
                                         vN[:, q, b * P + HD * h:b * P + HD * h + HD],
                                         start=b == 0, stop=b == i)
                    last.then_inc(pv, 1)

                def turn_y(p, g):
                    if g == 0:
                        pe.wait_ge(yn, 16 * p + 17)
                    pe.wait_ge(tcopy, T_PAIR * p + (T_PAIR + 2))
                    for c in range(4):
                        last = pe.transpose(turned[g][:, c * P:c * P + P], yN[:, 4 * g + c, :], K.ident[:, :])
                    last.then_inc(y_turn, 1)

                def pair(p, q, more):
                    u = 0
                    for slot in range(19):
                        if slot < 16:
                            score(p, q, slot)
                        n_units = UNITS[slot] if more else int(slot < 2 * KT)
                        units(p + 1, u, u + n_units)
                        u += n_units
                        if 1 <= slot <= 16:
                            if slot == 1:
                                pe.wait_ge(y_out, 2 * p + 2)
                            turn_weights(p, slot - 1)
                        if 2 <= slot <= 17:
                            values(p, q, slot - 2)
                        if more and slot in (8, 9):
                            turn_v(p + 1, slot - 8)
                    for g in range(2):
                        turn_y(p, g)

                pe.sem_inc(pv, 2)
                pe.sem_inc(turn, 4)
                for c in range(4):
                    units(0, 16 * c, 16 * c + 16)
                    if c == 1:
                        for g in range(2):
                            turn_v(0, g)
                with pe.Fori(0, 3) as i:
                    for q in range(2):
                        pair(2 * i + q, q, True)
                pair(6, 0, True)
                pair(7, 1, False)

            @block.scalar
            def _(act):
                def split(p, c):
                    if not (isinstance(p, int) and p == 0 and c < 2):
                        act.wait_ge(dn, 8 * p + (2 * c - 2))
                    K.split_hi(act, 2 * p + (n0 // 2 + c // 2), c % 2)

                def copy_v(p, q, g):
                    act.wait_ge(v_turn, 2 * p + (g + 1))
                    if not (isinstance(p, int) and p == 0):
                        act.wait_ge(pv, 16 * p - 14)
                    act.activation(vN[:, q, g * H:g * H + H], pV[:, :], ACT.Copy).then_inc(v_copy, 1)

                def gate(p, q):
                    act.wait_ge(evac, 8 * p + 10)
                    act.activation(gT[:, q, :], gT[:, q, :], ACT.Silu).then_inc(silu, 1)

                def high(p, q, c):
                    act.wait_ge(evac, 8 * p + (2 * c + 4))
                    src, at, done = (qT, 0, q_hi) if c == TQ else (kT, 2, k_hi)
                    for h in range(2):
                        rows_h = slice(HD * h, HD * h + HD)
                        last = act.activation(stack[rows_h, q, at + h, :], src[rows_h, :], ACT.Copy)
                    last.then_inc(done, 1)

                def weights(p, r):
                    h, i = ROWS[r]
                    n = (i + 1) * P
                    act.wait_ge(biased, 16 * p + (r + 2))
                    act.activation(rows[:, r % 2, 0:n], rows[:, r % 2, 0:n], ACT.Exp, scale=-1.0,
                                   bias=stat[:, r:r + 1], accum_out=rsum[:, r:r + 1]).then_inc(ex, 1)

                def copy_weights(p, r):
                    h, i = ROWS[r]
                    act.wait_ge(pv, 16 * p + (r + 1))
                    for g in range(T_GROUPS[r]):
                        n = T_BEFORE[r] + g
                        act.wait_ge(turn, T_PAIR * p + (n + 5))
                        cols = (min(4 * g + 4, i + 1) - 4 * g) * P
                        act.activation(wT[:, r % 2, g * H:g * H + cols], turned[n % 2][:, 0:cols],
                                       ACT.Copy).then_inc(tcopy, 1)

                def pair(p, q, more):
                    for slot in range(19):
                        if slot == 0 and not more:
                            split(p + 1, 1)
                        if slot < 16:
                            weights(p, slot)
                        if slot == 1:
                            gate(p, q)
                        if 1 <= slot <= 16:
                            copy_weights(p, slot - 1)
                        if more:
                            if slot == 0:
                                split(p + 1, 1)
                            if slot == half_done_slot(0, 1) + 1:
                                split(p + 1, 2)
                            if slot == half_done_slot(1, 1) + 1:
                                split(p + 1, 3)
                            if slot in (9, 10):
                                copy_v(p + 1, 1 - q, slot - 9)
                            for c in (TQ, TK):
                                if slot == half_done_slot(c, 1) + 1:
                                    high(p + 1, 1 - q, c)
                        if more and slot == half_done_slot(2, 1) + 1:
                            split(p + 2, 0)
                act.sem_inc(v_copy, 1)
                act.sem_inc(tcopy, 2)
                split(0, 2)
                for g in range(2):
                    copy_v(0, 0, g)
                high(0, 0, TQ)
                split(0, 3)
                high(0, 0, TK)
                split(1, 0)
                with act.Fori(0, 3) as i:
                    for q in range(2):
                        pair(2 * i + q, q, True)
                pair(6, 0, True)
                pair(7, 1, False)

            @block.vector
            def _(dve):
                def split(p, c):
                    K.split_lo(dve, 2 * p + (n0 // 2 + c // 2), c % 2)

                def scale(p, q, c, half):
                    cols = slice(half * H, half * H + H)
                    dve.wait_ge(dn, 8 * p + (2 * c + half + 1))
                    if c == TV and not (isinstance(p, int) and p == 0):
                        dve.wait_ge(v_turn, 2 * p)
                    dst = {TV: vT[:, cols], TQ: qT[:, cols], TK: kT[:, cols], TG: gT[:, q, cols]}[c]
                    if c == TQ:
                        dve.scalar_tensor_tensor(dst, D[:, cols], HD ** -0.5, K.R[:, cols],
                                                 ALU.mult, ALU.mult).then_inc(evac, 1)
                    else:
                        dve.tensor_tensor(dst, D[:, cols], K.R[:, cols], ALU.mult).then_inc(evac, 1)

                def low(p, q, c):
                    src, at, hi_done, done = (qT, 0, q_hi, q_lo) if c == TQ else (kT, 2, k_hi, k_lo)
                    dve.wait_ge(hi_done, p + 1)
                    for h in range(2):
                        rows_h = slice(HD * h, HD * h + HD)
                        dst = q_low[rows_h, :] if c == TQ else k_low[rows_h, q, :]
                        last = dve.tensor_tensor(dst, src[rows_h, :], stack[rows_h, q, at + h, :].bitcast(F32),
                                                 ALU.subtract)
                    last.then_inc(done, 1)

                def add_bias(p, r):
                    h, i = ROWS[r]
                    n = (i + 1) * P
                    dve.wait_ge(qk, 16 * p + (r + 1))
                    if i == 0:
                        dve.wait_ge(b_land[h], 16 * p + 16)
                    dve.wait_ge(turn, T_PAIR * p + (T_BEFORE[r - 1] + 4 if r >= 1 else 2))
                    dve.sem_inc(reduce_go, 1)
                    dve.tensor_tensor_reduce(rows[:, r % 2, 0:n], scores[:, 0:n], bias[:, h, S - n:S],
                                             -1.0, 3e38, ALU.add, ALU.min, stat[:, r:r + 1]).then_inc(biased, 1)

                def normalise(p, r):
                    h, i = ROWS[r]
                    dve.wait_ge(ex, 16 * p + (r + 1))
                    dve.reciprocal(rinv[:, r:r + 1], rsum[:, r:r + 1]).then_inc(ri, 1)
                    dve.wait_ge(ri, 16 * p + (r + 1))
                    dve.wait_ge(pv, 16 * p + (r + 3))
                    if r == 0:
                        dve.wait_ge(y_turn, 2 * p + 1)
                    dve.tensor_scalar(yN[:, i, HD * h:HD * h + HD], pO[:, 0:HD],
                                      rinv[:, r:r + 1], None, ALU.mult).then_inc(yn, 1)

                def output(p, q, g):
                    cols = slice(g * H, g * H + H)
                    dve.wait_ge(y_turn, 2 * p + (g + 2))
                    dve.wait_ge(silu, p + 1)
                    dve.wait_ge(y_free, p + 1)
                    dve.tensor_tensor(y_sb[:, q, cols], turned[g][:, :], gT[:, q, cols], ALU.mult).then_inc(y_out, 1)

                def pair(p, q, more):
                    for slot in range(19):
                        if slot == 0 and not more:
                            split(p + 1, 1)
                        if slot >= 3:
                            normalise(p, slot - 3)
                        if slot < 16:
                            add_bias(p, slot)
                        if more:
                            for c in range(4):
                                for half in range(2):
                                    if half_done_slot(c, half) + 1 == slot:
                                        scale(p + 1, 1 - q, c, half)
                                if c in (TQ, TK) and slot == half_done_slot(c, 1) + 2:
                                    low(p + 1, 1 - q, c)
                            if slot == 0:
                                split(p + 1, 1)
                            if slot == half_done_slot(0, 1) + 1:
                                split(p + 1, 2)
                            if slot == half_done_slot(1, 1) + 1:
                                split(p + 1, 3)
                        if more and slot == half_done_slot(2, 1) + 1:
                            split(p + 2, 0)
                    if more:
                        scale(p + 1, 1 - q, 3, 1)
                    for g in range(2):
                        output(p, q, g)

                dve.sem_inc(evac, 2)
                dve.sem_inc(biased, 1)
                dve.sem_inc(yn, 1)
                dve.sem_inc(y_out, 2)
                dve.sem_inc(y_free, 2)
                dve.sem_inc(y_turn, 1)
                for c in range(4):
                    for half in range(2):
                        scale(0, 0, c, half)
                    if c < 2:
                        split(0, c + 2)
                    if c in (TQ, TK):
                        low(0, 0, c)
                    if c == 2:
                        split(1, 0)
                with dve.Fori(0, 3) as i:
                    for q in range(2):
                        pair(2 * i + q, q, True)
                pair(6, 0, True)
                pair(7, 1, False)


def stage_pb(K, D, xhi, xlo, y_dram, y, yhi, ylo, spill, merged):
    nc, n0 = K.nc, FIRST["pb"]
    with ExitStack() as ctx:
        sem = K.semaphores("pb_")
        D2 = ctx.enter_context(nc.psum_tensor("pb_D2", [P, S], F32))
        gate, part_a = K.sq[:, 0, :], K.sq[:, 1, :]
        y_hi, y_lo, y_land = sem("y_hi"), sem("y_lo"), [sem(f"y_land{k}") for k in range(KT // 2)]
        mm, g_scaled, g_sig, prod, m_done, a_land = sem("mm"), sem("gs"), sem("sig"), sem("prod"), sem("merged"), sem("a_land")
        with nc.Block() as block:
            @block.sync
            def _(sp):
                for k in range(KT // 2):
                    sp.dma_start(y[:, KT // 2 + k, :], y_dram[KT // 2 + k, :, :]).then_inc(y_land[k], 16)
                K.load_ahead(sp, "pb")

            @block.gpsimd
            def _(pool):
                with pool.Fori(0, KT) as j:
                    pool.wait_ge(m_done, j + 1)
                    pool.dma_start(part_a, spill[j, :, :]).then_inc(a_land, 16)

            @block.tensor
            def _(pe):
                def tile(j, first=False):
                    if first:
                        pe.sem_inc(mm, 1)
                    else:
                        pe.wait_ge(K.w_lo, 2 * j + (n0 + 1))
                        pe.wait_ge(g_scaled, j)
                        K.dense(pe, D[:, :], 0, xhi, xlo).then_inc(mm, 1)
                    pe.wait_ge(K.w_lo, 2 * j + (n0 + 2))
                    if not first:
                        pe.wait_ge(prod, j)
                    K.dense(pe, D2[:, :], 1, yhi, ylo, y_lo if first else None).then_inc(mm, 1)

                tile(0, first=True)
                with pe.Fori(1, KT) as j:
                    tile(j)

            @block.scalar
            def _(act):
                def tile(j):
                    act.wait_ge(g_scaled, j + 1)
                    act.activation(gate, gate, ACT.Sigmoid).then_inc(g_sig, 1)
                    for s in range(2):
                        act.wait_ge(mm, 2 * j + s + 1)
                        K.split_hi(act, j + (n0 // 2 + 1), s)

                for k in range(KT):
                    if k >= KT // 2:
                        act.wait_ge(y_land[k - KT // 2], 16)
                    K.tile_hi(act, yhi, y, k, None, y_hi)
                with act.Fori(0, KT) as j:
                    tile(j)

            @block.vector
            def _(dve):
                def tile(j):
                    dve.wait_ge(mm, 2 * j + 1)
                    dve.wait_ge(m_done, j + 1)
                    dve.tensor_tensor(gate, D[:, :], K.R[:, :], ALU.mult).then_inc(g_scaled, 1)
                    K.split_lo(dve, j + (n0 // 2 + 1), 0)
                    dve.wait_ge(mm, 2 * j + 2)
                    dve.wait_ge(g_sig, j + 1)
                    dve.tensor_tensor(gate, D2[:, :], gate, ALU.mult).then_inc(prod, 1)
                    dve.wait_ge(prod, j + 1)
                    dve.wait_ge(a_land, 16 * j + 16)
                    dve.tensor_tensor(merged[:, j, :], gate, part_a, ALU.add).then_inc(m_done, 1)
                    K.split_lo(dve, j + (n0 // 2 + 1), 1)

                dve.sem_inc(m_done, 1)
                for k in range(KT):
                    K.tile_lo(dve, ylo, yhi, y, k, None, y_hi, y_lo)
                with dve.Fori(0, KT) as j:
                    tile(j)


def stage_residual(K, name, src, xhi, xlo, f_sb, x_dram, src_dram=None):
    nc, n0 = K.nc, FIRST[name]
    with ExitStack() as ctx:
        sem = K.semaphores(name + "_")
        D = ctx.enter_context(nc.psum_tensor(name + "_D", [P, 2, S], F32))
        x_hi, x_lo, mm, added, landed = sem("x_hi"), sem("x_lo"), sem("mm"), sem("added"), sem("landed")
        sq_done, acc_done = sem("sq"), sem("acc")
        src_land = [sem(f"src_land{k}") for k in range(KT // 2)]
        with nc.Block() as block:
            @block.sync
            def _(sp):
                if src_dram is not None:
                    for k in range(KT // 2):
                        sp.dma_start(src[:, KT // 2 + k, :], src_dram[KT // 2 + k, :, :]).then_inc(src_land[k], 16)
                sp.dma_start(f_sb[:, :, :], x_dram).then_inc(landed, 16)
                K.load_ahead(sp, name)

            @block.gpsimd
            def _(pool):
                K.sum_tiles(pool, K.sq, sq_done, acc_done)

            @block.tensor
            def _(pe):
                def tiles(i, first=False):
                    for s in range(2):
                        n = 2 * i + s
                        pe.wait_ge(K.w_lo, n + (n0 + 1))
                        if not first:
                            pe.wait_ge(added, n - 1)
                        K.dense(pe, D[:, s, :], s, xhi, xlo, x_lo if first and s == 0 else None).then_inc(mm, 1)

                tiles(0, first=True)
                with pe.Fori(1, KT // 2) as i:
                    tiles(i)

            @block.scalar
            def _(act):
                for k in range(KT):
                    if src_dram is not None and k >= KT // 2:
                        act.wait_ge(src_land[k - KT // 2], 16)
                    K.tile_hi(act, xhi, src, k, None, x_hi)

                def tiles(i, first=False):
                    for s in range(2):
                        n = 2 * i + s
                        act.wait_ge(mm, n + 1)
                        K.split_hi(act, i + (n0 // 2 + 1), s)
                        K.square_tile(act, K.sq[:, s, :], f_sb[:, n, :], n, added, n + 1, acc_done,
                                      first).then_inc(sq_done, 1)

                tiles(0, first=True)
                with act.Fori(1, KT // 2) as i:
                    tiles(i)

            @block.vector
            def _(dve):
                def tiles(i):
                    for s in range(2):
                        n = 2 * i + s
                        dve.wait_ge(mm, n + 1)
                        dve.tensor_tensor(f_sb[:, n, :], D[:, s, :], f_sb[:, n, :], ALU.add).then_inc(added, 1)
                        K.split_lo(dve, i + (n0 // 2 + 1), s)

                for k in range(KT):
                    K.tile_lo(dve, xlo, xhi, src, k, None, x_hi, x_lo)
                dve.wait_ge(landed, 16)
                with dve.Fori(0, KT // 2) as i:
                    tiles(i)


SH = 32
GH = SH // GROUPS
SD = 64
GC = GH * SD
TAPS = 4
Z_FIRST, Z_UNITS, Z_LAST = 20, [(1, 3)] * 7 + [(1, 2), (1, 2), (1, 0)], 9
assert Z_FIRST + sum(a + b for a, b in Z_UNITS) + Z_LAST == GT * 2 * KT
Y_EARLY = 6 * P
OUTS = 6 * 2 + GT * 2 + KT * 2


def stage_dt(K, x_sb, f_sb, xhi, xlo, dt, dte, acum, e_acum, e_end, acum_dram):
    nc, io = K.nc, K.io
    with ExitStack() as ctx:
        sem = K.semaphores("dt_")
        sb = lambda n, shape, dt=F32: ctx.enter_context(nc.sbuf_tensor("dt_" + n, shape, dt))
        D = ctx.enter_context(nc.psum_tensor("dt_D", [P, S], F32))
        spread = ctx.enter_context(nc.psum_tensor("dt_spread", [P, S], F32))
        sums = ctx.enter_context(nc.psum_tensor("dt_sums", [P, H], F32))
        pN = ctx.enter_context(nc.psum_tensor("dt_pN", [P, H], F32))
        pA = ctx.enter_context(nc.psum_tensor("dt_pA", [P, H], F32))
        raw, hi, lo = sb("raw", [P, KT, P]), sb("hi", [P, KT, P], F32R), sb("lo", [P, KT, P], F32R)
        tri = sb("tri", [P, P])
        head = sb("head", [P, 2, SH])
        expA = sb("expA", [P, SH])
        rows = sb("rows", [SH, S])
        W = NC * SH
        v, e, l, d, r, dA, end = (sb(n, [P, W]) for n in ("v", "e", "l", "d", "r", "dA", "end"))
        f_done, x_hi, x_lo, sq_done, acc_done = sem("f"), sem("x_hi"), sem("x_lo"), sem("sq"), sem("acc")
        sums_done, root_done, rtok_done = sem("sums"), sem("root"), sem("rtok")
        diag_done, spread_done, r_done = sem("diag"), sem("spread"), sem("r")
        sums2, root2, rtok2, diag2, spread2, r2 = (sem(n + "2") for n in ("sums", "root", "rtok", "diag", "spread", "r"))
        landed, h_done, l_done, mm = sem("landed"), sem("hi"), sem("lo"), sem("mm")
        a_step, v_step, t_step, stored = sem("a_step"), sem("v_step"), sem("t_step"), sem("stored")
        copied, copy_go = sem("copied"), sem("copy_go")
        by_head = lambda t: t.rearrange("p (c h) -> p c h", c=NC)
        all_blocks = lambda t: t.unsqueeze(1).to_broadcast([P, NC, SH])
        with nc.Block() as block:
            @block.sync
            def _(sp):
                sp.dma_start(raw[:, :, :], io["w_dt"][:, :, :]).then_inc(landed, 16)
                sp.dma_start(head[:, :, :], io["dt_head"][:, :].partition_broadcast(P)).then_inc(landed, 16)
                sp.dma_start(tri[:, :], io["causal"][:, :]).then_inc(landed, 16)
                sp.wait_ge(copied, 2)
                sp.dma_start(acum_dram, rows[:, :]).then_inc(stored, 16)
                sp.wait_ge(stored, 16)

            @block.tensor
            def _(pe):
                K.norm_sums(pe, sums, sums_done)
                K.norm_spread(pe, spread, diag_done, spread_done)
                pe.wait_ge(l_done, 1)
                for k in range(KT):
                    pe.wait_ge(x_lo, k + 1)
                    for half in range(2):
                        cols = slice(half * H, half * H + H)
                        pe.matmul(D[:, cols], hi[:, k, :], xhi[:, k, cols], start=k == 0, stop=False)
                        pe.matmul(D[:, cols], hi[:, k, :], xlo[:, k, cols], start=False, stop=False)
                        last = pe.matmul(D[:, cols], lo[:, k, :], xhi[:, k, cols], start=False, stop=k == KT - 1)
                last.then_inc(mm, 1)
                pe.wait_ge(acc_done, KT)
                K.norm_sums(pe, sums, sums2)
                pe.wait_ge(copied, 1)
                for c in range(NC):
                    last = pe.transpose(pN[:, c * SH:c * SH + SH], rows[:, c * P:c * P + P], K.ident[0:SH, 0:SH])
                last.then_inc(t_step, 1)
                pe.wait_ge(r_done, 1)
                K.norm_spread(pe, spread, diag2, spread2)
                pe.wait_ge(v_step, 9)
                for c in range(NC):
                    last = pe.matmul(D[0:SH, c * P:c * P + P], dA[:, c * SH:c * SH + SH], tri[:, :],
                                     start=True, stop=True)
                last.then_inc(t_step, 1)
                pe.matmul(pA[:, 0:W], tri[:, :], dA[:, :], start=True, stop=True)
                pe.matmul(pA[:, W:2 * W], K.ones[:, :], dA[:, :], start=True, stop=True).then_inc(t_step, 1)

            @block.scalar
            def _(act):
                act.wait_ge(landed, 48)
                K.norm_root(act, sums, DM, sums_done, root_done)
                act.activation(hi[:, :, :], raw[:, :, :], ACT.Copy).then_inc(h_done, 1)
                act.activation(expA[:, :], head[:, 1, :], ACT.Exp).then_inc(a_step, 1)
                for k in range(KT):
                    act.wait_ge(f_done, k + 1)
                    K.tile_hi(act, xhi, f_sb, k, "m_norm", x_hi)
                    K.square(act, f_sb[:, k, :], k, sq_done, acc_done)
                K.norm_root(act, sums, DM, sums2, root2)
                act.wait_ge(mm, 1)
                act.activation(rows[:, :], D[0:SH, :], ACT.Copy).then_inc(copied, 1)
                act.wait_ge(v_step, 2)
                act.activation(e[:, :], v[:, :], ACT.Abs).then_inc(a_step, 1)
                act.wait_ge(a_step, 2)
                act.activation(e[:, :], e[:, :], ACT.Exp, scale=-1.0).then_inc(a_step, 1)
                act.wait_ge(a_step, 3)
                act.activation(l[:, :], e[:, :], ACT.Ln, bias=K.ones[:, 0:1]).then_inc(a_step, 1)
                act.wait_ge(t_step, 2)
                act.activation(rows[:, :], D[0:SH, :], ACT.Copy).then_inc(copied, 1)
                act.wait_ge(v_step, 11)
                act.activation(e_acum[:, :], acum[:, :], ACT.Exp).then_inc(a_step, 1)
                act.activation(dte[:, :], dte[:, :], ACT.Exp).then_inc(a_step, 1)
                act.wait_ge(v_step, 12)
                act.activation(e_end[:, :], end[:, :], ACT.Exp).then_inc(a_step, 1)

            @block.vector
            def _(dve):
                dve.wait_ge(h_done, 1)
                dve.tensor_tensor(lo[:, :, :], raw[:, :, :], hi[:, :, :].bitcast(F32), ALU.subtract).then_inc(l_done, 1)
                K.norm_recip(dve, root_done, rtok_done)
                K.norm_diag(dve, diag_done)
                K.norm_copy(dve, spread, spread_done, r_done)
                for k in range(KT + 1):
                    if k < KT:
                        dve.scalar_tensor_tensor(f_sb[:, k, :], x_sb[:, k, :], K.gain("g_final", k), K.R[:, :],
                                                 ALU.mult, ALU.mult).then_inc(f_done, 1)
                    if k >= 1:
                        dve.wait_ge(f_done, k)
                        K.tile_lo(dve, xlo, xhi, f_sb, k - 1, "m_norm", x_hi, x_lo)
                dve.wait_ge(diag_done, 1)
                dve.wait_ge(f_done, KT)
                K.norm_recip(dve, root2, rtok2)
                K.norm_diag(dve, diag2)
                steps = [0]

                def step(ins):
                    steps[0] += 1
                    ins.then_inc(v_step, 1)
                    dve.wait_ge(v_step, steps[0])

                dve.wait_ge(t_step, 1)
                step(dve.tensor_tensor(by_head(v[:, :]), by_head(pN[:, 0:W]),
                                       K.rtok[:, :].unsqueeze(2).to_broadcast([P, NC, SH]), ALU.mult))
                dve.wait_ge(landed, 48)
                step(dve.tensor_tensor(by_head(v[:, :]), by_head(v[:, :]), all_blocks(head[:, 0, :]), ALU.add))
                K.norm_copy(dve, spread, spread2, r2)
                dve.wait_ge(a_step, 4)
                step(dve.tensor_scalar(d[:, :], e[:, :], 1.0, None, ALU.add))
                step(dve.tensor_scalar(d[:, :], d[:, :], -1.0, 1e-30, ALU.add, ALU.add))
                step(dve.reciprocal(r[:, :], d[:, :]))
                step(dve.scalar_tensor_tensor(l[:, :], l[:, :], 1e-30, r[:, :], ALU.add, ALU.mult))
                step(dve.tensor_tensor(l[:, :], l[:, :], e[:, :], ALU.mult))
                step(dve.scalar_tensor_tensor(dt[:, :], v[:, :], 0.0, l[:, :], ALU.max, ALU.add))
                step(dve.scalar_tensor_tensor(by_head(dA[:, :]), by_head(dt[:, :]), -1.0, all_blocks(expA[:, :]),
                                              ALU.mult, ALU.mult))
                dve.wait_ge(t_step, 3)
                step(dve.tensor_copy(acum[:, :], pA[:, 0:W]))
                step(dve.tensor_tensor(dte[:, :], pA[:, W:2 * W], acum[:, :], ALU.subtract))
                dve.tensor_copy(end[:, :], pA[:, W:2 * W]).then_inc(v_step, 1)
                dve.wait_ge(a_step, 6)
                dve.tensor_tensor(dte[:, :], dte[:, :], dt[:, :], ALU.mult)

            @block.gpsimd
            def _(pool):
                K.sum_squares(pool, KT, sq_done, acc_done)


def stage_ssm(K, xhi, xlo, f_sb, dt, dte, acum, e_acum, e_end, acum_dram):
    nc, io, n0 = K.nc, K.io, FIRST["ssm"]
    with ExitStack() as ctx:
        sem = K.semaphores("ssm_")
        sb = lambda n, shape, dt=F32: ctx.enter_context(nc.sbuf_tensor("ssm_" + n, shape, dt))
        D = ctx.enter_context(nc.psum_tensor("ssm_D", [P, S], F32))
        pX = ctx.enter_context(nc.psum_tensor("ssm_pX", [P, H], F32))
        pCB = ctx.enter_context(nc.psum_tensor("ssm_pCB", [P, H], F32))
        pY = ctx.enter_context(nc.psum_tensor("ssm_pY", [P, S], F32))
        pS = ctx.enter_context(nc.psum_tensor("ssm_pS", [P, H], F32))
        pT = ctx.enter_context(nc.psum_tensor("ssm_pT", [P, H], F32))
        banks = [D[:, 0:H], D[:, H:S], pX[:, :], pT[:, :]]
        BC = sb("BC", [P, 2, S])
        xs = sb("xs", [P, GT, S])
        with ExitStack() as shared:
            scratch = shared.enter_context(nc.sbuf_tensor("ssm_scratch", [P, GT, S], F32))
        yhi = sb("yhi", [P, GT, S], F32R)
        xd_odd = scratch[:, GT - 1, :]
        with ExitStack() as shared:
            z = shared.enter_context(nc.sbuf_tensor("ssm_z", [P, GT, S], F32))
        ylo = sb("ylo", [P, GT, S], F32R)
        cb = sb("cb", [P, 2, 2, P])
        state, decayed = sb("state", [P, GC]), sb("decayed", [P, GC])
        y_sb = sb("y_sb", [P, GC])
        u = K.sq
        E = [K.sq[:, s, :].rearrange("p (h l) -> p h l", h=GH) for s in range(2)]
        x_dt, x_dte = [t[:, 0:GC] for t in (K.acc[:, :], xd_odd)], [t[:, GC:2 * GC] for t in (K.acc[:, :], xd_odd)]
        tmp = K.sq[:, 1, :]

        dn, evac = sem("dn"), sem("evac")
        cv_a, cv_d, cv_s = sem("cv_a"), sem("cv_d"), sem("cv_s")
        row_land = [sem("row0"), sem("row1")]
        seg, sel, ex, weighted, select_go = sem("seg"), sem("sel"), sem("ex"), sem("weighted"), sem("select_go")
        s1, ps_done, s2, s3, cb_copy, xd = sem("s1"), sem("ps"), sem("s2"), sem("s3"), sem("cb_copy"), sem("xd")
        y_inter, y_done, st_decay, st_done, y_turned = sem("y_inter"), sem("y_done"), sem("st_decay"), sem("st_done"), sem("y_turned")
        yz_early, y_hi_early, high_go = sem("yz_early"), sem("y_hi_early"), sem("high_go")
        silu, yz, y_hi, y_lo = sem("silu"), sem("yz"), sem("y_hi"), sem("y_lo")
        sq_done, acc_done = sem("sq"), sem("acc")
        sums_done, root_done, rtok_done = sem("sums"), sem("root"), sem("rtok")
        diag_done, spread_done, r_done, scaled = sem("diag"), sem("spread"), sem("r"), sem("scaled")
        Rg = K.acc

        def heads(t, c, g, width):
            return t[:, bass.ds(8 * g + c * SH, GH)].unsqueeze(2).to_broadcast([P, GH, width])

        with nc.Block() as block:
            @block.sync
            def _(sp):
                def group(g):
                    def load(m):
                        n = GROUP_TILES * g + (n0 + m)
                        sp.wait_ge(K.w_lo, n + 1)
                        K.load_weight(sp, n + 2, m % 2)

                    def row(c):
                        if c == 0:
                            sp.wait_ge(cv_d, 18 * g + 18)
                        if c >= 2:
                            sp.wait_ge(s2, 8 * g + (c - 1))
                        sp.dma_start(E[c % 2], acum_dram[bass.ds(8 * g, GH), c * P:c * P + P]
                                     .partition_broadcast(P)).then_inc(row_land[c % 2], 16)

                    for m in range(6):
                        load(m)
                    for c in range(NC):
                        row(c)
                        if c % 2 == 1:
                            load(6 + c // 2)
                    for m in range(10, 14):
                        load(m)

                with sp.Fori(0, GROUPS) as g:
                    group(g)

            @block.tensor
            def _(pe):
                def units(g, c, a, b):
                    for q in range(a, b):
                        half, k = q // KT, q % KT
                        if q == 0:
                            pe.wait_ge(K.w_lo, GROUP_TILES * g + (n0 + c + 1))
                        if k == 0:
                            pe.wait_ge(evac, OUTS * g + (2 * c + half + 1))
                        last = K.products(pe, D[:, half * H:half * H + H], c % 2, k, k, xhi, xlo, half,
                                          k == 0, k == KT - 1)
                        if k == KT - 1:
                            last.then_inc(dn, 1)

                def turn_in(g, c):
                    cols = slice(c * P, c * P + P)
                    if c == 0:
                        pe.wait_ge(cv_s, 6 * g + 6)
                    pe.wait_ge(xd, 8 * g + (c + 1))
                    pe.wait_ge(cb_copy, 8 * g + (c + 1))
                    for k in range(GT):
                        pe.transpose(pX[:, k * P:k * P + P], xs[:, k, cols], K.ident[:, :])
                    pe.transpose(pCB[:, P:2 * P], BC[:, 0, cols], K.ident[:, :])
                    pe.matmul(pCB[:, 0:P], BC[:, 0, cols], BC[:, 1, cols], start=True, stop=True).then_inc(s1, 1)

                def products(g, c):
                    pe.wait_ge(st_done, 9 * g + (c + 1))
                    pe.wait_ge(y_done, 8 * g + (c + 1))
                    pe.matmul(pY[:, 0:H], BC[:, 1, c * P:c * P + P], state[:, :], start=True, stop=True)
                    pe.wait_ge(xd, 8 * g + (c + 2))
                    pe.wait_ge(cb_copy, 8 * g + (c + 2))
                    pe.matmul(pS[:, :], cb[:, c % 2, 1, :], x_dte[c % 2], start=True, stop=True).then_inc(ps_done, 1)
                    pe.wait_ge(weighted, 8 * g + (c + 1))
                    for h in range(GH):
                        last = pe.matmul(pY[:, H + h * SD:H + h * SD + SD], E[c % 2][:, h, :],
                                         x_dt[c % 2][:, h * SD:h * SD + SD], start=True, stop=True)
                    last.then_inc(s2, 1)

                def turn_out(g, c):
                    pe.wait_ge(y_done, 8 * g + (c + 2))
                    pe.wait_ge(y_turned, 8 * g + (c + 1))
                    for k in range(GT):
                        last = pe.transpose(pT[:, k * P:k * P + P], y_sb[:, k * P:k * P + P], K.ident[:, :])
                    last.then_inc(s3, 1)

                def group(g):
                    for c in range(6):
                        units(g, c, 0, 16)
                    def z_units(a, b):
                        for q in range(a, b):
                            units(g, 6 + q // 16, q % 16, q % 16 + 1)

                    z_units(0, Z_FIRST)
                    turn_in(g, 0)
                    q = Z_FIRST
                    for slot in range(10):
                        for part, n in enumerate(Z_UNITS[slot]):
                            z_units(q, q + n)
                            q += n
                            if part == 0 and 1 <= slot <= 8:
                                products(g, slot - 1)
                        if slot >= 2:
                            turn_out(g, slot - 2)
                        if slot < 7:
                            turn_in(g, slot + 1)
                    z_units(q, q + Z_LAST)

                    def out_products(o, k):
                        j, half = o // 2, o % 2
                        return K.products(pe, banks[o % 4], j // 2 % 2, 4 * (j % 2) + k, k, yhi, ylo, half,
                                          k == 0, k == GT - 1)

                    pe.wait_ge(K.w_lo, GROUP_TILES * g + (n0 + 11))
                    pe.wait_ge(xd, 8 * g + 9)
                    pe.wait_ge(y_turned, 8 * g + 9)
                    for o in (2, 3, 0, 1):
                        if o < 2:
                            pe.wait_ge(evac, OUTS * g + (20 + o + 1))
                        for k in range(GT - 1):
                            if o == 2:
                                pe.wait_ge(y_lo, 4 * g + (k + 1))
                            out_products(o, k)
                    pe.wait_ge(y_lo, 4 * g + 4)
                    for o in range(4):
                        out_products(o, GT - 1).then_inc(dn, 1)
                    pe.wait_ge(acc_done, 3 * g + 3)
                    K.norm_sums(pe, pCB, sums_done)
                    pe.wait_ge(diag_done, g + 1)
                    for half in range(2):
                        last = pe.matmul(pY[:, half * H:half * H + H], K.ones[:, :],
                                         K.sq[:, 0, half * H:half * H + H], start=True, stop=True)
                    last.then_inc(spread_done, 1)
                    for o in range(4, 2 * KT):
                        if o % 4 == 0:
                            pe.wait_ge(K.w_lo, GROUP_TILES * g + (n0 + 11 + o // 4))
                        pe.wait_ge(evac, OUTS * g + (20 + o - 1))
                        for k in range(GT):
                            last = out_products(o, k)
                        last.then_inc(dn, 1)

                with pe.Fori(0, GROUPS) as g:
                    group(g)

            @block.scalar
            def _(act):
                def split(g, m, outs):
                    act.wait_ge(dn, OUTS * g + outs)
                    K.split_hi(act, 7 * g + (n0 // 2 + m // 2), m % 2)

                def conv_tile(c, g):
                    return (BC[:, c, :], 16 + 4 * c + g) if c < 2 else (xs[:, c - 2, :], 4 * g + (c - 2))

                def group(g):
                    for c in range(6):
                        dst, t = conv_tile(c, g)
                        act.wait_ge(evac, OUTS * g + (2 * c + 4))
                        act.activation(dst, u[:, c % 2, :], ACT.Identity,
                                       scale=K.vec[:, bass.ds(4 * t + (VEC["conv_w"] + 3), 1)],
                                       bias=K.vec[:, bass.ds(t + VEC["conv_b"], 1)]).then_inc(cv_a, 1)
                        split(g, c + 2, 2 * c + 2)
                        act.wait_ge(cv_d, 18 * g + (3 * c + 3))
                        act.activation(dst, dst, ACT.Silu).then_inc(cv_s, 1)

                    def silu_z(zt):
                        act.wait_ge(evac, OUTS * g + (12 + 2 * zt + 4))
                        act.activation(z[:, zt, :], z[:, zt, :], ACT.Silu).then_inc(silu, 1)
                        split(g, 8 + zt, 14 + 2 * zt)

                    silu_z(0)
                    q = Z_FIRST
                    for slot in range(10):
                        if slot < 8:
                            c = slot
                            act.wait_ge(s1, 8 * g + (c + 1))
                            if c >= 2:
                                act.wait_ge(s2, 8 * g + (c - 1))
                            act.activation(cb[:, c % 2, :, :], pCB[:, 0:2 * P].rearrange("p (a b) -> p a b", a=2),
                                           ACT.Copy).then_inc(cb_copy, 1)
                            act.wait_ge(sel, 8 * g + (c + 1))
                            act.activation(E[c % 2], E[c % 2], ACT.Exp).then_inc(ex, 1)
                        q_old, q = q, q + sum(Z_UNITS[slot])
                        if q // 16 > q_old // 16:
                            silu_z(q // 16 - 1)

                    def high_y(k, cols):
                        act.sem_inc(high_go, 1)
                        return act.activation(yhi[:, k, cols], xs[:, k, cols], ACT.Copy,
                                              scale=K.vec[:, bass.ds(4 * g + (VEC["y_norm"] + k), 1)])

                    def square_y(k):
                        if k >= 2:
                            act.wait_ge(acc_done, 3 * g + 1)
                        act.activation(K.sq[:, k % 2, :], xs[:, k, :], ACT.Square).then_inc(sq_done, 1)

                    for k in range(GT - 1):
                        act.wait_ge(yz_early, 3 * g + (k + 1))
                        high_y(k, slice(0, Y_EARLY)).then_inc(y_hi_early, 1)
                    for k in range(GT - 1):
                        act.wait_ge(yz, 4 * g + (k + 1))
                        high_y(k, slice(Y_EARLY, S)).then_inc(y_hi, 1)
                    square_y(0)
                    square_y(1)
                    silu_z(GT - 1)
                    square_y(2)
                    act.wait_ge(yz, 4 * g + GT)
                    high_y(GT - 1, slice(0, S)).then_inc(y_hi, 1)
                    square_y(GT - 1)
                    act.wait_ge(sums_done, g + 1)
                    act.activation(K.root[:, :], pCB[:, 0:NC], ACT.Sqrt, scale=1.0 / GC,
                                   bias=K.eps[:, 0:1]).then_inc(root_done, 1)
                    for m in range(4):
                        split(g, 12 + m, 24 + 4 * m)

                act.sem_inc(cb_copy, 1)
                with act.Fori(0, GROUPS) as g:
                    group(g)

            @block.vector
            def _(dve):
                def split(g, m):
                    K.split_lo(dve, 7 * g + (n0 // 2 + m // 2), m % 2)

                def scale(g, o, dst, half):
                    cols = slice(half * H, half * H + H)
                    dve.wait_ge(dn, OUTS * g + (o + 1))
                    dve.tensor_tensor(dst[:, cols], D[:, cols], K.R[:, cols], ALU.mult).then_inc(evac, 1)

                def block_work(g, c):
                    pXh = pX[:, :].rearrange("p (h d) -> p h d", h=GH)
                    dve.wait_ge(s1, 8 * g + (c + 1))
                    dve.tensor_tensor(x_dt[c % 2].rearrange("p (h d) -> p h d", h=GH), pXh, heads(dt, c, g, SD),
                                      ALU.mult)
                    dve.tensor_tensor(x_dte[c % 2].rearrange("p (h d) -> p h d", h=GH), pXh, heads(dte, c, g, SD),
                                      ALU.mult).then_inc(xd, 1)

                def weigh(g, c):
                    dve.wait_ge(ex, 8 * g + (c + 1))
                    dve.wait_ge(cb_copy, 8 * g + (c + 2))
                    dve.tensor_tensor(E[c % 2], E[c % 2], cb[:, c % 2, 0, :].unsqueeze(1).to_broadcast([P, GH, P]),
                                      ALU.mult).then_inc(weighted, 1)

                def finish(g, c):
                    y3 = y_sb[:, :].rearrange("p (h d) -> p h d", h=GH)
                    dve.wait_ge(ps_done, 8 * g + (c + 1))
                    dve.wait_ge(st_decay, 8 * g + (c + 1))
                    dve.tensor_tensor(state[:, :], decayed[:, :], pS[:, :], ALU.add).then_inc(st_done, 1)
                    dve.wait_ge(s2, 8 * g + (c + 1))
                    if c >= 1:
                        dve.wait_ge(s3, 8 * g + c)
                    dve.tensor_tensor(y3, pY[:, 0:H].rearrange("p (h d) -> p h d", h=GH),
                                      heads(e_acum, c, g, SD), ALU.mult).then_inc(y_inter, 1)
                    dve.wait_ge(y_inter, 8 * g + (c + 1))
                    dve.tensor_tensor(y_sb[:, :], y_sb[:, :], pY[:, H:S], ALU.add).then_inc(y_done, 1)

                def skip(g, c):
                    cols = slice(c * P, c * P + P)
                    dve.wait_ge(s3, 8 * g + (c + 1))
                    for k in range(GT):
                        last = dve.scalar_tensor_tensor(xs[:, k, cols], xs[:, k, cols],
                                                        K.vec[:, bass.ds(4 * g + (VEC["d_skip"] + k), 1)],
                                                        pT[:, k * P:k * P + P], ALU.mult, ALU.add)
                    last.then_inc(y_turned, 1)

                def group(g):
                    for c in range(6):
                        dst, t = (BC[:, c, :], 16 + 4 * c + g) if c < 2 else (xs[:, c - 2, :], 4 * g + (c - 2))
                        for half in range(2):
                            scale(g, 2 * c + half, u[:, c % 2, :], half)
                        dve.wait_ge(cv_a, 6 * g + (c + 1))
                        for tap in range(3):
                            lag = 3 - tap
                            w = K.vec[:, bass.ds(4 * t + (VEC["conv_w"] + tap), 1)]
                            dve.scalar_tensor_tensor(dst[:, lag:S], u[:, c % 2, 0:S - lag], w, dst[:, lag:S],
                                                     ALU.mult, ALU.add).then_inc(cv_d, 1)
                            dve.wait_ge(cv_d, 18 * g + (3 * c + tap + 1))
                        split(g, c + 2)
                    def scale_z(o):
                        scale(g, 12 + o, z[:, o // 2, :], o % 2)
                        if o % 2 == 1:
                            split(g, 8 + o // 2)

                    def gate_y(k, cols):
                        dve.wait_ge(silu, 4 * g + (k + 1))
                        return dve.tensor_tensor(xs[:, k, cols], xs[:, k, cols], z[:, k, cols], ALU.mult)

                    def low_y(k, cols):
                        return dve.scalar_tensor_tensor(ylo[:, k, cols], xs[:, k, cols],
                                                        K.vec[:, bass.ds(4 * g + (VEC["y_norm"] + k), 1)],
                                                        yhi[:, k, cols].bitcast(F32), ALU.mult, ALU.subtract)

                    dve.memset(state[:, :], 0.0).then_inc(st_done, 1)
                    scale_z(0)
                    scale_z(1)
                    block_work(g, 0)
                    weigh(g, 0)
                    q = Z_FIRST
                    for slot in range(10):
                        if 1 <= slot <= 8:
                            if slot < 8:
                                block_work(g, slot)
                            finish(g, slot - 1)
                            if slot < 8:
                                weigh(g, slot)
                        q_old, q = q, q + sum(Z_UNITS[slot])
                        if q // 8 > q_old // 8:
                            scale_z(q // 8 - 1)
                        if slot >= 2:
                            skip(g, slot - 2)
                        if slot == 7:
                            dve.wait_ge(y_turned, 8 * g + 7)
                            for k in range(GT - 1):
                                gate_y(k, slice(0, Y_EARLY)).then_inc(yz_early, 1)
                        if slot == 8:
                            for k in range(GT - 1):
                                dve.wait_ge(y_hi_early, 3 * g + (k + 1))
                                low_y(k, slice(0, Y_EARLY))
                    late = slice(Y_EARLY, S)
                    dve.wait_ge(y_turned, 8 * g + 9)
                    for k in range(GT - 1):
                        gate_y(k, late).then_inc(yz, 1)
                    scale_z(6)
                    for k in range(GT - 1):
                        dve.wait_ge(y_hi, 4 * g + (k + 1))
                        low_y(k, late).then_inc(y_lo, 1)
                    scale_z(7)
                    dve.wait_ge(sq_done, 4 * g + 2)
                    dve.tensor_tensor(K.acc[:, :], K.sq[:, 0, :], K.sq[:, 1, :], ALU.add).then_inc(acc_done, 1)
                    gate_y(GT - 1, slice(0, S)).then_inc(yz, 1)
                    dve.wait_ge(acc_done, 3 * g + 1)
                    dve.wait_ge(sq_done, 4 * g + 3)
                    dve.tensor_tensor(K.acc[:, :], K.acc[:, :], K.sq[:, 0, :], ALU.add).then_inc(acc_done, 1)
                    dve.wait_ge(y_hi, 4 * g + GT)
                    low_y(GT - 1, slice(0, S)).then_inc(y_lo, 1)
                    dve.wait_ge(acc_done, 3 * g + 2)
                    dve.wait_ge(sq_done, 4 * g + 4)
                    dve.tensor_tensor(K.acc[:, :], K.acc[:, :], K.sq[:, 1, :], ALU.add).then_inc(acc_done, 1)
                    dve.wait_ge(root_done, g + 1)
                    dve.reciprocal(K.rtok[:, :], K.root[:, :]).then_inc(rtok_done, 1)
                    dve.wait_ge(rtok_done, g + 1)
                    K.norm_diag(dve, diag_done)
                    dve.wait_ge(spread_done, g + 1)
                    dve.tensor_copy(Rg[:, :], pY[:, :]).then_inc(r_done, 1)
                    dve.wait_ge(r_done, g + 1)
                    for j in range(KT):
                        for half in range(2):
                            cols = slice(half * H, half * H + H)
                            dve.wait_ge(dn, OUTS * g + (20 + 2 * j + half + 1))
                            dve.tensor_tensor(tmp[:, cols], banks[(2 * j + half) % 4], Rg[:, cols],
                                              ALU.mult).then_inc(evac, 1)
                            dve.wait_ge(evac, OUTS * g + (20 + 2 * j + half + 3))
                            dve.tensor_tensor(f_sb[:, j, cols], f_sb[:, j, cols], tmp[:, cols], ALU.add).then_inc(scaled, 1)
                        if j % 2 == 1:
                            split(g, 12 + j // 2)
                        dve.wait_ge(scaled, 16 * g + (2 * j + 2))

                dve.sem_inc(evac, 2)
                for q in (xd, y_done, y_turned):
                    dve.sem_inc(q, 1)
                with dve.Fori(0, GROUPS) as g:
                    group(g)

            @block.gpsimd
            def _(pool):
                def group(g):
                    for c in range(NC):
                        pool.wait_ge(st_done, 9 * g + (c + 1))
                        pool.tensor_tensor(decayed[:, :].rearrange("p (h d) -> p h d", h=GH),
                                           state[:, :].rearrange("p (h d) -> p h d", h=GH),
                                           heads(e_end, c, g, SD), ALU.mult).then_inc(st_decay, 1)
                        for b in ([0, 1] if c == 0 else [c + 1] if c + 1 < NC else []):
                            pool.wait_ge(row_land[b % 2], 64 * g + (16 * (b // 2) + 16))
                            pool.tensor_tensor(E[b % 2], E[b % 2], heads(acum, b, g, P), ALU.subtract).then_inc(seg, 1)
                            pool.wait_ge(seg, 8 * g + (b + 1))
                            pool.sem_inc(select_go, 1)
                            pool.affine_select(out=E[b % 2], in_=E[b % 2], compare_op=ALU.is_ge, fill=NEG, base=0,
                                               pattern=[[0, GH], [1, P]], channel_multiplier=-1).then_inc(sel, 1)

                with pool.Fori(0, GROUPS) as g:
                    group(g)


AUX_SLOT = dict(k_square=6, k_sum=7, k_turn0=8, k_turn1=9, k_back0=10, k_back1=11, v_turn0=12,
                v_turn1=13, k_parts=12, q_parts=16, q_square=16, q_sum=17)


def stage_stick(K, xhi, xlo, f_sb, f_dram, stack, out):
    nc, io = K.nc, K.io
    name = "stick"
    n0 = FIRST[name]
    TK, TV, TQ, TG = range(4)
    with ExitStack() as ctx:
        sem = K.semaphores(name + "_")
        sb = lambda n, shape: ctx.enter_context(nc.sbuf_tensor(f"{name}_{n}", shape, F32))
        ps = lambda n, cols: ctx.enter_context(nc.psum_tensor(f"{name}_{n}", [P, cols], F32))
        D = ps("D", S)
        scores = ps("scores", S)
        turned = [ps(f"turned{b}", H) for b in range(2)]
        pO = ps("pO", H)
        pV = ps("pV", H)
        vN, gT, y_sb = (sb(n, [P, 2, S]) for n in ("vN", "gT", "y"))
        qT = sb("qT", [P, S])
        q_low = ctx.enter_context(nc.sbuf_tensor("stick_q_low", [P, S], F32R))
        k_low = ctx.enter_context(nc.sbuf_tensor("stick_k_low", [P, 2, S], F32R))
        vT = K.acc
        keep = sb("keep", [P, 2, S + 1])
        rows = sb("rows", [P, 2, S])
        wT = sb("wT", [P, 2, S])
        yN = sb("yN", [P, NC, P])
        k_root, k_inv = sb("k_root", [P, 16]), sb("k_inv", [P, 16])
        q_root, q_inv = sb("q_root", [P, 16]), sb("q_inv", [P, 16])
        q_pos, q_neg = sb("q_pos", [P, 2, 16]), sb("q_neg", [P, 2, 16])
        gains = sb("gains", [P, 1])
        select = sb("select", [P, 2])
        raw_mask = K.sq[:, 1, 0:P]
        identr = ctx.enter_context(nc.sbuf_tensor("stick_identr", [P, P], F32R))
        maskr = ctx.enter_context(nc.sbuf_tensor("stick_maskr", [P, P], F32R))
        kT = K.sq[:, 0, :]
        kRaw, square, kN = K.sq[:, 0, :], K.sq[:, 1, :], K.sq[:, 1, :]

        dn, evac = sem("dn"), sem("evac")
        v_turn, v_copy = sem("v_turn"), sem("v_copy")
        qk, sig, scan, ex = sem("qk"), sem("sig"), sem("scan"), sem("ex")
        squared, summed, rooted, k_ready, q_ready = sem("squared"), sem("summed"), sem("rooted"), sem("k_ready"), sem("q_ready")
        k_turn, kn_done, k_back, k_done = sem("k_turn"), sem("kn_done"), sem("k_back"), sem("k_done")
        landed, masks, w_gain, recip = sem("landed"), sem("masks"), sem("w_gain"), sem("recip")
        turn, tcopy, pv, yn = sem("turn"), sem("tcopy"), sem("pv"), sem("yn")
        y_turn, y_out, silu, gated = sem("y_turn"), sem("y_out"), sem("silu"), sem("gated")

        x_hi, x_lo, sums_done, root_done = sem("x_hi"), sem("x_lo"), sem("sums"), sem("root")
        rtok_done, diag_done, spread_done, r_done = sem("rtok"), sem("diag"), sem("spread"), sem("r")
        f_stored, reloaded = sem("f_stored"), sem("reloaded")
        q_hi, q_lo, k_hi, k_lo, stacked = sem("q_hi"), sem("q_lo"), sem("k_hi"), sem("k_lo"), sem("stacked")
        y_left, y_free, dma_go = sem("y_left"), sem("y_free"), sem("dma_go")

        with nc.Block() as block:
            @block.sync
            def _(sp):
                sp.dma_start(select[:, :], io["select"][:, :]).then_inc(landed, 16)
                sp.dma_start(raw_mask, io["strict"][:, :]).then_inc(landed, 16)
                sp.dma_start(f_dram, f_sb[:, :, :]).then_inc(f_stored, 16)

                def pair(p):
                    for c in range(4):
                        n = 4 * p + (n0 + 4 + c)
                        sp.wait_ge(K.w_lo, n + 1)
                        K.load_weight(sp, n + 2, c % 2)

                for c in range(4):
                    sp.wait_ge(K.w_lo, n0 + c + 1)
                    K.load_weight(sp, n0 + c + 2, c % 2)
                with sp.Fori(0, PAIRS - 1) as p:
                    pair(p)
                sp.wait_ge(y_turn, 2 * (PAIRS - 1) + 1)
                sp.wait_ge(y_free, 2 + (PAIRS - 2))
                sp.dma_start(f_sb[:, 0:4, :], out[0:4].rearrange("k p t -> p k t")).then_inc(reloaded, 16)
                sp.wait_ge(reloaded, 16)

            @block.tensor
            def _(pe):
                def units(p, a, b):
                    for u in range(a, b):
                        c, half, k = u // (2 * KT), (u // KT) % 2, u % KT
                        if half == 0 and k == 0:
                            pe.wait_ge(K.w_lo, 4 * p + (n0 + c + 1))
                        if k == 0:
                            pe.wait_ge(evac, 8 * p + (2 * c + half + 1))
                        if isinstance(p, int) and p == 0 and u < KT:
                            pe.wait_ge(x_lo, k + 1)
                        last = K.products(pe, D[:, half * H:half * H + H], c % 2, k, k, xhi, xlo, half,
                                          k == 0, k == KT - 1)
                        if k == KT - 1:
                            last.then_inc(dn, 1)

                def turn_v(p, g):
                    if g == 0:
                        pe.wait_ge(evac, 8 * p + (2 * TV + 4))
                        pe.wait_ge(k_done, 2 * p + 2)
                    else:
                        pe.wait_ge(v_copy, 2 * p + 1)
                    for c in range(4):
                        col = (4 * g + c) * P
                        last = pe.transpose(pV[:, c * P:c * P + P], vT[:, col:col + P], K.ident[:, :])
                    last.then_inc(v_turn, 1)

                def head_sums(p, which):
                    pe.wait_ge(squared, 2 * p + (which + 1))
                    if which == 1:
                        pe.wait_ge(v_copy, 2 * p + 2)
                    elif not (isinstance(p, int) and p == 0):
                        pe.wait_ge(rooted, 2 * p)
                    for c in range(NC):
                        last = pe.matmul(pV[:, 2 * c:2 * c + 2], square[:, c * P:c * P + P], select[:, :],
                                         start=True, stop=True)
                    last.then_inc(summed, 1)

                def turn_k(p, g):
                    if g == 0:
                        pe.wait_ge(rooted, 2 * p + 1)
                    else:
                        pe.wait_ge(kn_done, 2 * p + 1)
                    for c in range(4):
                        col = (4 * g + c) * P
                        last = pe.transpose(pV[:, c * P:c * P + P], kRaw[:, col:col + P], K.ident[:, :])
                    last.then_inc(k_turn, 1)

                def back_k(p, g):
                    pe.wait_ge(kn_done, 2 * p + 2)
                    if g == 1:
                        pe.wait_ge(k_done, 2 * p + 1)
                    for c in range(4):
                        col = (4 * g + c) * P
                        last = pe.transpose(pV[:, c * P:c * P + P], kN[:, col:col + P], K.ident[:, :])
                    last.then_inc(k_back, 1)

                def score(p, q, r):
                    h, i = ROWS[r]
                    rows_h = slice(HD * h, HD * h + HD)
                    if r == 0:
                        pe.wait_ge(k_lo, p + 1)
                        pe.wait_ge(stacked, 64 * p + 64)
                    pe.wait_ge(sig, 16 * p + (r + 1))
                    for c0 in range(0, (i + 1) * P, H):
                        c1 = min(c0 + H, (i + 1) * P)
                        pe.matmul(scores[:, c0:c1], stack[:, q, h, i * P:i * P + P], stack[:, q, 2 + h, c0:c1],
                                  start=True, stop=False)
                        pe.matmul(scores[:, c0:c1], stack[rows_h, q, h, i * P:i * P + P],
                                  k_low[rows_h, q, c0:c1], start=False, stop=c1 <= i * P)
                    pe.matmul(scores[:, i * P:i * P + P], identr[:, :], maskr[:, :],
                              start=False, stop=True).then_inc(qk, 1)

                def turn_weights(p, r):
                    h, i = ROWS[r]
                    pe.wait_ge(ex, 16 * p + (r + 3))
                    for g in range(T_GROUPS[r]):
                        n = T_BEFORE[r] + g
                        pe.wait_ge(tcopy, T_PAIR * p + (n + 1))
                        for b in range(4 * g, min(4 * g + 4, i + 1)):
                            last = pe.transpose(turned[n % 2][:, (b % 4) * P:(b % 4) * P + P],
                                                rows[:, r % 2, b * P:b * P + P], K.ident[:, :])
                        last.then_inc(turn, 1)

                def values(p, q, r):
                    h, i = ROWS[r]
                    if r == 0:
                        pe.wait_ge(v_copy, 2 * p + 2)
                    pe.wait_ge(tcopy, T_PAIR * p + (T_BEFORE[r + 1] + 2))
                    pe.wait_ge(yn, 16 * p + (r + 1))
                    for b in range(i + 1):
                        last = pe.matmul(pO[:, 0:HD], wT[:, r % 2, b * P:b * P + P],
                                         vN[:, q, b * P + HD * h:b * P + HD * h + HD],
                                         start=b == 0, stop=b == i)
                    last.then_inc(pv, 1)

                def turn_y(p, g):
                    if g == 0:
                        pe.wait_ge(yn, 16 * p + 17)
                    pe.wait_ge(tcopy, T_PAIR * p + (T_PAIR + 2))
                    for c in range(4):
                        last = pe.transpose(turned[g][:, c * P:c * P + P], yN[:, 4 * g + c, :], K.ident[:, :])
                    last.then_inc(y_turn, 1)

                def aux(p, slot):
                    for step, when in AUX_SLOT.items():
                        if when == slot and step in AUX:
                            AUX[step](p)

                AUX = dict(k_sum=lambda p: head_sums(p, 0), q_sum=lambda p: head_sums(p, 1),
                           k_turn0=lambda p: turn_k(p, 0), k_turn1=lambda p: turn_k(p, 1),
                           k_back0=lambda p: back_k(p, 0), k_back1=lambda p: back_k(p, 1),
                           v_turn0=lambda p: turn_v(p, 0), v_turn1=lambda p: turn_v(p, 1))

                def pair(p, q, more):
                    u = 0
                    for slot in range(19):
                        if slot < 16:
                            score(p, q, slot)
                        if more:
                            units(p + 1, u, u + UNITS[slot])
                            u += UNITS[slot]
                        if 1 <= slot <= 16:
                            if slot == 1:
                                pe.wait_ge(y_out, 2 * p + 2)
                            turn_weights(p, slot - 1)
                        if 2 <= slot <= 17:
                            values(p, q, slot - 2)
                        if more:
                            aux(p + 1, slot)
                    for g in range(2):
                        turn_y(p, g)

                pe.sem_inc(pv, 2)
                pe.sem_inc(turn, 4)
                K.norm_sums(pe, pV, sums_done)
                units(0, 0, KT)
                K.norm_spread(pe, scores, diag_done, spread_done)
                units(0, KT, 4 * 2 * KT)
                pe.wait_ge(masks, 4)
                for slot in range(19):
                    aux(0, slot)
                with pe.Fori(0, 3) as i:
                    for q in range(2):
                        pair(2 * i + q, q, True)
                pair(6, 0, True)
                pair(7, 1, False)

            @block.scalar
            def _(act):
                def split(p, c):
                    if not (isinstance(p, int) and p == 0 and c < 2):
                        act.wait_ge(dn, 8 * p + (2 * c - 2))
                    if not (isinstance(p, int) and p == PAIRS):
                        act.wait_ge(w_gain, 4 * p + (c + 1))
                    K.split_hi(act, 2 * p + (n0 // 2 + c // 2), c % 2)

                def copy_v(p, q, g):
                    act.wait_ge(v_turn, 2 * p + (g + 1))
                    if not (isinstance(p, int) and p == 0):
                        act.wait_ge(pv, 16 * p - 14)
                    act.activation(vN[:, q, g * H:g * H + H], pV[:, :], ACT.Copy).then_inc(v_copy, 1)

                def square_of(p, q, which):
                    act.wait_ge(evac, 8 * p + (2 * (TQ if which else TK) + 4))
                    if which:
                        act.wait_ge(k_back, 2 * p + 2)
                    elif not (isinstance(p, int) and p == 0):
                        act.wait_ge(summed, 2 * p)
                    act.activation(square, qT[:, :] if which else kRaw, ACT.Square).then_inc(squared, 1)

                def root_of(p, which):
                    act.wait_ge(summed, 2 * p + (which + 1))
                    act.activation((q_root if which else k_root)[:, :], pV[:, 0:16], ACT.Sqrt, scale=1.0 / HD,
                                   bias=K.eps[:, 0:1]).then_inc(rooted, 1)

                def store_k(p, q, g):
                    act.wait_ge(k_back, 2 * p + (g + 1))
                    act.activation(kT[:, g * H:g * H + H], pV[:, :], ACT.Copy,
                                   scale=gains[:, 0:1]).then_inc(k_done, 1)

                def aux(p, q, slot):
                    for step, when in AUX_SLOT.items():
                        if when == slot and step in AUX:
                            AUX[step](p, q)

                def high(p, q, c):
                    if c == TQ:
                        act.wait_ge(evac, 8 * p + (2 * TQ + 4))
                    else:
                        act.wait_ge(k_done, 2 * p + 2)
                    src, at, done = (qT, 0, q_hi) if c == TQ else (kT, 2, k_hi)
                    for h in range(2):
                        rows_h = slice(HD * h, HD * h + HD)
                        last = act.activation(stack[rows_h, q, at + h, :], src[rows_h, :], ACT.Copy)
                    last.then_inc(done, 1)

                AUX = dict(k_parts=lambda p, q: high(p, q, TK), q_parts=lambda p, q: high(p, q, TQ),
                           k_square=lambda p, q: square_of(p, q, 0), q_square=lambda p, q: square_of(p, q, 1),
                           k_sum=lambda p, q: root_of(p, 0), q_sum=lambda p, q: root_of(p, 1),
                           k_back0=lambda p, q: store_k(p, q, 0), k_back1=lambda p, q: store_k(p, q, 1),
                           v_turn0=lambda p, q: copy_v(p, q, 0), v_turn1=lambda p, q: copy_v(p, q, 1))

                def gate(p, q):
                    act.wait_ge(evac, 8 * p + 10)
                    act.wait_ge(v_turn, 2 * p + 2)
                    act.activation(K.acc[:, :], gT[:, q, :], ACT.Sigmoid).then_inc(silu, 1)

                def weights(p, q, r):
                    h, i = ROWS[r]
                    n = (i + 1) * P
                    act.wait_ge(qk, 16 * p + (r + 1))
                    if r == 0:
                        act.wait_ge(q_ready, p + 1)
                    act.wait_ge(ex, 16 * p + (r + 1))
                    act.wait_ge(turn, T_PAIR * p + (T_BEFORE[r - 1] + 4 if r >= 1 else 2))
                    col = 2 * i + h
                    act.activation(keep[:, r % 2, S - n:S], scores[:, 0:n], ACT.Sigmoid,
                                   scale=q_neg[:, q, col:col + 1])
                    act.activation(rows[:, r % 2, 0:n], scores[:, 0:n], ACT.Sigmoid,
                                   scale=q_pos[:, q, col:col + 1]).then_inc(sig, 1)

                def copy_weights(p, r):
                    h, i = ROWS[r]
                    act.wait_ge(pv, 16 * p + (r + 1))
                    for g in range(T_GROUPS[r]):
                        n = T_BEFORE[r] + g
                        act.wait_ge(turn, T_PAIR * p + (n + 5))
                        cols = (min(4 * g + 4, i + 1) - 4 * g) * P
                        act.activation(wT[:, r % 2, g * H:g * H + cols], turned[n % 2][:, 0:cols],
                                       ACT.Copy).then_inc(tcopy, 1)

                def pair(p, q, more):
                    for slot in range(19):
                        if slot == 0 and not more:
                            split(p + 1, 1)
                        if slot < 16:
                            weights(p, q, slot)
                        if slot == 0:
                            gate(p, q)
                        if 1 <= slot <= 16:
                            copy_weights(p, slot - 1)
                        if more:
                            if slot == 0:
                                split(p + 1, 1)
                            if slot == half_done_slot(0, 1) + 1:
                                split(p + 1, 2)
                            if slot == half_done_slot(1, 1) + 1:
                                split(p + 1, 3)
                            aux(p + 1, 1 - q, slot)
                        if more and slot == half_done_slot(2, 1) + 1:
                            split(p + 2, 0)
                act.sem_inc(tcopy, 2)
                act.sem_inc(sig, 1)
                act.wait_ge(masks, 4)
                split(0, 0)
                for k in range(KT):
                    K.tile_hi(act, xhi, f_sb, k, None, x_hi)
                    if k == 3:
                        K.norm_root(act, pV, DM, sums_done, root_done)
                for c in range(1, 4):
                    split(0, c)
                split(1, 0)
                act.wait_ge(x_lo, KT)
                act.wait_ge(f_stored, 16)
                for slot in range(19):
                    aux(0, 0, slot)
                with act.Fori(0, 3) as i:
                    for q in range(2):
                        pair(2 * i + q, q, True)
                pair(6, 0, True)
                pair(7, 1, False)

            @block.vector
            def _(dve):
                def split(p, c):
                    K.split_lo(dve, 2 * p + (n0 // 2 + c // 2), c % 2)

                def scale(p, q, c, half):
                    cols = slice(half * H, half * H + H)
                    dve.wait_ge(dn, 8 * p + (2 * c + half + 1))
                    if c == TV and not (isinstance(p, int) and p == 0):
                        dve.wait_ge(v_turn, 2 * p)
                    dst = {TV: vT[:, cols], TQ: qT[:, cols], TK: kRaw[:, cols], TG: gT[:, q, cols]}[c]
                    dve.tensor_tensor(dst, D[:, cols], K.R[:, cols], ALU.mult).then_inc(evac, 1)

                def gate(p, q):
                    dve.wait_ge(silu, p + 1)
                    dve.tensor_tensor(gT[:, q, :], gT[:, q, :], K.acc[:, :], ALU.mult).then_inc(gated, 1)

                def products(p, r):
                    h, i = ROWS[r]
                    n = (i + 1) * P
                    dve.wait_ge(sig, 16 * p + (r + 2))
                    k = keep[:, r % 2, S - n:S][:, ::-1]
                    dve.tensor_tensor_scan(k, k, k, 1.0, ALU.mult, ALU.bypass).then_inc(scan, 1)

                def store_y(p, r):
                    h, i = ROWS[r]
                    dve.wait_ge(pv, 16 * p + (r + 3))
                    if r == 0:
                        dve.wait_ge(y_turn, 2 * p + 1)
                    dve.tensor_copy(yN[:, i, HD * h:HD * h + HD], pO[:, 0:HD]).then_inc(yn, 1)

                def inverse_k(p):
                    dve.wait_ge(rooted, 2 * p + 1)
                    dve.reciprocal(k_inv[:, :], k_root[:, :]).then_inc(recip, 1)
                    dve.wait_ge(recip, 2 * p + 1)

                def norm_k(p, g):
                    dve.wait_ge(k_turn, 2 * p + (g + 1))
                    r = k_inv[:, 8 * g:8 * g + 8].unsqueeze(2).to_broadcast([P, 8, HD])
                    dve.tensor_tensor(kN[:, g * H:g * H + H].rearrange("p (a d) -> p a d", d=HD),
                                      pV[:, :].rearrange("p (a d) -> p a d", d=HD), r, ALU.mult).then_inc(kn_done, 1)

                def inverse_q(p, q):
                    dve.wait_ge(rooted, 2 * p + 2)
                    dve.reciprocal(q_inv[:, :], q_root[:, :]).then_inc(recip, 1)
                    dve.wait_ge(recip, 2 * p + 2)
                    dve.tensor_scalar(q_pos[:, q, :], q_inv[:, :], HD ** -0.5, None, ALU.mult)
                    dve.tensor_scalar(q_neg[:, q, :], q_inv[:, :], -HD ** -0.5, None, ALU.mult).then_inc(q_ready, 1)

                def low(p, q, c):
                    src, at, hi_done, done = (qT, 0, q_hi, q_lo) if c == TQ else (kT, 2, k_hi, k_lo)
                    dve.wait_ge(hi_done, p + 1)
                    for h in range(2):
                        rows_h = slice(HD * h, HD * h + HD)
                        dst = q_low[rows_h, :] if c == TQ else k_low[rows_h, q, :]
                        last = dve.tensor_tensor(dst, src[rows_h, :], stack[rows_h, q, at + h, :].bitcast(F32),
                                                 ALU.subtract)
                    last.then_inc(done, 1)

                def aux(p, q, slot):
                    if slot == AUX_SLOT["k_sum"]:
                        inverse_k(p)
                    if slot == AUX_SLOT["k_parts"] + 1:
                        low(p, q, TK)
                    if slot == AUX_SLOT["q_parts"] + 1:
                        low(p, q, TQ)
                    for g in range(2):
                        if slot == AUX_SLOT[f"k_turn{g}"]:
                            norm_k(p, g)
                    if slot == AUX_SLOT["q_sum"]:
                        inverse_q(p, q)

                def output(p, q, g):
                    cols = slice(g * H, g * H + H)
                    dve.wait_ge(y_turn, 2 * p + (g + 2))
                    dve.wait_ge(gated, p + 1)
                    dve.wait_ge(y_free, p + 1)
                    dve.tensor_tensor(y_sb[:, q, cols], turned[g][:, :], gT[:, q, cols], ALU.mult).then_inc(y_out, 1)

                def pair(p, q, more):
                    for slot in range(19):
                        if slot == 0 and not more:
                            split(p + 1, 1)
                        if slot >= 3:
                            store_y(p, slot - 3)
                        if slot < 16:
                            products(p, slot)
                        if slot == 1:
                            gate(p, q)
                        if more:
                            for c in range(4):
                                for half in range(2):
                                    if half_done_slot(c, half) + 1 == slot:
                                        scale(p + 1, 1 - q, c, half)
                            if slot == 0:
                                split(p + 1, 1)
                            if slot == half_done_slot(0, 1) + 1:
                                split(p + 1, 2)
                            if slot == half_done_slot(1, 1) + 1:
                                split(p + 1, 3)
                        if more and slot == half_done_slot(2, 1) + 1:
                            split(p + 2, 0)
                        if more:
                            aux(p + 1, 1 - q, slot)
                    if more:
                        scale(p + 1, 1 - q, 3, 1)
                    for g in range(2):
                        output(p, q, g)

                dve.sem_inc(evac, 2)
                dve.wait_ge(landed, 32)
                dve.tensor_copy(identr[:, :], K.ident[:, :]).then_inc(masks, 1)
                dve.tensor_copy(maskr[:, :], raw_mask).then_inc(masks, 1)
                dve.memset(keep[:, :, S:S + 1], 1.0).then_inc(masks, 1)
                dve.tensor_tensor(gains[:, :], K.gain("q_g", 0), K.gain("k_g", 0), ALU.mult).then_inc(masks, 1)
                dve.sem_inc(yn, 1)
                dve.sem_inc(y_out, 2)
                dve.sem_inc(y_free, 2)
                dve.sem_inc(y_turn, 1)
                split(0, 0)
                for k in range(KT):
                    K.tile_lo(dve, xlo, xhi, f_sb, k, None, x_hi, x_lo)
                    if k == 3:
                        K.norm_recip(dve, root_done, rtok_done)
                        K.norm_diag(dve, diag_done)
                split(0, 1)
                K.norm_copy(dve, scores, spread_done, r_done)
                for c in range(4):
                    for half in range(2):
                        scale(0, 0, c, half)
                    if c < 2:
                        split(0, c + 2)
                    if c == 2:
                        split(1, 0)
                for slot in range(19):
                    aux(0, 0, slot)
                with dve.Fori(0, 3) as i:
                    for q in range(2):
                        pair(2 * i + q, q, True)
                pair(6, 0, True)
                pair(7, 1, False)

            @block.gpsimd
            def _(pool):
                def gain(p, c):
                    n = (p + (n0 // 4)) * 2 + c // 2
                    pool.wait_ge(K.w_land[c % 2], 16 * n + 16)
                    g = K.vec[:, VEC["kv_norm"]:VEC["kv_norm"] + KT] if c in (TK, TV) else \
                        K.vec[:, VEC["s_norm"]:VEC["s_norm"] + KT]
                    tile = K.wraw[:, c % 2, :, :]
                    pool.tensor_tensor(tile, tile, g.unsqueeze(2).to_broadcast([P, KT, P]), ALU.mult).then_inc(w_gain, 1)

                def weigh(p, r):
                    h, i = ROWS[r]
                    n = (i + 1) * P
                    pool.wait_ge(scan, 16 * p + (r + 1))
                    pool.tensor_tensor(rows[:, r % 2, 0:n], rows[:, r % 2, 0:n],
                                       keep[:, r % 2, S - n + 1:S + 1], ALU.mult).then_inc(ex, 1)

                def stack_parts(p, q, c):
                    pool.wait_ge(q_lo if c == TQ else k_hi, p + 1)
                    pool.sem_inc(dma_go, 1)
                    for h in range(2):
                        own, other = slice(HD * h, HD * h + HD), slice(HD - HD * h, P - HD * h)
                        if c == TQ:
                            pool.dma_start(stack[other, q, h, :], q_low[own, :]).then_inc(stacked, 16)
                        else:
                            pool.dma_start(stack[other, q, 2 + h, :], stack[own, q, 2 + h, :]).then_inc(stacked, 16)

                def store(p, q):
                    if not (isinstance(p, int) and p == 0):
                        pool.wait_ge(y_left, 16 * p)
                        pool.sem_inc(y_free, 1)
                    pool.wait_ge(y_out, 2 * p + 4)
                    pool.sem_inc(dma_go, 1)
                    pool.dma_start(out[p, :, :], y_sb[:, q, :]).then_inc(y_left, 16)

                def pair(p, q, more, more2):
                    for slot in range(19):
                        if slot < 16:
                            weigh(p, slot)
                        if more and slot in (1, 3):
                            gain(p + 1, 2 + slot // 2)
                        if more2 and slot in (8, 14):
                            gain(p + 2, int(slot == 14))
                        if more and slot == AUX_SLOT["k_parts"] + 2:
                            stack_parts(p + 1, 1 - q, TK)
                        if more and slot == AUX_SLOT["q_parts"] + 2:
                            stack_parts(p + 1, 1 - q, TQ)
                    store(p, q)

                pool.sem_inc(ex, 2)
                pool.wait_ge(masks, 4)
                for c in range(4):
                    gain(0, c)
                gain(1, 0)
                gain(1, 1)
                for c in (TK, TQ):
                    stack_parts(0, 0, c)
                for p in range(2):
                    pair(p, p, True, True)
                with pool.Fori(1, 3) as i:
                    for q in range(2):
                        pair(2 * i + q, q, True, True)
                pair(6, 0, True, False)
                pair(7, 1, False, False)
                pool.wait_ge(y_left, 16 * PAIRS)


def alibi_table():
    d = np.arange(P)[:, None] - np.arange(S)[None, :] + (S - P)
    count = np.zeros(d.shape)
    for window, dilation in ((128, 1), (512, 4), (2048, 16)):
        count += (d >= 0) & (d % dilation == 0) & (d <= window)
    log_count = np.where(count > 0, np.log(np.maximum(count, 1)), 0.0)
    slopes = 2.0 ** (-8.0 * np.arange(1, HEADS + 1) / HEADS)
    table = -slopes[:, None, None] * d + log_count
    return np.where(count > 0, table, NEG).astype(np.float32)


def weight_tiles(w):
    k, n = w.shape
    return w.reshape(k // P, P, n // P, P).transpose(2, 1, 0, 3)


def columns(v):
    return np.reshape(v, (-1, P)).T


def stage_ple(K, layer, xhi, xlo, f_sb, unused, squared, out=None):
    nc, io, name = K.nc, K.io, f"ple{layer}"
    n0 = FIRST[name]
    KP = 2
    with ExitStack() as ctx:
        sem = K.semaphores(name + "_")
        sb = lambda n, shape, dt=F32: ctx.enter_context(nc.sbuf_tensor(f"{name}_{n}", shape, dt))
        D = ctx.enter_context(nc.psum_tensor(name + "_D", [P, 2, S], F32))
        pP = ctx.enter_context(nc.psum_tensor(name + "_pP", [P, 2, S], F32))
        p_raw, p_hi, p_lo = unused[:, 0:KP, :], sb("p_hi", [P, KP, S], F32R), sb("p_lo", [P, KP, S], F32R)
        w_raw = unused[:, KP:2 * KP, :].rearrange("p a (b m) -> p (a b) m", m=P)
        w_raw = w_raw.rearrange("p (j k) m -> p j k m", k=KP)
        w_hi, w_lo = sb("w_hi", [P, KT, KP, P], F32R), sb("w_lo", [P, KT, KP, P], F32R)
        gate = K.sq
        squares = sb("squares", [P, 2, S]) if out is None else None
        sums, spread = pP[:, 1, :], pP[:, 1, :]
        landed, parts, p_lows = sem("landed"), sem("parts"), sem("p_lows")
        mm, pm, scaled, sig, gated, added = sem("mm"), sem("pm"), sem("scaled"), sem("sig"), sem("gated"), sem("added")
        x_hi, x_lo, sq_done, acc_done = sem("x_hi"), sem("x_lo"), sem("sq"), sem("acc")
        sums_done, root_done, rtok_done = sem("sums"), sem("root"), sem("rtok")
        diag_done, spread_done, r_done = sem("diag"), sem("spread"), sem("r")
        new_sq, new_acc, stored = sem("new_sq"), sem("new_acc"), sem("stored")
        with nc.Block() as block:
            @block.sync
            def _(sp):
                sp.dma_start(p_raw[:, :, :], io["pT"][layer].rearrange("(k p) t -> p k t", p=P)).then_inc(landed, 16)
                sp.dma_start(w_raw[:, :, :, :], io["w_ple"][layer].rearrange("j p k m -> p j k m")).then_inc(landed, 16)
                K.load_ahead(sp, name, skip_last=layer == 1)

            @block.tensor
            def _(pe):
                if squared:
                    K.norm_sums(pe, sums, sums_done)
                for j in range(KT):
                    s = j % 2
                    pe.wait_ge(K.w_lo, n0 + j + 1)
                    if j >= 2:
                        pe.wait_ge(added, j + 1)
                    K.dense(pe, D[:, s, :], s, xhi, xlo, x_lo if j == 0 else None).then_inc(mm, 1)
                    if j == 0:
                        pe.wait_ge(p_lows, 2)
                    if j == 1:
                        if not squared:
                            pe.wait_ge(acc_done, KT)
                            K.norm_sums(pe, sums, sums_done)
                            K.norm_spread(pe, spread, diag_done, spread_done)
                        pe.wait_ge(r_done, 1)
                    for k in range(KP):
                        for half in range(2):
                            cols = slice(half * H, half * H + H)
                            pe.matmul(pP[:, s, cols], w_hi[:, j, k, :], p_hi[:, k, cols], start=k == 0, stop=False)
                            pe.matmul(pP[:, s, cols], w_hi[:, j, k, :], p_lo[:, k, cols], start=False, stop=False)
                            last = pe.matmul(pP[:, s, cols], w_lo[:, j, k, :], p_hi[:, k, cols],
                                             start=False, stop=k == KP - 1)
                    last.then_inc(pm, 1)
                    if j == 0 and squared:
                        K.norm_spread(pe, spread, diag_done, spread_done)

            @block.scalar
            def _(act):
                for k in range(KT):
                    K.tile_hi(act, xhi, f_sb, k, name, x_hi)
                if squared:
                    K.norm_root(act, sums, DM, sums_done, root_done)
                act.wait_ge(landed, 32)
                act.activation(p_hi[:, :, :], p_raw[:, :, :], ACT.Copy).then_inc(parts, 1)
                act.activation(w_hi[:, :, :, :], w_raw[:, :, :, :], ACT.Copy).then_inc(parts, 1)
                if not squared:
                    for k in range(KT):
                        K.square(act, f_sb[:, k, :], k, sq_done, acc_done)
                    K.norm_root(act, sums, DM, sums_done, root_done)

                def tiles(i, first=False, last=False):
                    for s in range(2):
                        n = 2 * i + s
                        act.wait_ge(scaled, n + 1)
                        act.activation(gate[:, s, :], gate[:, s, :], ACT.Sigmoid).then_inc(sig, 1)
                        if not last:
                            act.wait_ge(mm, n + 1)
                            K.split_hi(act, i + (n0 // 2 + 1), s)
                        if out is None:
                            K.square_tile(act, squares[:, s, :], f_sb[:, n, :], n, added, n + 3, new_acc,
                                          first).then_inc(new_sq, 1)

                tiles(0, first=True)
                with act.Fori(1, KT // 2 - 1) as i:
                    tiles(i)
                tiles(KT // 2 - 1, last=True)

            @block.gpsimd
            def _(pool):
                if out is None:
                    K.sum_tiles(pool, squares, new_sq, new_acc)
                else:
                    tiles = out.rearrange("(k p) t -> k p t", p=P)
                    with pool.Fori(0, KT) as n:
                        pool.wait_ge(added, n + 3)
                        pool.dma_start(tiles[n, :, :], f_sb[:, n, :]).then_inc(stored, 16)
                    pool.wait_ge(stored, 16 * KT)

            @block.vector
            def _(dve):
                for k in range(KT):
                    K.tile_lo(dve, xlo, xhi, f_sb, k, name, x_hi, x_lo)
                dve.wait_ge(parts, 2)
                dve.tensor_tensor(p_lo[:, :, :], p_raw[:, :, :], p_hi[:, :, :].bitcast(F32), ALU.subtract).then_inc(p_lows, 1)
                dve.tensor_tensor(w_lo[:, :, :, :], w_raw[:, :, :, :], w_hi[:, :, :, :].bitcast(F32),
                                  ALU.subtract).then_inc(p_lows, 1)
                if not squared:
                    K.sum_squares(dve, KT, sq_done, acc_done)
                K.norm_recip(dve, root_done, rtok_done)
                K.norm_diag(dve, diag_done)
                K.norm_copy(dve, spread, spread_done, r_done)
                dve.sem_inc(added, 2)

                def tiles(i, last=False):
                    for s in range(2):
                        n = 2 * i + s
                        dve.wait_ge(mm, n + 1)
                        dve.wait_ge(added, n + 1)
                        dve.tensor_tensor(gate[:, s, :], D[:, s, :], K.R[:, :], ALU.mult).then_inc(scaled, 1)
                        if not last:
                            K.split_lo(dve, i + (n0 // 2 + 1), s)
                        dve.wait_ge(pm, n + 1)
                        dve.wait_ge(sig, n + 1)
                        dve.tensor_tensor(gate[:, s, :], pP[:, s, :], gate[:, s, :], ALU.mult).then_inc(gated, 1)
                        dve.wait_ge(gated, n + 1)
                        dve.tensor_tensor(f_sb[:, n, :], f_sb[:, n, :], gate[:, s, :], ALU.add).then_inc(added, 1)

                with dve.Fori(0, KT // 2 - 1) as i:
                    tiles(i)
                tiles(KT // 2 - 1, last=True)


def bass_program(nc, io, out):
    with ExitStack() as ctx:
        K = Kernel(nc, ctx, io)

        def tensors(stack, *names, dt=F32):
            return [stack.enter_context(nc.sbuf_tensor(n, [P, KT, S], dt)) for n in names]

        branch_a = nc.dram_tensor("branch_a", (KT, P, S), F32, kind="Internal").ap()
        y_dram = nc.dram_tensor("y_b", (KT, P, S), F32, kind="Internal").ap()
        f_dram = nc.dram_tensor("f_copy", (P, KT, S), F32, kind="Internal").ap()
        acum_dram = nc.dram_tensor("acum_rows", (SH, S), F32, kind="Internal").ap()
        x_dram = io["xT"].rearrange("(k p) t -> p k t", p=P)

        ctx.callback(K.clear_semaphores)

        with ExitStack() as b1:
            with ExitStack() as shared:
                stack = shared.enter_context(nc.sbuf_tensor("stack", [P, 2, 4, S], F32R))
            f_sb, = tensors(b1, "f1")
            with ExitStack() as b2:
                xhi, xlo = tensors(b2, "x1hi", "x1lo", dt=F32R)
                vN = f_sb
                with ExitStack() as b3:
                    x_sb, = tensors(b3, "x_sb")
                    stage_v(K, x_sb, xhi, xlo, vN)
                with ExitStack() as b3:
                    yhi, ylo = tensors(b3, "ya_hi", "ya_lo", dt=F32R)
                    D = b3.enter_context(nc.psum_tensor("a_D", [P, 2, S], F32))
                    stage_ug(K, D, xhi, xlo, vN, yhi, ylo)
                    stage_pa(K, D, xhi, xlo, yhi, ylo, branch_a)
                y = f_sb
                with ExitStack() as b3:
                    D = b3.enter_context(nc.psum_tensor("b_D", [P, S], F32))
                    stage_attention(K, D, xhi, xlo, stack, y_dram, y)
                    yhi, ylo = tensors(b3, "yb_hi", "yb_lo", dt=F32R)
                    stage_pb(K, D, xhi, xlo, y_dram, y, yhi, ylo, branch_a, y)
                with ExitStack() as b3:
                    heads = [b3.enter_context(nc.sbuf_tensor("heads_" + n, [P, NC * SH], F32))
                             for n in ("dt", "dte", "acum", "e_acum", "e_end")]
                    with ExitStack() as b4:
                        merged = f_sb
                        x1, = tensors(b4, "x1")
                        stage_residual(K, "out", merged, xhi, xlo, x1, x_dram)
                        stage_dt(K, x1, f_sb, xhi, xlo, *heads, acum_dram)
                    K.clear_semaphores()
                    stage_ssm(K, xhi, xlo, f_sb, *heads, acum_dram)
                with nc.sbuf_tensor("ple_in", [P, 4, S], F32) as unused:
                    stage_ple(K, 0, xhi, xlo, f_sb, unused, squared=False)
                K.clear_semaphores()
                stage_stick(K, xhi, xlo, f_sb, f_dram, stack, y_dram)
                with ExitStack() as b3:
                    h, = tensors(b3, "h")
                    stage_residual(K, "sout", f_sb, xhi, xlo, h, f_dram, y_dram)
                    stage_ple(K, 1, xhi, xlo, h, f_sb, squared=True, out=out)


def kernel(**inputs):
    import concourse.bacc as bacc
    from concourse.bass_utils import run_bass_kernel_spmd

    a = {k: np.asarray(v) for k, v in inputs.items()}
    def merge(*xs):
        return np.stack(xs, 1).reshape(-1, P, KT, P)

    u, v, gate, q, k, val, b_gate, g_a, g_b = weight_tiles(a["w_in"][0]).reshape(9, 8, P, KT, P)
    weights = [v, merge(u, gate), merge(g_a, weight_tiles(a["w_proj_a"][0])), merge(val, q, k, b_gate),
               merge(g_b, weight_tiles(a["w_proj_b"][0])), weight_tiles(a["w_out"][0])]
    m_in = a["m_in_2"][0]
    channels, state = GROUPS * GC, GROUPS * P
    z, xs, b, c = (weight_tiles(m_in[:, i:j]) for i, j in (
        (0, channels), (channels, 2 * channels), (2 * channels, 2 * channels + state),
        (2 * channels + state, 2 * channels + 2 * state)))
    for g in range(GROUPS):
        of = slice(GT * g, GT * g + GT)
        m_out = weight_tiles(a["m_out_2"][0][GC * g:GC * g + GC]).reshape(4, 2, P, GT, P)
        weights += [b[g:g + 1], c[g:g + 1], xs[of], z[of], m_out.transpose(0, 2, 1, 3, 4).reshape(4, P, KT, P)]
    k2, v2 = weight_tiles(a["w_kv_2"]).reshape(2, 8, P, KT, P)
    q2, gate2 = weight_tiles(a["s_in_2"][0]).reshape(2, 8, P, KT, P)
    weights += [weight_tiles(a["ple_gate_2"][0]), merge(k2, v2, q2, gate2), weight_tiles(a["s_out_2"][0]),
                weight_tiles(a["ple_gate_2"][1])]

    w_dt = np.zeros((DM, P), np.float32)
    w_dt[:, :SH] = m_in[:, -SH:]
    vec = np.zeros((P, N_VEC), np.float32)

    def put(name, v):
        vec[:, VEC[name]:VEC[name] + VEC_WIDTH[name]] = columns(v)

    put("g_norm", a["g_norm"][0])
    put("g_v", a["g_v"][0])
    put("g_final", a["g_final"])
    put("m_norm", a["m_norm_2"][0])
    vec[:, VEC["conv_w"]:VEC["conv_w"] + 96] = a["m_conv_w_2"][0].reshape(TAPS, 24, P).transpose(2, 1, 0).reshape(P, 96)
    put("conv_b", a["m_conv_b_2"][0])
    put("d_skip", np.repeat(a["m_D_2"][0], SD))
    put("y_norm", a["m_ynorm_2"][0])
    put("kv_norm", a["kv_norm_2"])
    put("s_norm", a["s_norm_2"][0])
    put("ple0", a["ple_norm_2"][0])
    put("ple1", a["ple_norm_2"][1])
    put("q_g", np.tile(a["q_norm_2"][0], 2))
    put("k_g", np.tile(a["k_norm_2"], 2))
    arrays = {
        "w": np.concatenate(weights), "vec": vec, "xT": np.ascontiguousarray(a["x"][0].T),
        "ones": np.ones((P, P), np.float32), "ident": np.eye(P, dtype=np.float32),
        "causal": np.triu(np.ones((P, P), np.float32)),
        "strict": np.where(np.tril(np.ones((P, P)), -1) > 0, 0.0, NEG).astype(np.float32),
        "select": np.repeat(np.eye(2, dtype=np.float32), HD, axis=0),
        "w_sT": np.ascontiguousarray(a["w_s"][0].transpose(0, 2, 1)), "b_s": a["b_s"][0],
        "alibi": alibi_table(),
        "w_dt": np.ascontiguousarray(weight_tiles(w_dt)[0]),
        "dt_head": np.stack([a["m_dt_bias_2"][0], a["m_A_log_2"][0]]),
        "pT": np.ascontiguousarray(a["p_2"][:, 0].transpose(0, 2, 1)),
        "w_ple": np.stack([weight_tiles(a["ple_proj_2"][i]) for i in range(2)]),
    }
    nc = bacc.Bacc("TRN2", target_bir_lowering=False, num_devices=1)
    io = {n: nc.dram_tensor(n + "_dram", v.shape, mybir.dt.from_np(v.dtype), kind="ExternalInput").ap()
          for n, v in arrays.items()}
    out = nc.dram_tensor("out_dram", (DM, S), F32, kind="ExternalOutput").ap()
    bass_program(nc, io, out)
    r = run_bass_kernel_spmd(nc, [{n + "_dram": v for n, v in arrays.items()}], core_ids=[0])
    return np.ascontiguousarray(r.results[0]["out_dram"].T)[None]
```
